# Optimizing a Trainium2 kernel written in Bass

```python
import math, functools
import jax, jax.numpy as jnp
from jax import lax
import numpy as np

D_MODEL = 1024
BATCH = 1
SEQ = 512
DEPTH = 1
DEC_BATCH = 8
DEC_SEQ = 8
PAST_LEN = 512
PAGE_SIZE = 128

D_MIX = D_MODEL
C_POOL = D_MIX // 2
POOL_WINDOWS = (2, 4, 8, 16)
POOL_GC = C_POOL // len(POOL_WINDOWS)
POOL_HIST = max(POOL_WINDOWS) - 1
D_ATT = D_MIX - C_POOL
HEAD_DIM = 64
N_HEADS = D_ATT // HEAD_DIM
IDX_HEADS = 8
IDX_DIM = 64
TOPK_MAX = 256
N_BUCKETS = 32
MAX_DISTANCE = 128
D_FF = 4 * D_MODEL
Q_BLOCK = 128
EPS = 1e-6
OFF_Q = C_POOL
OFF_K = OFF_Q + D_ATT
OFF_V = OFF_K + D_ATT
OFF_QI = OFF_V + D_ATT
OFF_KI = OFF_QI + IDX_HEADS * IDX_DIM
OFF_WI = OFF_KI + IDX_DIM
D_IN = OFF_WI + IDX_HEADS

kernel_name = "hybrid_pool_dsa_decoder_step"

def rms_norm(x, g):
    x32 = x.astype(jnp.float32)
    y = x32 * lax.rsqrt(jnp.mean(x32 * x32, axis=-1, keepdims=True) + EPS)
    return (y * g.astype(jnp.float32)).astype(x.dtype)

def t5_bucket(dist):
    n = jnp.maximum(dist, 0)
    max_exact = N_BUCKETS // 2
    large = max_exact + (jnp.log(jnp.maximum(n, 1).astype(jnp.float32) / max_exact)
                         / math.log(MAX_DISTANCE / max_exact)
                         * (N_BUCKETS - max_exact)).astype(jnp.int32)
    large = jnp.minimum(large, N_BUCKETS - 1)
    return jnp.where(n < max_exact, n, large)

def split_proj(z):
    B, T, _ = z.shape
    u = z[..., :OFF_Q]
    q = z[..., OFF_Q:OFF_K].reshape(B, T, N_HEADS, HEAD_DIM)
    k = z[..., OFF_K:OFF_V].reshape(B, T, N_HEADS, HEAD_DIM)
    v = z[..., OFF_V:OFF_QI].reshape(B, T, N_HEADS, HEAD_DIM)
    qi = z[..., OFF_QI:OFF_KI].reshape(B, T, IDX_HEADS, IDX_DIM)
    ki = z[..., OFF_KI:OFF_WI]
    wi = z[..., OFF_WI:]
    return u, q, k, v, qi, ki, wi

def pool_mix(u_ext, n_hist, pos0, pool_w_l, pool_scale_l):
    B, E, C = u_ext.shape
    u32 = u_ext.astype(jnp.float32)
    cs = jnp.concatenate([jnp.zeros((B, 1, C), jnp.float32), jnp.cumsum(u32, axis=1)], axis=1)
    row = jnp.arange(n_hist, E)
    pos = pos0 + row
    outs = []
    for g, w in enumerate(POOL_WINDOWS):
        sl = slice(g * POOL_GC, (g + 1) * POOL_GC)
        win_sum = cs[:, row + 1, sl] - cs[:, jnp.maximum(row + 1 - w, 0), sl]
        cnt = jnp.minimum(pos + 1, w).astype(jnp.float32)[None, :, None]
        pooled = win_sum / cnt - u32[:, n_hist:, sl]
        outs.append(jnp.einsum('btc,cd->btd', pooled.astype(u_ext.dtype), pool_w_l[g]))
    return jnp.concatenate(outs, axis=-1) * pool_scale_l

def sparse_attention(q, qi, wi, qpos, k_all, v_all, ki_all, n_sel, rel_bias):
    B, Tq = q.shape[:2]
    L = k_all.shape[1]
    kpos = jnp.arange(L, dtype=jnp.int32)
    causal = kpos[None, :] <= qpos[:, None]
    dots = jnp.einsum('bthd,bsd->bths', qi.astype(jnp.float32), ki_all.astype(jnp.float32)) * IDX_DIM ** -0.5
    score = jnp.einsum('bth,bths->bts', wi.astype(jnp.float32) * IDX_HEADS ** -0.5, jax.nn.relu(dots))
    score = jnp.where(causal[None], score, -jnp.inf)
    _, sel = lax.top_k(score, n_sel)
    gather = jax.vmap(lambda rows, idx: rows[idx])
    k_sel = gather(k_all, sel)
    v_sel = gather(v_all, sel)
    logits = jnp.einsum('bthd,btnhd->bthn', q, k_sel).astype(jnp.float32) * HEAD_DIM ** -0.5
    dist = qpos[None, :, None] - sel
    bias = rel_bias[t5_bucket(dist)].astype(jnp.float32)
    logits = logits + jnp.transpose(bias, (0, 1, 3, 2))
    valid = (dist >= 0)[:, :, None, :]
    logits = jnp.where(valid, logits, -jnp.inf)
    p = jax.nn.softmax(logits, axis=-1)
    out = jnp.einsum('bthn,btnhd->bthd', p.astype(v_sel.dtype), v_sel)
    return out.reshape(B, Tq, N_HEADS * HEAD_DIM)

def prompt_mixer(z, pool_w_l, pool_scale_l, rel_bias, n_sel):
    u, q, k, v, qi, ki, wi = split_proj(z)
    B, T, _ = z.shape
    y_pool = pool_mix(u, 0, 0, pool_w_l, pool_scale_l)
    nb = T // Q_BLOCK
    blk = lambda a: jnp.moveaxis(a.reshape((B, nb, Q_BLOCK) + a.shape[2:]), 1, 0)
    qpos = jnp.arange(T, dtype=jnp.int32).reshape(nb, Q_BLOCK)
    y_att = lax.map(lambda a: sparse_attention(a[0], a[1], a[2], a[3], k, v, ki, n_sel, rel_bias),
                    (blk(q), blk(qi), blk(wi), qpos))
    y_att = jnp.moveaxis(y_att, 0, 1).reshape(B, T, D_ATT)
    return jnp.concatenate([y_pool, y_att], axis=-1), (k, v, ki, u[:, T - POOL_HIST:])

def sample_mixer(z, layer, cache_k, cache_v, cache_kidx, state_pool, page_table, pool_w_l, pool_scale_l, rel_bias, n_sel):
    u, q, k, v, qi, ki, wi = split_proj(z)
    B, T, _ = z.shape
    past = lambda pool: pool[layer, page_table].reshape((B, -1) + pool.shape[3:]).astype(z.dtype)
    k_all = jnp.concatenate([past(cache_k), k], axis=1)
    v_all = jnp.concatenate([past(cache_v), v], axis=1)
    ki_all = jnp.concatenate([past(cache_kidx), ki], axis=1)
    qpos = PAST_LEN + jnp.arange(T, dtype=jnp.int32)
    y_att = sparse_attention(q, qi, wi, qpos, k_all, v_all, ki_all, n_sel, rel_bias)
    u_ext = jnp.concatenate([state_pool[layer].astype(u.dtype), u], axis=1)
    y_pool = pool_mix(u_ext, POOL_HIST, PAST_LEN - POOL_HIST, pool_w_l, pool_scale_l)
    return jnp.concatenate([y_pool, y_att], axis=-1), (k, v, ki, u_ext[:, -POOL_HIST:])

def decoder_layer(x, c, mix_fn, ada_w_l, ada_b_l, ln1_pre_l, ln1_post_l, ln2_pre_l, ln2_post_l,
                  w_in_l, w_out_l, w_ff1_l, w_ff2_l):
    mod = (c @ ada_w_l + ada_b_l)[:, None, :]
    sh1, sc1, g1, sh2, sc2, g2 = jnp.split(mod, 6, axis=-1)
    h = rms_norm(x, ln1_pre_l) * (1 + sc1) + sh1
    mixed, new_state = mix_fn(h @ w_in_l)
    x = x + g1 * rms_norm(mixed @ w_out_l, ln1_post_l)
    h = rms_norm(x, ln2_pre_l) * (1 + sc2) + sh2
    f = jnp.square(jax.nn.relu(h @ w_ff1_l)) @ w_ff2_l
    x = x + g2 * rms_norm(f, ln2_post_l)
    return x, new_state

def setup_inputs(seed: int = 0) -> dict:
    key = jax.random.key(seed)
    ks = jax.random.split(key, 24)
    f32 = jnp.float32
    n_pages = PAST_LEN // PAGE_SIZE
    n_phys = (DEC_BATCH * n_pages * 5) // 4
    nrm = lambda k, shape, s: jax.random.normal(k, shape, f32) * s
    page_table = jax.random.permutation(ks[0], n_phys)[:DEC_BATCH * n_pages]
    page_table = page_table.reshape(DEC_BATCH, n_pages).astype(jnp.int32)
    return {
        "x_prompt": nrm(ks[1], (BATCH, SEQ, D_MODEL), 1.0),
        "x_sample": nrm(ks[2], (DEC_BATCH, DEC_SEQ, D_MODEL), 1.0),
        "cache_k": nrm(ks[3], (DEPTH, n_phys, PAGE_SIZE, N_HEADS, HEAD_DIM), 1.0),
        "cache_v": nrm(ks[4], (DEPTH, n_phys, PAGE_SIZE, N_HEADS, HEAD_DIM), 1.0),
        "cache_kidx": nrm(ks[5], (DEPTH, n_phys, PAGE_SIZE, IDX_DIM), 1.0),
        "state_pool": nrm(ks[6], (DEPTH, DEC_BATCH, POOL_HIST, C_POOL), 1.0),
        "page_table": page_table,
        "c_prompt": nrm(ks[7], (BATCH, D_MODEL), 1.0),
        "c_sample": nrm(ks[8], (DEC_BATCH, D_MODEL), 1.0),
        "rel_bias": nrm(ks[9], (N_BUCKETS, N_HEADS), 0.5),
        "ada_w": nrm(ks[10], (DEPTH, D_MODEL, 6 * D_MODEL), 0.3 * D_MODEL ** -0.5),
        "ada_b": nrm(ks[11], (DEPTH, 6 * D_MODEL), 0.02),
        "ln1_pre": 1.0 + nrm(ks[12], (DEPTH, D_MODEL), 0.05),
        "ln1_post": 1.0 + nrm(ks[13], (DEPTH, D_MODEL), 0.05),
        "ln2_pre": 1.0 + nrm(ks[14], (DEPTH, D_MODEL), 0.05),
        "ln2_post": 1.0 + nrm(ks[15], (DEPTH, D_MODEL), 0.05),
        "w_in": nrm(ks[16], (DEPTH, D_MODEL, D_IN), D_MODEL ** -0.5),
        "pool_w": nrm(ks[17], (DEPTH, len(POOL_WINDOWS), POOL_GC, POOL_GC), POOL_GC ** -0.5),
        "pool_scale": 1.0 + nrm(ks[18], (DEPTH, C_POOL), 0.1),
        "w_out": nrm(ks[19], (DEPTH, D_MIX, D_MODEL), D_MIX ** -0.5),
        "w_ff1": nrm(ks[20], (DEPTH, D_MODEL, D_FF), D_MODEL ** -0.5),
        "w_ff2": nrm(ks[21], (DEPTH, D_FF, D_MODEL), D_FF ** -0.5),
    }

def reference(x_prompt, x_sample, cache_k, cache_v, cache_kidx, state_pool, page_table, c_prompt, c_sample,
              rel_bias, ada_w, ada_b, ln1_pre, ln1_post, ln2_pre, ln2_post, w_in, pool_w, pool_scale,
              w_out, w_ff1, w_ff2):
    n_sel_prompt = min(TOPK_MAX, SEQ // 4)
    n_sel_sample = min(TOPK_MAX, (PAST_LEN + DEC_SEQ) // 4)
    xp, xs = x_prompt, x_sample
    outs_p = [[], [], [], []]
    outs_s = [[], [], [], []]
    for l in range(DEPTH):
        shared = (ada_w[l], ada_b[l], ln1_pre[l], ln1_post[l], ln2_pre[l], ln2_post[l],
                  w_in[l], w_out[l], w_ff1[l], w_ff2[l])
        mix_p = functools.partial(prompt_mixer, pool_w_l=pool_w[l], pool_scale_l=pool_scale[l],
                                  rel_bias=rel_bias, n_sel=n_sel_prompt)
        xp, st_p = decoder_layer(xp, c_prompt, mix_p, *shared)
        mix_s = functools.partial(sample_mixer, layer=l, cache_k=cache_k, cache_v=cache_v,
                                  cache_kidx=cache_kidx, state_pool=state_pool, page_table=page_table,
                                  pool_w_l=pool_w[l], pool_scale_l=pool_scale[l],
                                  rel_bias=rel_bias, n_sel=n_sel_sample)
        xs, st_s = decoder_layer(xs, c_sample, mix_s, *shared)
        for lst, a in zip(outs_p, st_p):
            lst.append(a)
        for lst, a in zip(outs_s, st_s):
            lst.append(a)
    new_k_p, new_v_p, new_ki_p, new_pool_p = [jnp.stack(a) for a in outs_p]
    new_k_s, new_v_s, new_ki_s, new_pool_s = [jnp.stack(a) for a in outs_s]
    return (xp, xs, new_k_p, new_v_p, new_ki_p, new_pool_p, new_k_s, new_v_s, new_ki_s, new_pool_s)


_drawn_inputs = setup_inputs


def setup_inputs(seed=0):
    import zlib

    import numpy as np

    out = dict(_drawn_inputs(seed))
    spreads = {}
    factors = {'ln1_post': 3.843, 'ln2_pre': 3.854, 'ln2_post': 4.048}
    for name, (base, spread) in spreads.items():
        noise = np.random.default_rng([zlib.crc32(name.encode()), seed]).standard_normal(out[name].shape)
        drawn = base * np.exp(spread * noise) if base else spread * noise
        out[name] = __import__('jax').numpy.asarray(drawn.astype(out[name].dtype))
    for name, factor in factors.items():
        out[name] = (out[name] * factor).astype(out[name].dtype)
    return out
```

```python
from contextlib import ExitStack

import numpy as np
import concourse.bass as bass
from concourse import mybir

F32 = mybir.dt.float32
F32R = mybir.dt.float32r
I32 = mybir.dt.int32
ALU = mybir.AluOpType
ACT = mybir.ActivationFunctionType
AX_X = mybir.AxisListType.X

D = 1024
KC = D // 128
TP = 512
NT = TP // 128
DB, DS = 8, 8
TS = DB * DS
PAST, PAGE = 512, 128
NPG = PAST // PAGE
H, HD = 8, 64
CP_ = 512
NG = 4
WINDOWS = (2, 4, 8, 16)
HIST = 15
NB, MAXD = 32, 128
DFF = 4096
D_IN = 4 * 512 + 512 + 64 + 8
OFF_Q, OFF_K, OFF_V, OFF_QI, OFF_KI, OFF_WI = 512, 1024, 1536, 2048, 2560, 2624
SEL_P = min(256, TP // 4)
SEL_S = min(256, (PAST + DS) // 4)
LS = PAST + DS
EPS = 1e-6
NEG = -(2.0 ** 100)
TAKEN = -3.0e38
NRAW, NSPLIT = 2, 2
QF = 4
SEG = 1 + HIST + DS
UW = 16 + TP + DB * SEG


def t5_bucket(n):
    n = np.maximum(n, 0)
    exact = NB // 2
    large = exact + (np.log(np.maximum(n, 1).astype(np.float32) / exact)
                     / np.log(MAXD / exact) * (NB - exact)).astype(np.int32)
    return np.where(n < exact, n, np.minimum(large, NB - 1))


def constants():
    parts = {}
    r = np.arange(128)
    parts["ident"] = np.eye(128)
    parts["flip"] = np.eye(128)[::-1]
    parts["causal"] = np.where(r[None, :] > r[:, None], NEG, 0.0)
    onehot = np.zeros((128, 384))
    x = np.arange(384)
    onehot[t5_bucket(255 - x), x] += 1.0
    onehot[NB - 1, :] -= 1.0
    parts["bucket"] = onehot
    unflip = np.zeros((128, 128))
    for b2 in range(2):
        for h in range(H):
            for t in range(DS):
                unflip[h * DS + (DS - 1 - t), b2 * 64 + h * DS + t] = 1.0
    parts["unflip"] = unflip
    own = np.zeros((128, 4, DB))
    for bp in range(4):
        for b2 in range(2):
            own[64 * b2:64 * b2 + 64, bp, 2 * bp + b2] = 1.0
    parts["own"] = own.reshape(128, 4 * DB)
    sel_t = np.zeros((128, 9)); sel_p = np.zeros((128, 128)); sel_s = np.zeros((128, 64))
    for m in range(9):
        sel_t[m, m] = sel_t[32 + m, m] = 1.0
    sel_t[41, :] = 1.0
    sel_p[[0, 32, 41], :] = 1.0
    for b in range(DB):
        sel_s[[1 + b, 33 + b], b * DS:(b + 1) * DS] = 1.0
    sel_s[41, :] = 1.0
    parts["sel_t"], parts["sel_p"], parts["sel_s"] = sel_t, sel_p, sel_s
    heads = np.zeros((128, 64)); step = np.zeros((128, 64))
    for h in range(H):
        heads[h, h * DS:(h + 1) * DS] = 1.0
        for t in range(DS):
            step[h * DS + t, t::DS] = 1.0
    parts["heads"], parts["step"] = heads, step
    inv = np.zeros((128, 4, 16))
    for g, w in enumerate(WINDOWS):
        inv[:, g, :] = 1.0 / np.minimum(np.arange(16) + 1, w)
    parts["invcnt"] = inv.reshape(128, 64)
    new = np.zeros((128, 8))
    for b in range(DB):
        for t in range(DS):
            new[b * DS + t, t + 1:] = NEG
    parts["newmask"] = new
    at, spans = 0, {}
    for k, v in parts.items():
        spans[k] = (at, at + v.shape[1])
        at += v.shape[1]
    return np.concatenate(list(parts.values()), axis=1).astype(np.float32), spans


FILL = [*range(12, 20), *range(8, 12), *range(20, 24)]


def plan_pieces():
    p = [("ada", i) for i in range(8)]
    p += [("qi", 0), ("qi", 1), ("kiwi", 0), ("k", 0), ("k", 1), ("u", 0), ("u", 1)]
    p += [("q", 0), ("q", 1), ("v", 0), ("v", 1), ("poolw", 0)]
    p += [("ada", i) for i in FILL]
    p += [("wo", i) for i in range(4)]
    for f in range(QF):
        p += [("w1", 4 * f + i) for i in range(4)] + [("w2", 4 * f + i) for i in range(4)]
    return p


PIECES = plan_pieces()
AT = {key: n for n, key in enumerate(PIECES)}
COL0 = {"qi": OFF_QI, "k": OFF_K, "q": OFF_Q, "v": OFF_V, "u": 0}
ADA_ROW = {i: (i if i < 8 else i - 12 if 12 <= i < 20 else i - 8 if i < 12 else i - 16) for i in range(24)}


def piece_size(kind):
    return {"kiwi": KC * 136, "poolw": NG * 128}.get(kind, 2048)


def plan_banks():
    use, count = {}, [0] * 8

    def take(key, bank):
        count[bank] += 1
        use[key] = (bank, count[bank])

    take("cT", 3)
    take("rowsT", 4)
    for i in range(8):
        take(("ada", i), i % 2)
    take(("modT", 0), 3)
    for kc in range(KC):
        take(("hT", 0, kc), kc % 2)
    take(("hTS", 0), 2)
    for i in range(2):
        take(("qi", 2 * i), 0), take(("qi", 2 * i + 1), 1), take(("qiS", i), 2)
    take("ki", 0), take("kiS", 2), take("kiwi", 3)
    take("wiT", 4), take("wiR", 5)
    take("biasrow", 6)
    for j in range(4):
        take(("toep", j), 6 + j % 2)
    take("toepS", 6)
    for t in range(1, NT):
        for h in range(H):
            take(("ix", t, h), 3 + h % 2)
    for b in range(DB):
        take(("kxT", b), 5)
        take(("ixS", b), 6), take(("ixSn", b), 7)
        if b == 0:
            take("scS", 3), take("scSn", 4)
    take("hist", 5)
    for kind in ("k", "u", "q"):
        for i in range(2):
            take((kind, 2 * i), 0), take((kind, 2 * i + 1), 1), take((kind + "S", i), 2)
            if kind == "u":
                for g in (2 * i, 2 * i + 1):
                    take(("uo", g), 3 + g % 2)
        if kind == "k":
            for t in range(NT + 1):
                take(("kout", t), 5 + t % 2)
    for t in range(NT + 1):
        take(("v", t), 3 + t)
    for g in range(NG):
        take(("pm", g), g % 2), take(("pmS", g), 2)
    for n in range(NT * H + 4):
        if n < NT * H:
            take(("lg", n), 3 + n % 2)
        if n >= 4:
            take(("pv", n - 4), 6 + n % 2)
        if 2 <= n <= NT * H + 1:
            take(("pT", n - 2), 5 if n % 2 else 2)
        if n < NT * H and n % 2 == 1:
            take(("ada", FILL[n // 2]), (n // 2) % 2)
        if n == 17:
            take(("modT", 1), 2)
    for b in range(DB):
        for c in range(4):
            take(("KT", b, c), c % 2)
    for bp in range(4):
        take(("lgS", bp), 3), take(("lgSn", bp), 4)
        take(("pTS", bp), 5), take(("pTSn", bp), 6)
        take(("pvS", bp), 7)
    for j in range(2):
        take(("gP", 0, j), j), take(("gS", 0, j), 2)
    for nh in range(2):
        for t in range(NT + 1):
            take(("wo", nh, t), 3 + t)
    for kc in range(KC):
        take(("hT", 1, kc), kc % 2)
    take(("hTS", 1), 2)
    for j in range(2):
        take(("gP", 1, j), j), take(("gS", 1, j), 2)
    for f in range(QF):
        for i in range(4):
            take(("w1", 8 * f + 2 * i), 0), take(("w1", 8 * f + 2 * i + 1), 1), take(("w1S", 4 * f + i), 2)
        for nh in range(2):
            for t in range(NT + 1):
                take(("w2", f, nh, t), 3 + t)
    return use


USE = plan_banks()


def last_use(kind, i):
    if kind == "ada":
        return ("ada", i)
    if kind in ("qi", "k", "q", "u"):
        return (kind + "S", i)
    return {"kiwi": "kiwi", "v": ("v", NT), "poolw": ("pmS", NG - 1)}.get(kind) or {
        "wo": ("wo", i // 2, NT), "w1": ("w1S", i), "w2": ("w2", i // 4, i % 4 // 2, NT)}[kind]


def build_program(nc, a, o, spans):
    ctx = ExitStack()
    with ctx:
        def sem(name):
            return ctx.enter_context(nc.semaphore(name))

        psum = [ctx.enter_context(nc.psum_tensor(f"bank{i}", [128, 512], F32)) for i in range(8)]

        def sb(name, shape, dt=F32, stack=ctx):
            return stack.enter_context(nc.sbuf_tensor(name, shape, dt))

        cst = sb("cst", [128, spans["newmask"][1]])
        raw = sb("raw", [128, NRAW, 2048])
        w_hi = sb("w_hi", [128, NSPLIT, 2048], F32R)
        w_lo = sb("w_lo", [128, NSPLIT, 2048], F32R)
        act_hi = sb("act_hi", [128, KC, TP], F32R)
        act_lo = sb("act_lo", [128, KC, TP], F32R)
        act_s = sb("act_s", [128, KC, 2 * TS], F32R)
        mod_rows = sb("mod_rows", [42, 2048])
        mod_t = sb("mod_t", [128, 4 * KC, 9])
        over = ExitStack()
        pu_hi = sb("pu_hi", [128, TP], F32R, over)
        pu_lo = sb("pu_lo", [128, TP], F32R, over)
        over.close()
        stage = sb("stage", [128, 2, TP])
        stage_s = sb("stage_s", [128, KC, TS])
        c_split = sb("c_split", [128, KC, 96], F32R)
        rows_t = sb("rows_t", [128, 20])
        ss = sb("ss", [128, 8])
        rstd = sb("rstd", [128, 8])

        def cc(name, rows=128):
            x, y = spans[name]
            return cst[0:rows, x:y]

        dram_bias = nc.dram_tensor("bias_rows", (H, 384), F32, kind="Internal").ap()

        mix = ExitStack()
        head = ExitStack()
        x_in = sb("x_in", [128, NT + 1, D], stack=head)
        x_nrm = sb("x_nrm", [128, NT + 1, D], stack=head)
        c_in = sb("c_in", [9, D], stack=head)
        rows_in = sb("rows_in", [20, 128], stack=head)
        head.close()
        q_hi = sb("q_hi", [128, 4, TP], F32R, mix)
        q_lo = sb("q_lo", [128, 4, TP], F32R, mix)
        k_hi = sb("k_hi", [128, 4, TP], F32R, mix)
        k_lo = sb("k_lo", [128, 4, TP], F32R, mix)
        qiv_hi = sb("qiv_hi", [128, 4, TP], F32R, mix)
        qiv_lo = sb("qiv_lo", [128, 4, TP], F32R, mix)
        kp_hi = sb("kp_hi", [128, TP + TS], F32R, mix)
        kp_lo = sb("kp_lo", [128, TP + TS], F32R, mix)
        ki_hi, ki_lo = kp_hi[:, 0:TP], kp_lo[:, 0:TP]
        pages = sb("pages", [128, 2, NPG, 512], stack=mix)
        score = [None] + [sb(f"score{t}", [128, 128 * (t + 1)], stack=mix) for t in range(1, NT)]
        score_s = sb("score_s", [TS, LS], stack=mix)
        probs = sb("probs", [128, 3, TP], stack=mix)
        rows = probs[:, :, :].rearrange("p a n -> p (a n)")[:, 0:2 * UW].rearrange("p (a n) -> p a n", a=2)
        toep = sb("toep", [128, H, 256], stack=mix)
        toep_s = sb("toep_s", [128, 136], stack=mix)
        small = sb("small", [128, 21], stack=mix)
        top8, zero1 = small[:, 0:8], small[:, 20:21]
        soft = small[:, 8:20].rearrange("p (m n) -> p m n", n=4)
        near = sb("near", [128, 2, TP], stack=mix)
        pt_hi, pt_lo = kp_hi, kp_lo
        slots = pages[:, :, :, :].rearrange("p s a b -> p (s a b)")
        u_t = slots[:, 0:NG * UW].rearrange("p (g u) -> p g u", g=NG)
        hist_t = slots[:, NG * UW:NG * (UW + DB * HIST)].rearrange("p (g n) -> p g n", g=NG)
        hist_in = pages[0:DB * HIST, 1, NPG - 1, :]
        qi_s = near[0:64, 0, :].rearrange("p (b n) -> p b n", b=DB)
        wi_b = near[0:64, 1, :].rearrange("p (b n) -> p b n", b=DB)
        tmp_s = near[0:TS, 1, :]
        brow = rows[0:H, 1, 0:384]
        expand = near[0:TS, 0, :]
        kiwi = sb("kiwi", [128, NT + 1, 72], stack=mix)
        wi = sb("wi", [128, NT + 1, 8], stack=mix)
        v_s = sb("v_s", [TS, 512], stack=mix)
        q_s = sb("q_s", [128, 4, TS], stack=mix)
        k_s = sb("k_s", [128, 4, TS], stack=mix)
        ki_s = sb("ki_s", [64, TS], stack=mix)
        wi_t = sb("wi_t", [8, TS], stack=mix)
        ident_r = sb("ident_r", [128, 128], F32R, mix)
        table = sb("table", [1, 32], I32, mix)
        relb = toep[0:NB, 0, 0:H]
        mix.close()
        dec = ExitStack()
        q_pad = sb("q_pad", [128, 4, DB, 64], stack=dec)
        k_t = sb("k_t", [128, 2, 4, PAST], stack=dec)
        p_t = sb("p_t", [128, 5, 128], stack=dec)
        p_new = sb("p_new", [128, 64], stack=dec)
        v_pages = sb("v_pages", [128, 2, NPG, 512], stack=dec)
        dec.close()
        mlp = ExitStack()
        hid_hi = sb("hid_hi", [128, 8, TP], F32R, mlp)
        hid_lo = sb("hid_lo", [128, 8, TP], F32R, mlp)
        hid_s = sb("hid_s", [128, 8, 2 * TS], F32R, mlp)
        x_res = sb("x_res", [128, NT + 1, D], stack=mlp)
        out_t = sb("out_t", [128, NT + 1, D], stack=mlp)
        gate_p = sb("gate_p", [128, D], stack=mlp)
        gate_s = sb("gate_s", [TS, D], stack=mlp)
        ln_post = sb("ln_post", [128, D], stack=mlp)
        half_s = sb("half_s", [TS, 512], stack=mlp)
        mlp.close()
        raw_landed = [sem(f"raw_landed{i}") for i in range(NRAW)]
        hi_ready, lo_ready = sem("hi_ready"), sem("lo_ready")
        bank_full = [sem(f"bank_full{i}") for i in range(8)]
        bank_free = [sem(f"bank_free{i}") for i in range(8)]
        act_chain, dve_chain, pool_chain = sem("act_chain"), sem("dve_chain"), sem("pool_chain")
        class Signals(dict):
            def __missing__(self, name):
                self[name] = sem(name)
                return self[name]

        S = Signals()
        stage_out = [sem("stage_out0"), sem("stage_out1")]
        k_page_in = [sem("k_page_in0"), sem("k_page_in1")]
        v_page_in = [sem("v_page_in0"), sem("v_page_in1")]
        block = ctx.enter_context(nc.Block())

        def full(eng, key):
            b, n = USE[key]
            eng.wait_ge(bank_full[b], n)
            return psum[b]

        def free(ins, key):
            ins.then_inc(bank_free[USE[key][0]], 1)

        def evacuated(eng, key):
            b, n = USE[key]
            eng.wait_ge(bank_free[b], n)

        class Chain:

            def __init__(self, eng, s):
                self.eng, self.s, self.n = eng, s, 0

            def __call__(self, ins):
                self.n += 1
                ins.then_inc(self.s, 1)
                self.eng.wait_ge(self.s, self.n)

        def rows_of(t):
            return 128 if t < NT else TS

        landed_at, total = [], [0] * NRAW
        for n, (kind, i) in enumerate(PIECES):
            total[n % NRAW] += 16 * (3 if kind == "kiwi" else 1)
            landed_at.append(total[n % NRAW])

        w_in = a["w_in"][0].rearrange("(c p) n -> p c n", p=128)
        ada = a["ada_w"][0].rearrange("(c p) n -> p c n", p=128)
        w_o = a["w_out"][0].rearrange("(c p) n -> p c n", p=128)
        w_1 = a["w_ff1"][0].rearrange("(c p) n -> p c n", p=128)
        w_2 = a["w_ff2"][0].rearrange("(c p) n -> p c n", p=128)
        ck = a["cache_k"][0].rearrange("g p h d -> g p (h d)")
        cv = a["cache_v"][0].rearrange("g p h d -> g p (h d)")
        cx = a["cache_kidx"][0]
        xp = a["x_prompt"][0].rearrange("(t p) d -> p t d", p=128)
        xs = a["x_sample"].rearrange("b t d -> (b t) d")
        kidx_pages = pages[:, 0, :, :].rearrange("p a (b d) -> p (a b) d", d=HD)
        hankel = pages[:, 1, :, :].rearrange("p a (h j) -> p (a h) j", j=256)
        hankel_s = rows[0:64, 0, 0:136]
        N_AT = NT * H

        def turned_probs(m):
            return (pt_hi[:, 0:TP], pt_lo[:, 0:TP]) if m % 2 == 0 else (pu_hi[:, :], pu_lo[:, :])

        @block.sync
        def _(sp):
            def load_piece(n):
                kind, i = PIECES[n]
                if n >= NRAW:
                    sp.wait_ge(lo_ready, n - NRAW + 1)
                s, r = raw_landed[n % NRAW], raw[:, n % NRAW, :]

                def view(c):
                    return r[:, 0:piece_size(kind)].rearrange("p (c n) -> p c n", c=c)

                if kind == "ada":
                    sp.dma_start(view(KC), ada[:, :, 256 * i:256 * i + 256]).then_inc(s, 16)
                elif kind in COL0:
                    x = COL0[kind] + 256 * i
                    sp.dma_start(view(KC), w_in[:, :, x:x + 256]).then_inc(s, 16)
                elif kind == "kiwi":
                    v = view(KC)
                    sp.dma_start(v[:, :, 0:64], w_in[:, :, OFF_KI:OFF_WI]).then_inc(s, 16)
                    sp.dma_start(v[:, :, 64:128], w_in[:, :, OFF_KI:OFF_WI]).then_inc(s, 16)
                    sp.dma_start(v[:, :, 128:136], w_in[:, :, OFF_WI:D_IN]).then_inc(s, 16)
                elif kind == "poolw":
                    sp.dma_start(view(NG), a["pool_w"][0].rearrange("g p n -> p g n")).then_inc(s, 16)
                elif kind == "wo":
                    nh, k = i // 2, 4 * (i % 2)
                    sp.dma_start(view(4), w_o[:, k:k + 4, 512 * nh:512 * nh + 512]).then_inc(s, 16)
                elif kind == "w1":
                    sp.dma_start(view(KC), w_1[:, :, 256 * i:256 * i + 256]).then_inc(s, 16)
                else:
                    f, nh, k = i // 4, i % 4 // 2, 4 * (i % 2)
                    sp.dma_start(view(4), w_2[:, 8 * f + k:8 * f + k + 4, 512 * nh:512 * nh + 512]).then_inc(s, 16)

            def page_of(i):
                return sp.value_load(table[0:1, i:i + 1], min_val=0, max_val=ck.shape[0] - 1)

            sp.dma_start(c_in[0:1, :], a["c_prompt"]).then_inc(S["c_in_landed"], 16)
            sp.dma_start(c_in[1:9, :], a["c_sample"]).then_inc(S["c_in_landed"], 16)
            sp.dma_start(cst[:], a["consts"]).then_inc(S["consts_in"], 16)
            load_piece(0)
            load_piece(1)
            sp.dma_start(x_in[:, 0:NT, :], xp).then_inc(S["x_landed"], 16)
            sp.dma_start(x_in[0:TS, NT, :], xs).then_inc(S["x_landed"], 16)
            for n in range(2, AT[("k", 0)]):
                load_piece(n)
            sp.wait_ge(S["table_in"], 16)
            for i in range(DB * NPG):
                sp.dma_start(kidx_pages[:, i, :], cx[bass.ds(page_of(i), 1)].rearrange("o p d -> (o p) d"))\
                    .then_inc(S["kidx_in"], 16)
            for n in range(AT[("k", 0)], AT[("ada", 12)] + 2):
                load_piece(n)

            def load_pages(b, cache, slots, landed):
                for g in range(NPG):
                    sp.dma_start(slots[:, b % 2, g, :],
                                 cache[bass.ds(page_of(b * NPG + g), 1)].rearrange("o p n -> (o p) n"))\
                        .then_inc(landed[b % 2], 16)

            sp.wait_ge(S["pool_lo"], NG)
            for b in range(2):
                load_pages(b, ck, pages, k_page_in)
            for n in range(AT[("ada", 12)] + 2, AT[("wo", 0)] + 2):
                load_piece(n)
            full(sp, ("pv", N_AT - 1))
            for bp in range(4):
                if bp == 0:
                    for b in range(2):
                        load_pages(b, cv, v_pages, v_page_in)
                if bp < 3:
                    for b in (2 * bp + 2, 2 * bp + 3):
                        full(sp, ("KT", b - 2, 3))
                        load_pages(b, ck, pages, k_page_in)
                if bp:
                    full(sp, ("pvS", bp - 1))
                    for b in (2 * bp, 2 * bp + 1):
                        load_pages(b, cv, v_pages, v_page_in)
            for n in range(AT[("wo", 0)] + 2, len(PIECES)):
                load_piece(n)

        @block.gpsimd
        def _(pool):
            link = Chain(pool, pool_chain)
            pool.dma_start(rows_in[0:8, :], a["ln1_pre"].rearrange("o (c p) -> (o c) p", p=128)).then_inc(S["small_in"], 16)
            pool.dma_start(rows_in[8:16, :], a["ln2_pre"].rearrange("o (c p) -> (o c) p", p=128)).then_inc(S["small_in"], 16)
            pool.dma_start(rows_in[16:20, :], a["pool_scale"].rearrange("o (c p) -> (o c) p", p=128)).then_inc(S["small_in"], 16)
            pool.dma_start(relb, a["rel_bias"]).then_inc(S["small_in"], 16)
            pool.dma_start(mod_rows[41:42, :], a["ada_b"][:, 0:2048]).then_inc(S["bias_in"], 16)
            pool.dma_start(table[:], a["page_table"].rearrange("a b -> (a b)").rearrange("(o n) -> o n", o=1))\
                .then_inc(S["table_in"], 16)
            pool.dma_start(o["pool_s"][0, :, 0:HIST - DS, :], a["state_pool"][0, :, DS:HIST, :]).then_inc(S["outs"], 16)
            nc.gpsimd.memset(wi_b, 0.0).then_inc(S["pad_zero"], 1)
            full(pool, ("modT", 0))
            pool.dma_start(mod_rows[41:42, :], a["ada_b"][:, 3072:5120]).then_inc(S["bias_in"], 16)
            evacuated(pool, "biasrow")
            pool.dma_start(dram_bias, brow[:]).then_inc(S["bias_row_out"], 16)
            pool.wait_ge(S["bias_row_out"], 16)
            pool.dma_start(hankel, bass.AP(tensor=dram_bias.tensor, offset=0, ap=[[1, 128], [384, H], [1, 256]]))\
                .then_inc(S["hankel_in"], 16)
            for h in range(H):
                pool.dma_start(rows[h * DS:(h + 1) * DS, 0, 0:136],
                               bass.AP(tensor=dram_bias.tensor, offset=384 * h + 120, ap=[[1, DS], [1, 136]]))\
                    .then_inc(S["hankel_s_in"], 16)
            evacuated(pool, "kiwi")
            pool.dma_start(o["kidx_p"][0, 0].rearrange("(t p) d -> p t d", p=128), kiwi[:, 0:NT, 0:64]).then_inc(S["outs"], 16)
            pool.dma_start(o["kidx_s"][0].rearrange("b t d -> (b t) d"), kiwi[0:TS, NT, 0:64]).then_inc(S["outs"], 16)

            full(pool, ("ixSn", DB - 1))
            full(pool, ("ixS", DB - 1))
            pool.dma_start(hist_in, a["state_pool"][0].rearrange("b i c -> (b i) c")).then_inc(S["hist_in"], 16)
            nc.gpsimd.memset(u_t, 0.0).then_inc(S["u_zero"], 1)

            stored = [0]

            def store(dst, rows_from, rows_to):
                n = stored[0]
                pool.dma_start(dst, stage[rows_from:rows_to, n % 2, :]).then_inc(stage_out[n % 2], 16)
                stored[0] += 1

            for t in range(NT):
                evacuated(pool, ("kout", t))
                store(o["k_p"][0, 0, 128 * t:128 * t + 128].rearrange("p h d -> p (h d)"), 0, 128)
            evacuated(pool, ("kout", NT))
            store(o["k_s"][0].rearrange("b t h d -> (b t) (h d)"), 0, TS)
            for g in range(NG):
                u = u_t[:, g, :]
                evacuated(pool, ("uS", g // 2))
                if g == 0:
                    evacuated(pool, "hist")
                    evacuated(pool, "scSn")
                link(nc.gpsimd.tensor_copy(u[:, 16 + TP:].rearrange("p (b s) -> p b s", b=DB)[:, :, 1:1 + HIST],
                                           hist_t[:, g, :].rearrange("p (b i) -> p b i", b=DB)))
                if g >= 1:
                    pool.wait_ge(S["pooled"], g)
                src, lo = u, 0
                for lev in range(g + 1):
                    sh = 1 << lev
                    lo += sh
                    dst = rows[:, lev % 2, :]
                    link(nc.gpsimd.tensor_tensor(dst[:, lo:UW], src[:, lo:UW], src[:, lo - sh:UW - sh], ALU.add))
                    src = dst
                dst = rows[:, (g + 1) % 2, :]
                link(nc.gpsimd.tensor_scalar(dst[:, 16:UW], src[:, 16:UW], 1.0 / WINDOWS[g], None, ALU.mult))
                link(nc.gpsimd.tensor_tensor(dst[:, 16:32], src[:, 16:32], cc("invcnt")[:, 16 * g:16 * g + 16], ALU.mult))
                full(pool, ("uo", g))
                nc.gpsimd.tensor_tensor(u[:, 16:UW], dst[:, 16:UW], u[:, 16:UW], ALU.subtract).then_inc(S["pooled"], 1)
            evacuated(pool, ("uo", NG - 1))
            pool.dma_start(o["pool_p"][0, 0], near[128 - HIST:128, 0, :]).then_inc(S["state_out"], 16)
            for b in range(DB):
                pool.dma_start(o["pool_s"][0, b, HIST - DS:HIST, :], near[b * DS:(b + 1) * DS, 0, :])\
                    .then_inc(S["state_out"], 16)
            for t in range(NT):
                pool.wait_ge(S["v_staged"], t + 1)
                store(o["v_p"][0, 0, 128 * t:128 * t + 128].rearrange("p h d -> p (h d)"), 0, 128)
            evacuated(pool, ("v", NT))
            pool.dma_start(o["v_s"][0].rearrange("b t h d -> (b t) (h d)"), v_s[:]).then_inc(S["outs"], 16)

            pool.wait_ge(S["state_out"], 16 * (1 + DB))
            evacuated(pool, ("v", NT))
            for t in range(NT):
                L = 128 * (t + 1)
                w = min(L, 256)
                mask = cc("causal") if t == 0 else score[t]
                pool.wait_ge(S["chosen"], t)
                if t == 0:
                    evacuated(pool, ("toep", 3))
                for h in range(H):
                    n = t * H + h
                    if n >= 2:
                        pool.wait_ge(S["peaks"], n - 1)
                    if n == 18:
                        full(pool, ("modT", 1))
                        pool.dma_start(mod_rows[41:42, 0:1024], a["ada_b"][:, 2048:3072]).then_inc(S["bias_in"], 16)
                        pool.dma_start(mod_rows[41:42, 1024:2048], a["ada_b"][:, 5120:6144]).then_inc(S["bias_in"], 16)
                    if h < 2 and L > w:
                        link(nc.gpsimd.tensor_copy(near[:, n % 2, 0:L - w], mask[:, 0:L - w]))
                    nc.gpsimd.tensor_tensor(near[:, n % 2, L - w:L], toep[:, h, 256 - w:256], mask[:, L - w:L],
                                            ALU.add).then_inc(S["near_ok"], 1)
            evacuated(pool, ("qS", 1))
            full(pool, ("pv", N_AT - 1))
            link(nc.gpsimd.tensor_copy(expand.rearrange("p (b h t) -> p b h t", b=DB, h=H),
                                       cc("ident", TS)[:, 0:TS].rearrange("p (b t) -> p b t", b=DB).unsqueeze(2)
                                       .to_broadcast([TS, DB, H, DS])))
            link(nc.gpsimd.memset(q_pad[:], 0.0))
            for c in range(4):
                for hh in range(2):
                    nc.gpsimd.tensor_copy(
                        q_pad[64 * hh:64 * hh + 64, c, :, (2 * c + hh) * DS:(2 * c + hh + 1) * DS],
                        q_s[64 * hh:64 * hh + 64, c, :].rearrange("p (b t) -> p b t", b=DB)).then_inc(S["padded"], 1)
            evacuated(pool, ("pvS", 3))
            pool.wait_ge(S["outs"], 16 * 4)
            pool.dma_start(x_res[:, 0:NT, :], xp).then_inc(S["x_again"], 16)
            pool.dma_start(x_res[0:TS, NT, :], xs).then_inc(S["x_again"], 16)
            pool.dma_start(ln_post[:], a["ln1_post"].to_broadcast([128, D])).then_inc(S["gain_in"], 16)
            evacuated(pool, ("gS", 0, 1))
            pool.dma_start(ln_post[:], a["ln2_post"].to_broadcast([128, D])).then_inc(S["gain_in"], 16)
            yp = o["y_p"][0].rearrange("(t p) d -> p t d", p=128)
            for t in range(NT + 1):
                pool.wait_ge(S["y_ok"], t + 1)
                if t < NT:
                    pool.dma_start(yp[:, t, :], x_res[:, t, :]).then_inc(S["y_out"], 16)
                else:
                    pool.dma_start(o["y_s"].rearrange("b t d -> (b t) d"), x_res[0:TS, t, :]).then_inc(S["y_out"], 16)
            pool.wait_ge(S["y_out"], 16 * (NT + 1))
            for n in (stored[0], stored[0] + 1):
                pool.wait_ge(stage_out[n % 2], 16 * (n // 2))
            pool.wait_ge(S["outs"], 16 * 4)

        @block.tensor
        def _(pe):
            uses = [0] * 8

            def claim(key):
                b, n = USE[key]
                uses[b] += 1
                assert n == uses[b], key
                if n > 1:
                    pe.wait_ge(bank_free[b], n - 1)
                return psum[b]

            def done(ins, key):
                ins.then_inc(bank_full[USE[key][0]], 1)

            def piece(kind, i):
                n = AT[(kind, i)]
                pe.wait_ge(lo_ready, n + 1)
                s, size = n % NSPLIT, piece_size(kind)
                return w_hi[:, s, 0:size], w_lo[:, s, 0:size]

            def mm(out, lhsT, rhs, start, stop):
                return nc.tensor.matmul(out, lhsT, rhs, start=start, stop=stop, skip_group_check=True)

            def turn(out, in_, k, start=True, stop=True):
                return nc.tensor.transpose(out, in_, cc("ident")[0:k, 0:k])

            pe.wait_ge(S["c_in_landed"], 32)
            pe.wait_ge(S["consts_in"], 16)
            t_ = claim("cT")
            for kc in range(KC):
                last = turn(t_[:, 9 * kc:9 * kc + 9], c_in[:, 128 * kc:128 * kc + 128], 9)
            done(last, "cT")
            pe.wait_ge(S["small_in"], 64)
            done(turn(claim("rowsT")[:, 0:20], rows_in[:, :], 20), "rowsT")
            pe.wait_ge(S["c_hi"], 1)
            evacuated(pe, "cT")

            def modulation(i):
                hi, lo = (w.rearrange("p (c n) -> p c n", c=KC) for w in piece("ada", i))
                out = claim(("ada", i))[0:96, 0:256]
                for kc in range(KC):
                    mm(out, c_split[:, kc, :], hi[:, kc, :], kc == 0, False)
                    last = mm(out, c_split[:, kc, :], lo[:, kc, :], False, kc == KC - 1)
                done(last, ("ada", i))

            def turned_modulation(k):
                evacuated(pe, ("ada", 7 + 12 * k))
                pe.wait_ge(S["bias_in"], 16 * (k + 1))
                out = claim(("modT", k))
                for j in range(16):
                    last = mm(out[:, 9 * j:9 * j + 9], mod_rows[:, 128 * j:128 * j + 128], cc("sel_t", 42), True, True)
                done(last, ("modT", k))

            def turned_hidden(k, src):
                pe.wait_ge(S["normed"], (NT + 1) * (k + 1))
                for kc in range(KC):
                    out = claim(("hT", k, kc))
                    for t in range(NT):
                        last = turn(out[:, 128 * t:128 * t + 128], src[:, t, 128 * kc:128 * kc + 128], 128)
                    done(last, ("hT", k, kc))
                out = claim(("hTS", k))
                for kc in range(KC):
                    last = turn(out[:, TS * kc:TS * kc + TS], src[0:TS, NT, 128 * kc:128 * kc + 128], TS)
                done(last, ("hTS", k))

            for i in range(8):
                modulation(i)
            turned_modulation(0)
            turned_hidden(0, x_nrm)

            def chunk_p(out, hi, lo, cols):
                for kc in range(KC):
                    mm(out, hi[:, kc, cols], act_hi[:, kc, :], kc == 0, False)
                    mm(out, hi[:, kc, cols], act_lo[:, kc, :], False, False)
                    last = mm(out, lo[:, kc, cols], act_hi[:, kc, :], False, kc == KC - 1)
                return last

            def chunk_s(out, hi, lo, cols):
                for kc in range(KC):
                    mm(out, hi[:, kc, cols], act_s[:, kc, 0:TS], kc == 0, False)
                    mm(out, hi[:, kc, cols], act_s[:, kc, TS:2 * TS], False, False)
                    last = mm(out, lo[:, kc, cols], act_s[:, kc, 0:TS], False, kc == KC - 1)
                return last

            def project(kind, i, key=None):
                key = key or kind
                hi, lo = (w.rearrange("p (c n) -> p c n", c=KC) for w in piece(kind, i))
                for j in range(2):
                    k = (key, 2 * i + j)
                    done(chunk_p(claim(k)[:, :], hi, lo, slice(128 * j, 128 * j + 128)), k)
                k = (key + "S", i)
                out = claim(k)
                for j in range(2):
                    last = chunk_s(out[:, TS * j:TS * j + TS], hi, lo, slice(128 * j, 128 * j + 128))
                done(last, k)

            evacuated(pe, ("hT", 0, 7))
            pe.wait_ge(S["h_hi"], KC)
            evacuated(pe, ("hTS", 0))
            pe.wait_ge(S["h_low"], KC)
            pe.wait_ge(S["hs_lo"], 1)
            for i in range(2):
                project("qi", i)
            hi, lo = (w.rearrange("p (c n) -> p c n", c=KC) for w in piece("kiwi", 0))
            done(chunk_p(claim("ki")[:, :], hi, lo, slice(0, 128)), "ki")
            done(chunk_s(claim("kiS")[:, 0:TS], hi, lo, slice(0, 128)), "kiS")
            out = claim("kiwi")
            for t in range(NT + 1):
                y = out[:, 72 * t:72 * t + 72]
                for kc in range(KC):
                    if t < NT:
                        tok = slice(128 * t, 128 * t + 128)
                        mm(y, act_hi[:, kc, tok], hi[:, kc, 64:136], kc == 0, False)
                        mm(y, act_hi[:, kc, tok], lo[:, kc, 64:136], False, False)
                        last = mm(y, act_lo[:, kc, tok], hi[:, kc, 64:136], False, kc == KC - 1)
                    else:
                        mm(y, act_s[:, kc, :], hi[:, kc, 64:136], kc == 0, False)
                        last = mm(y, act_s[:, kc, :], lo[:, kc, 64:136], False, kc == KC - 1)
            done(last, "kiwi")
            out = claim("biasrow")
            done(mm(out[0:H, 0:384], relb, cc("bucket", NB), True, True), "biasrow")
            pe.wait_ge(S["wi_ok"], 1)
            done(turn(claim("wiT")[0:H, 0:TS], wi[0:TS, NT, :], TS), "wiT")
            evacuated(pe, "wiT")
            done(mm(claim("wiR")[0:64, 0:TS], cc("heads", H), wi_t[:, :], True, True), "wiR")
            pe.wait_ge(S["hankel_in"], 16)
            for j in range(4):
                done(mm(claim(("toep", j))[:, :], cc("flip"), hankel[:, 2 * j:2 * j + 2, :], True, True), ("toep", j))
            pe.wait_ge(S["hankel_s_in"], 16 * H)
            done(mm(claim("toepS")[:, 0:136], cc("unflip", 64), hankel_s, True, True), "toepS")

            def by_head(out, q_h, q_l, k_h, k_l, h, tok, L):
                r, c = slice(64 * (h % 2), 64 * (h % 2) + 64), h // 2
                mm(out, q_h[r, c, tok], k_h(r, c), True, False)
                mm(out, q_h[r, c, tok], k_l(r, c), False, False)
                return mm(out, q_l[r, c, tok], k_h(r, c), False, True)

            evacuated(pe, ("qi", 3))
            evacuated(pe, "ki")
            for t in range(1, NT):
                L = 128 * (t + 1)
                for h in range(H):
                    out = claim(("ix", t, h))
                    done(by_head(out[:, 0:L], qiv_hi, qiv_lo, lambda r, c: ki_hi[r, 0:L], lambda r, c: ki_lo[r, 0:L],
                                 h, slice(128 * t, 128 * t + 128), L), ("ix", t, h))
            kx_t = pages[0:64, 1, :, :].rearrange("p a b -> p (a b)")
            pe.wait_ge(S["kidx_in"], 16 * DB * NPG)
            evacuated(pe, "kiS")
            evacuated(pe, ("qiS", 1))
            evacuated(pe, "wiR")

            def turn_kidx(b):
                out = claim(("kxT", b))
                for g in range(NPG):
                    last = turn(out[0:64, 128 * g:128 * g + 128], kidx_pages[:, NPG * b + g, :], 128)
                done(last, ("kxT", b))

            turn_kidx(0)
            for b in range(DB):
                evacuated(pe, ("kxT", b))
                done(mm(claim(("ixS", b))[0:64, :], qi_s[:, b, :], kx_t[:, 512 * (b % 2):512 * (b % 2) + 512], True, True), ("ixS", b))
                done(mm(claim(("ixSn", b))[0:64, 0:DS], qi_s[:, b, :], ki_s[:, b * DS:(b + 1) * DS], True, True), ("ixSn", b))
                if b + 1 < DB:
                    turn_kidx(b + 1)
                if b == 0:
                    sc, scn = claim("scS"), claim("scSn")
                evacuated(pe, ("ixSn", b))
                evacuated(pe, ("ixS", b))
                last1 = mm(sc[0:TS, :], wi_b[:, b, :], rows[0:64, b % 2, 0:PAST], b == 0, b == DB - 1)
                last2 = mm(scn[0:TS, 0:DS], wi_b[:, b, :], rows[0:64, b % 2, PAST:LS], b == 0, b == DB - 1)
                if b == DB - 1:
                    done(last1, "scS")
                    done(last2, "scSn")
                else:
                    last2.then_inc(S["relu_used"], 1)

            for i in range(2):
                project("k", i)
                if i == 0:
                    pe.wait_ge(S["hist_in"], 16)
                    out = claim("hist")
                    for g in range(NG):
                        last = turn(out[:, 120 * g:120 * g + 120], hist_in[:, 128 * g:128 * g + 128], 120)
                    done(last, "hist")

            def turn_keys():
                evacuated(pe, ("k", 3))
                evacuated(pe, ("kS", 1))
                pe.wait_ge(S["ident_ok"], 1)
                for t in range(NT + 1):
                    out = claim(("kout", t))
                    for c in range(4):
                        y = out[:, 128 * c:128 * c + 128]
                        if t < NT:
                            mm(y, k_hi[:, c, 128 * t:128 * t + 128], ident_r[:, :], True, False)
                            last = mm(y, k_lo[:, c, 128 * t:128 * t + 128], ident_r[:, :], False, True)
                        else:
                            last = turn(y[0:TS, :], k_s[:, c, :], 128)
                    done(last, ("kout", t))

            for i in range(2):
                project("u", i)
                evacuated(pe, ("u", 2 * i + 1))
                evacuated(pe, ("uS", i))
                for g in (2 * i, 2 * i + 1):
                    out = claim(("uo", g))
                    turn(out[:, 0:128], u_t[:, g, 16 + TP - 128:16 + TP], 128)
                    done(turn(out[0:TS, 128:256], stage_s[:, g % 2, :], 128), ("uo", g))
            project("q", 0)
            turn_keys()
            project("q", 1)
            outs = [claim(("v", t)) for t in range(NT + 1)]
            for i in range(2):
                hi, lo = (w.rearrange("p (c n) -> p c n", c=KC) for w in piece("v", i))
                for t in range(NT + 1):
                    y = outs[t][:, 256 * i:256 * i + 256]
                    for kc in range(KC):
                        if t < NT:
                            tok = slice(128 * t, 128 * t + 128)
                            mm(y, act_hi[:, kc, tok], hi[:, kc, :], kc == 0, False)
                            mm(y, act_hi[:, kc, tok], lo[:, kc, :], False, False)
                            last = mm(y, act_lo[:, kc, tok], hi[:, kc, :], False, kc == KC - 1)
                        else:
                            mm(y, act_s[:, kc, :], hi[:, kc, :], kc == 0, False)
                            last = mm(y, act_s[:, kc, :], lo[:, kc, :], False, kc == KC - 1)
                    if i == 1:
                        done(last, ("v", t))
                    elif t == NT:
                        last.then_inc(S["v_half"], 1)
            hi, lo = piece("poolw", 0)
            for g in range(NG):
                pe.wait_ge(S["pool_lo"], g + 1)
                wh, wl = hi[:, 128 * g:128 * g + 128], lo[:, 128 * g:128 * g + 128]
                for key, cols in ((("pm", g), slice(0, TP)), (("pmS", g), slice(TP, TP + TS))):
                    out = claim(key)[:, 0:cols.stop - cols.start]
                    mm(out, wh, pt_hi[:, cols], True, False)
                    mm(out, wh, pt_lo[:, cols], False, False)
                    done(mm(out, wl, pt_hi[:, cols], False, True), key)

            evacuated(pe, ("q", 3))
            evacuated(pe, ("v", NT))
            for n in range(N_AT + 4):
                if n < N_AT:
                    t, h = n // H, n % H
                    L = 128 * (t + 1)
                    out = claim(("lg", n))
                    done(by_head(out[:, 0:L], q_hi, q_lo, lambda r, c: k_hi[r, c, 0:L], lambda r, c: k_lo[r, c, 0:L],
                                 h, slice(128 * t, 128 * t + 128), L), ("lg", n))
                if n >= 4:
                    m = n - 4
                    t, h = m // H, m % H
                    evacuated(pe, ("pT", m))
                    out = claim(("pv", m))[:, 0:128]
                    ph, pl = turned_probs(m)
                    for kb in range(t + 1):
                        v = slice(128 * (h // 2), 128 * (h // 2) + 128)
                        p = slice(128 * kb, 128 * kb + 128)
                        mm(out, qiv_hi[:, kb, v], ph[:, p], kb == 0, False)
                        mm(out, qiv_hi[:, kb, v], pl[:, p], False, False)
                        last = mm(out, qiv_lo[:, kb, v], ph[:, p], False, kb == t)
                    done(last, ("pv", m))
                if 2 <= n <= N_AT + 1:
                    m = n - 2
                    pe.wait_ge(S["probs_ok"], m + 1)
                    out = claim(("pT", m))
                    for kb in range(m // H + 1):
                        last = turn(out[:, 128 * kb:128 * kb + 128], probs[:, m % 3, 128 * kb:128 * kb + 128], 128)
                    done(last, ("pT", m))
                if n < N_AT and n % 2 == 1:
                    modulation(FILL[n // 2])
                if n == 17:
                    turned_modulation(1)

            def turn_pages(b):
                pe.wait_ge(k_page_in[b % 2], 16 * NPG * (b // 2 + 1))
                for c in range(4):
                    out = claim(("KT", b, c))
                    for g in range(NPG):
                        last = turn(out[:, 128 * g:128 * g + 128], pages[:, b % 2, g, 128 * c:128 * c + 128], 128)
                    done(last, ("KT", b, c))

            turn_pages(0)
            turn_pages(1)
            pe.wait_ge(S["padded"], 8)
            pe.wait_ge(S["chosen"], NT)
            evacuated(pe, ("kS", 1))
            for bp in range(4):
                out, new = claim(("lgS", bp)), claim(("lgSn", bp))
                ex = expand[:, 128 * bp:128 * bp + 128]
                mm(out[:, :], ex, score_s[:, 0:PAST], True, False)
                mm(new[:, 0:DS], ex, score_s[:, PAST:LS], True, False)
                for b2 in range(2):
                    b, r = 2 * bp + b2, slice(64 * b2, 64 * b2 + 64)
                    for c in range(4):
                        evacuated(pe, ("KT", b, c))
                        last1 = mm(out[r, :], q_pad[:, c, b, :], k_t[:, b2, c, :], False, c == 3 and b2 == 1)
                        last2 = mm(new[r, 0:DS], q_pad[:, c, b, :], k_s[:, c, b * DS:(b + 1) * DS], False, c == 3 and b2 == 1)
                done(last1, ("lgS", bp))
                done(last2, ("lgSn", bp))
                if bp < 3:
                    turn_pages(2 * bp + 2)
                    turn_pages(2 * bp + 3)
                pe.wait_ge(S["prob_new"], bp + 1)
                out = claim(("pTS", bp))
                for g in range(NPG):
                    last = turn(out[:, 128 * g:128 * g + 128], rows[:, bp % 2, 128 * g:128 * g + 128], 128)
                done(last, ("pTS", bp))
                done(turn(claim(("pTSn", bp))[0:64, 0:128], p_new[:, :], 128), ("pTSn", bp))
                evacuated(pe, ("pTSn", bp))
                evacuated(pe, ("pTS", bp))
                out = claim(("pvS", bp))
                for b2 in range(2):
                    pe.wait_ge(v_page_in[b2], 16 * NPG * (bp + 1))
                    for c in range(4):
                        y = out[:, 16 * (4 * b2 + c):16 * (4 * b2 + c) + 16]
                        col = slice(64 * b2 + 16 * c, 64 * b2 + 16 * c + 16)
                        v = slice(128 * c, 128 * c + 128)
                        for g in range(NPG):
                            mm(y, v_pages[:, b2, g, v], p_t[:, g, col], g == 0, False)
                        last = mm(y, v_s[:, v], p_t[0:64, 4, col], False, True)
                done(last, ("pvS", bp))

            pe.wait_ge(S["bias_in"], 16 * 4)

            def gates(k):
                for j in range(2):
                    r = mod_rows[:, 1024 * k + 512 * j:1024 * k + 512 * j + 512]
                    done(mm(claim(("gP", k, j))[:, :], cc("sel_p", 42), r, True, True), ("gP", k, j))
                    done(mm(claim(("gS", k, j))[0:TS, :], cc("sel_s", 42), r, True, True), ("gS", k, j))

            evacuated(pe, ("ada", 22))
            evacuated(pe, ("ada", 23))
            gates(0)

            def by_token(kind, first, name, x_hi, x_lo, x_s, f=None):
                outs = [claim(name + (t,)) for t in range(NT + 1)]
                for half in range(2):
                    hi, lo = (w.rearrange("p (c n) -> p c n", c=4) for w in piece(kind, first + half))
                    if f is not None:
                        pe.wait_ge(S["w1_done"], 8 * f + 4 * (half + 1))
                        pe.wait_ge(S["w1s_done"], 4 * f + 2 * (half + 1))
                    for t in range(NT + 1):
                        for k4 in range(4):
                            k = 4 * half + k4
                            if t < NT:
                                tok = slice(128 * t, 128 * t + 128)
                                mm(outs[t][:, :], x_hi[:, k, tok], hi[:, k4, :], k == 0, False)
                                mm(outs[t][:, :], x_hi[:, k, tok], lo[:, k4, :], False, False)
                                last = mm(outs[t][:, :], x_lo[:, k, tok], hi[:, k4, :], False, k == 7)
                            else:
                                mm(outs[t][:, :], x_s[:, k, :], hi[:, k4, :], k == 0, False)
                                last = mm(outs[t][:, :], x_s[:, k, :], lo[:, k4, :], False, k == 7)
                        if half == 1:
                            done(last, name + (t,))
                    if half == 0:
                        last.then_inc(S["half_done"], 1)

            evacuated(pe, ("pmS", NG - 1))
            evacuated(pe, ("pm", NG - 1))
            evacuated(pe, ("pv", N_AT - 1))
            evacuated(pe, ("pvS", 3))
            for nh in range(2):
                by_token("wo", 2 * nh, ("wo", nh), act_hi, act_lo, act_s)

            turned_hidden(1, out_t)
            gates(1)
            evacuated(pe, ("hT", 1, 7))
            pe.wait_ge(S["h_hi"], 2 * KC)
            pe.wait_ge(S["h_low"], 2 * KC)
            pe.wait_ge(S["hs_lo"], 2)
            for f in range(QF):
                for i in range(4):
                    project("w1", 4 * f + i)
                for nh in range(2):
                    by_token("w2", 4 * f + 2 * nh, ("w2", f, nh), hid_hi, hid_lo, hid_s, f)

        def split_hi_of(act, n):
            kind, i = PIECES[n]
            act.wait_ge(raw_landed[n % NRAW], landed_at[n])
            if n >= NSPLIT:
                pk = PIECES[n - NSPLIT]
                piece_used(act, pk)
            size = piece_size(kind)
            nc.scalar.activation(w_hi[:, n % NSPLIT, 0:size], raw[:, n % NRAW, 0:size], ACT.Copy).then_inc(hi_ready, 1)

        def piece_used(eng, pk):
            kind, i = pk
            if kind == "v" and i == 0:
                eng.wait_ge(S["v_half"], 1)
            elif kind == "wo" and i % 2 == 0:
                eng.wait_ge(S["half_done"], 1 + i // 2)
            elif kind == "w2" and i % 2 == 0:
                eng.wait_ge(S["half_done"], 3 + i // 2)
            else:
                full(eng, last_use(kind, i))

        @block.scalar
        def _(act):
            link = Chain(act, act_chain)
            split = [0]

            def hi_until(n):
                while split[0] < min(n, len(PIECES)):
                    split_hi_of(act, split[0])
                    split[0] += 1

            def run(out, in_, func=ACT.Copy, **kw):
                return nc.scalar.activation(out, in_, func, **kw)

            squared = [0]

            def squares(src):
                junk = stage[:, :, :].rearrange("p a n -> p (a n)")
                for t in range(NT + 1):
                    r = rows_of(t)
                    if squared[0]:
                        act.wait_ge(S["squares"], squared[0])
                    squared[0] += 1
                    run(junk[0:r, :], src[0:r, t, :], ACT.Square, accum_out=ss[0:r, t:t + 1]).then_inc(S["squares"], 1)

            def root(k):
                act.wait_ge(S["mean_ok"], k + 1)
                run(rstd[:, 0:NT + 1], ss[:, 0:NT + 1], ACT.Sqrt).then_inc(S["root_ok"], 1)

            def turned_hidden(k):
                act.wait_ge(S["mod_ok"], 2 * (k + 1))
                for kc in range(KC):
                    out = full(act, ("hT", k, kc))
                    n = k * KC + kc
                    if k * KC + kc >= 2:
                        act.wait_ge(S["h_low"], n - 1)
                    free(run(stage[:, kc % 2, :], out[:, :], ACT.Identity,
                             scale=mod_t[:, 16 * k + 8 + kc, 0:1], bias=mod_t[:, 16 * k + kc, 0:1]), ("hT", k, kc))
                    evacuated(act, ("hT", k, kc))
                    run(act_hi[:, kc, :], stage[:, kc % 2, :]).then_inc(S["h_hi"], 1)
                act.wait_ge(S["hs_staged"], k + 1)
                run(act_s[:, :, 0:TS], stage_s[:, :, :]).then_inc(S["hs_hi"], 1)

            act.wait_ge(S["pad_zero2"], 1)
            out = full(act, "cT")
            run(c_split[:, :, 0:9], out[:, 0:72].rearrange("p (c m) -> p c m", m=9)).then_inc(S["c_hi"], 1)
            hi_until(2)
            free(run(rows_t[:, :], full(act, "rowsT")[:, 0:20]), "rowsT")
            act.wait_ge(S["pad_zero2"], 2)
            act.wait_ge(S["x_landed"], 32)
            squares(x_in)
            root(0)

            def modulation(i):
                out = full(act, ("ada", i))
                hi_until(AT[("ada", i)] + 3)
                if i in (12, 8):
                    full(act, ("modT", 0 if i == 12 else 1))
                x = 256 * ADA_ROW[i]
                free(run(mod_rows[0:41, x:x + 256], out[0:41, 0:256]), ("ada", i))

            for i in range(8):
                modulation(i)
            turned_hidden(0)

            def pair(kind, i, chunk, tail):
                for j in range(2):
                    chunk(2 * i + j, full(act, (kind, 2 * i + j)))
                n = AT[(kind, i)]
                hi_until(n + 3)
                tail(i, full(act, (kind + "S", i)))

            def qi_tail(i, out):
                for hh in range(2):
                    ins = run(qi_s.rearrange("p b (c x t) -> p x c b t", x=2, t=DS)[:, hh, 2 * i:2 * i + 2],
                              out[64 * hh:64 * hh + 64, 0:2 * TS].rearrange("p (c b t) -> p c b t", c=2, b=DB))
                free(ins, ("qiS", i))

            for i in range(2):
                pair("qi", i, lambda c, out: run(qiv_hi[:, c, :], out[:, :]).then_inc(S["proj_hi"], 1), qi_tail)
            run(ki_hi[:, :], full(act, "ki")[:, :]).then_inc(S["proj_hi"], 1)
            free(run(ki_s[:, :], full(act, "kiS")[0:64, 0:TS]), "kiS")
            out = full(act, "kiwi")
            hi_until(AT[("kiwi", 0)] + 3)
            run(kiwi[:, 0:NT, :], out[:, 0:72 * NT].rearrange("p (t n) -> p t n", t=NT)).then_inc(S["wi_low"], 1)
            run(stage_s[0:TS, 0:2, :].rearrange("p a b -> p (a b)")[:, 0:72], out[TS:2 * TS, 72 * NT:72 * NT + 72])\
                .then_inc(S["wi_low"], 1)
            run(brow[:, :], full(act, "biasrow")[0:H, 0:384]).then_inc(bank_free[USE["biasrow"][0]], 1)
            free(run(wi_t[:, :], full(act, "wiT")[0:H, 0:TS]), "wiT")
            for j in range(4):
                free(run(toep[:, 2 * j:2 * j + 2, :], full(act, ("toep", j))[:, :].rearrange("p (h j) -> p h j", h=2)), ("toep", j))
            free(run(toep_s[:, :], full(act, "toepS")[:, 0:136]), "toepS")
            act.wait_ge(S["consts_in"], 16)
            run(ident_r[:, :], cc("ident")).then_inc(S["ident_ok"], 1)

            full(act, "toepS")
            for t in range(1, NT):
                L = 128 * (t + 1)
                for h in range(H):
                    n = (t - 1) * H + h
                    out = full(act, ("ix", t, h))
                    if n >= 2:
                        act.wait_ge(S["relu_added"], n - 1)
                    free(run(rows[:, n % 2, 0:L], out[:, 0:L], ACT.Relu, scale=HD ** -0.5), ("ix", t, h))
            act.wait_ge(S["relu_added"], (NT - 1) * H)
            kx_t = pages[0:64, 1, :, :].rearrange("p a b -> p (a b)")

            def kidx_keep(b):
                free(run(kx_t[:, 512 * (b % 2):512 * (b % 2) + 512], full(act, ("kxT", b))[0:64, :]), ("kxT", b))

            kidx_keep(0)
            for b in range(DB):
                if b >= 2:
                    act.wait_ge(S["relu_used"], b - 1)
                free(run(rows[0:64, b % 2, 0:PAST], full(act, ("ixS", b))[0:64, :], ACT.Relu, scale=HD ** -0.5), ("ixS", b))
                free(run(rows[0:64, b % 2, PAST:LS], full(act, ("ixSn", b))[0:64, 0:DS], ACT.Relu, scale=HD ** -0.5), ("ixSn", b))
                if b + 1 < DB:
                    kidx_keep(b + 1)

            def k_tail(i, out):
                free(run(k_s[:, 2 * i:2 * i + 2, :], out[:, 0:2 * TS].rearrange("p (c n) -> p c n", c=2)), ("kS", i))

            def q_tail(i, out):
                free(run(q_s[:, 2 * i:2 * i + 2, :], out[:, 0:2 * TS].rearrange("p (c n) -> p c n", c=2),
                         scale=HD ** -0.5), ("qS", i))

            def k_chunk(c, out):
                run(k_hi[:, c, :], out[:, :]).then_inc(S["proj_hi"], 1)

            def q_chunk(c, out):
                run(q_hi[:, c, :], out[:, :], scale=HD ** -0.5).then_inc(S["proj_hi"], 1)

            staged = [0]

            def stage_copy(out, r):
                n = staged[0]
                if n >= 2:
                    act.wait_ge(stage_out[n % 2], 16 * (n // 2))
                ins = run(stage[0:r, n % 2, :], out)
                staged[0] += 1
                return ins

            pair("k", 0, k_chunk, k_tail)
            free(run(hist_t, full(act, "hist")[:, 0:480].rearrange("p (g n) -> p g n", g=NG)), "hist")
            pair("k", 1, k_chunk, k_tail)
            def u_chunk(g, out):
                if g == 0:
                    act.wait_ge(S["u_zero"], 1)
                free(run(u_t[:, g, 16:16 + TP], out[:, :]), ("u", g))

            def u_tail(i, out):
                run(stage_s[:, 0:2, :], out[:, 0:2 * TS].rearrange("p (a n) -> p a n", a=2))
                free(run(u_t[:, 2 * i:2 * i + 2, 16 + TP:].rearrange("p a (b s) -> p a b s", b=DB)[:, :, :, SEG - DS:],
                         out[:, 0:2 * TS].rearrange("p (a b t) -> p a b t", a=2, b=DB)), ("uS", i))

            for i in range(2):
                pair("u", i, u_chunk, u_tail)
                for g in (2 * i, 2 * i + 1):
                    out = full(act, ("uo", g))
                    run(near[64:128, 0, 128 * g:128 * g + 128], out[64:128, 0:128])
                    free(run(near[0:TS, 0, 128 * g:128 * g + 128], out[0:TS, 128:256]), ("uo", g))
            pair("q", 0, q_chunk, q_tail)
            for t in range(NT + 1):
                out = full(act, ("kout", t))
                free(stage_copy(out[0:rows_of(t), :], rows_of(t)), ("kout", t))
            pair("q", 1, q_chunk, q_tail)

            for i in range(2):
                hi_until(AT[("v", i)] + 3)
            for t in range(NT):
                out = full(act, ("v", t))
                run(qiv_hi[:, t, :], out[:, :])
                stage_copy(out[:, :], 128).then_inc(S["v_staged"], 1)
            run(tmp_s[:, :], full(act, ("v", NT))[TS:2 * TS, :]).then_inc(S["v_low_rows"], 1)

            hi_until(AT[("poolw", 0)] + 2)
            for g in range(NG):
                act.wait_ge(S["pooled"], g + 1)
                src = u_t[:, g, :]
                if g >= 1:
                    full(act, ("pmS", g - 1))
                run(pt_hi[:, 0:TP], src[:, 16:16 + TP])
                run(pt_hi[:, TP:TP + TS].rearrange("p (b t) -> p b t", b=DB),
                    src[:, 16 + TP:].rearrange("p (b s) -> p b s", b=DB)[:, :, SEG - DS:]).then_inc(S["pool_hi"], 1)
                for key, dst in ((("pm", g), act_hi[:, g, :]), (("pmS", g), act_s[:, g, 0:TS])):
                    out = full(act, key)
                    n = dst.shape[1]
                    run(dst, out[:, 0:n], scale=rows_t[:, 16 + g:17 + g]).then_inc(S["mixed_hi"], 1)
            hi_until(AT[("poolw", 0)] + 3)

            for k in (staged[0], staged[0] + 1):
                act.wait_ge(stage_out[k % 2], 16 * (k // 2))
            for n in range(N_AT + 5):
                if n >= 5:
                    m = n - 5
                    t, h = m // H, m % H
                    out = full(act, ("pv", m))
                    r = slice(64 * (h % 2), 64 * (h % 2) + 64)
                    run(act_hi[r, 4 + h // 2, 128 * t:128 * t + 128], out[r, 0:128]).then_inc(S["o_hi"], 1)
                if n < N_AT:
                    L = 128 * (n // H + 1)
                    act.wait_ge(S["peaks"], n + 1)
                    run(probs[:, n % 3, 0:L], probs[:, n % 3, 0:L], ACT.Exp, bias=soft[:, n % 3, 1:2],
                        accum_out=soft[:, n % 3, 2:3]).then_inc(S["exps"], 1)
                if 2 <= n <= N_AT + 1:
                    m = n - 2
                    L = 128 * (m // H + 1)
                    out = full(act, ("pT", m))
                    if m >= 2:
                        full(act, ("pv", m - 2))
                    run(turned_probs(m)[0][:, 0:L], out[:, 0:L]).then_inc(S["pt_hi_ok"], 1)
                if 0 < n <= N_AT and n % 2 == 0:
                    modulation(FILL[n // 2 - 1])

            def keep_keys(b, c):
                out = full(act, ("KT", b, c))
                if b >= 2:
                    full(act, ("lgS", b // 2 - 1))
                free(run(k_t[:, b % 2, c, :], out[:, :]), ("KT", b, c))

            for b in range(2):
                keep_keys(b, 0), keep_keys(b, 2)
            for bp in range(4):
                if bp < 3:
                    keep_keys(2 * bp + 2, 0)
                act.wait_ge(S["peak_s"], bp + 1)
                run(rows[:, bp % 2, 0:LS], rows[:, bp % 2, 0:LS], ACT.Exp, bias=soft[:, bp % 2, 1:2],
                    accum_out=soft[:, bp % 2, 2:3]).then_inc(S["exp_s"], 1)
                if bp < 3:
                    keep_keys(2 * bp + 2, 2), keep_keys(2 * bp + 3, 0), keep_keys(2 * bp + 3, 2)
                out = full(act, ("pTS", bp))
                if bp >= 1:
                    full(act, ("pvS", bp - 1))
                free(run(p_t[:, 0:4, :], out[:, :].rearrange("p (g n) -> p g n", g=NPG)), ("pTS", bp))
                free(run(p_t[0:64, 4, :], full(act, ("pTSn", bp))[0:64, 0:128]), ("pTSn", bp))
                out = full(act, ("pvS", bp))
                for hh in range(2):
                    r = slice(64 * hh, 64 * hh + 64)
                    run(act_s[r, 4:8, 16 * bp:16 * bp + 16].rearrange("p c (b t) -> p b c t", b=2),
                        out[r, 0:128].rearrange("p (b c x t) -> p x b c t", b=2, c=4, x=2)[:, hh]).then_inc(S["os_hi"], 1)

            def keep_tokens(kind, f, nh, copy, low, last_piece):
                for t in range(NT):
                    if copy:
                        free(run(out_t[:, t, 512 * nh:512 * nh + 512], full(act, (kind, *f, nh, t))[:, :]), (kind, *f, nh, t))
                out = full(act, (kind, *f, nh, NT))
                hi_until(last_piece + 3)
                if low >= 1:
                    prev = ("wo", 0, NT) if low == 1 else ("wo", 1, NT) if low == 2 else ("w2", (low - 3) // 2, (low - 3) % 2, NT)
                    evacuated(act, prev)
                run(half_s[:, :], out[TS:2 * TS, :]).then_inc(S["low_rows"], 1)

            for nh in range(2):
                hi_until(AT[("wo", 2 * nh)] + 3)
                keep_tokens("wo", (), nh, True, nh, AT[("wo", 2 * nh + 1)])
            evacuated(act, ("wo", 1, NT))
            squares(out_t)
            root(1)
            act.wait_ge(S["residual"], NT + 1)
            squares(x_res)
            root(2)
            turned_hidden(1)

            for f in range(QF):
                for i in range(4):
                    p = 4 * f + i
                    for n in (2 * p, 2 * p + 1):
                        out = full(act, ("w1", n))
                        if n >= 2:
                            act.wait_ge(S["w1_done"], n - 1)
                        free(run(stage[:, n % 2, :], out[:, :], ACT.Relu), ("w1", n))
                    for n in (2 * p, 2 * p + 1):
                        act.wait_ge(S["w1_squared"], n + 1)
                        run(hid_hi[:, n % 8, :], stage[:, n % 2, :]).then_inc(S["w1_hi"], 1)
                    hi_until(AT[("w1", p)] + 3)
                    out = full(act, ("w1S", p))
                    if p >= 2:
                        act.wait_ge(S["w1s_done"], p - 1)
                    st = stage_s[:, 2 * (p % 2):2 * (p % 2) + 2, :]
                    free(run(st, out[:, 0:2 * TS].rearrange("p (a n) -> p a n", a=2), ACT.Relu), ("w1S", p))
                    act.wait_ge(S["w1s_squared"], p + 1)
                    run(hid_s[:, 2 * i:2 * i + 2, 0:TS], st).then_inc(S["w1s_hi"], 1)
                for nh in range(2):
                    hi_until(AT[("w2", 4 * f + 2 * nh)] + 3)
                    keep_tokens("w2", (f,), nh, f == 0, 2 + 2 * f + nh, AT[("w2", 4 * f + 2 * nh + 1)])
            act.wait_ge(S["w1_done"], 2 * DFF // 256)
            for t in range(NT + 1):
                evacuated(act, ("w2", QF - 1, 1, t))
            squares(out_t)
            root(3)

        @block.vector
        def _(dve):
            link = Chain(dve, dve_chain)
            split = [0]

            def lo_until(n):
                while split[0] < min(n, len(PIECES)):
                    m = split[0]
                    size = piece_size(PIECES[m][0])
                    dve.wait_ge(hi_ready, m + 1)
                    nc.vector.tensor_tensor(w_lo[:, m % NSPLIT, 0:size], raw[:, m % NRAW, 0:size],
                                            w_hi[:, m % NSPLIT, 0:size].bitcast(F32), ALU.subtract).then_inc(lo_ready, 1)
                    split[0] += 1

            def minus(out, x, hi):
                return nc.vector.tensor_tensor(out, x, hi.bitcast(F32), ALU.subtract)

            def scaled_minus(out, x, scale, hi):
                return nc.vector.scalar_tensor_tensor(out, x, scale, hi.bitcast(F32), ALU.mult, ALU.subtract)

            nc.vector.memset(c_split[:].bitcast(F32), 0.0).then_inc(S["pad_zero2"], 1)
            nc.vector.memset(ss[:], 1.0).then_inc(S["pad_zero2"], 1)
            nc.vector.memset(zero1, 0.0)
            out = full(dve, "cT")
            dve.wait_ge(S["c_hi"], 1)
            dve.wait_ge(S["pad_zero2"], 1)
            ins = minus(c_split[:, :, 32:41], out[:, 0:72].rearrange("p (c m) -> p c m", m=9), c_split[:, :, 0:9])
            free(ins, "cT")
            lo_until(2)

            def mean(k):
                dve.wait_ge(S["squares"], (NT + 1) * (k + 1))
                nc.vector.tensor_scalar(ss[:, 0:NT + 1], ss[:, 0:NT + 1], 1.0 / D, EPS, ALU.mult, ALU.add)\
                    .then_inc(S["mean_ok"], 1)
                dve.wait_ge(S["root_ok"], k + 1)
                link(nc.vector.reciprocal(rstd[:, 0:NT + 1], rstd[:, 0:NT + 1]))

            def normalise(dst, src):
                for t in range(NT + 1):
                    r = rows_of(t)
                    nc.vector.tensor_scalar(dst[0:r, t, :], src[0:r, t, :], rstd[0:r, t:t + 1], None, ALU.mult)\
                        .then_inc(S["normed"], 1)

            mean(0)
            normalise(x_nrm, x_in)
            for i in range(8):
                lo_until(i + 3)

            def turned_hidden(k):
                out = full(dve, ("modT", k))
                m = mod_t[:, 16 * k:16 * k + 16, :]
                evacuated(dve, "rowsT")
                free(nc.vector.tensor_copy(m, out[:, 0:144].rearrange("p (j m) -> p j m", m=9)), ("modT", k))
                evacuated(dve, ("modT", k))
                gain = rows_t[:, 8 * k:8 * k + 8].unsqueeze(2).to_broadcast([128, 8, 9])
                nc.vector.scalar_tensor_tensor(m[:, 8:16, :], m[:, 8:16, :], 1.0, gain, ALU.add, ALU.mult)\
                    .then_inc(S["mod_ok"], 2)
                dve.wait_ge(S["mod_ok"], 2 * (k + 1))

            def split_hidden(k):
                for kc in range(KC):
                    dve.wait_ge(S["h_hi"], k * KC + kc + 1)
                    minus(act_lo[:, kc, :], stage[:, kc % 2, :], act_hi[:, kc, :]).then_inc(S["h_low"], 1)
                out = full(dve, ("hTS", k))
                m = mod_t[:, 16 * k:16 * k + 16, 1:9]
                dims = [128, KC, DB, DS]
                shape = dict(b=DB)
                st = stage_s[:, :, :].rearrange("p c (b t) -> p c b t", b=DB)
                free(nc.vector.tensor_tensor(st, out[:, :].rearrange("p (c b t) -> p c b t", c=KC, b=DB),
                                             m[:, 8:16, :].unsqueeze(3).to_broadcast(dims), ALU.mult), ("hTS", k))
                evacuated(dve, ("hTS", k))
                nc.vector.tensor_tensor(st, st, m[:, 0:8, :].unsqueeze(3).to_broadcast(dims), ALU.add)\
                    .then_inc(S["hs_staged"], 1)
                dve.wait_ge(S["hs_staged"], k + 1)
                dve.wait_ge(S["hs_hi"], k + 1)
                minus(act_s[:, :, TS:2 * TS], stage_s[:, :, :], act_s[:, :, 0:TS]).then_inc(S["hs_lo"], 1)

            turned_hidden(0)
            split_hidden(0)

            for i in range(2):
                for c in (2 * i, 2 * i + 1):
                    dve.wait_ge(S["proj_hi"], c + 1)
                    free(minus(qiv_lo[:, c, :], full(dve, ("qi", c))[:, :], qiv_hi[:, c, :]), ("qi", c))
                lo_until(AT[("qi", i)] + 3)
            dve.wait_ge(S["proj_hi"], 5)
            free(minus(ki_lo[:, :], full(dve, "ki")[:, :], ki_hi[:, :]), "ki")
            lo_until(AT[("kiwi", 0)] + 3)
            dve.wait_ge(S["wi_low"], 2)
            out = full(dve, "kiwi")
            free(nc.vector.tensor_tensor(kiwi[0:TS, NT, :], out[0:TS, 72 * NT:72 * NT + 72],
                                         stage_s[0:TS, 0:2, :].rearrange("p a b -> p (a b)")[:, 0:72], ALU.add), "kiwi")
            evacuated(dve, "kiwi")
            nc.vector.tensor_scalar(wi[:, 0:NT, :], kiwi[:, 0:NT, 64:72], H ** -0.5, None, ALU.mult)
            nc.vector.tensor_scalar(wi[0:TS, NT, :], kiwi[0:TS, NT, 64:72], H ** -0.5, None, ALU.mult).then_inc(S["wi_ok"], 1)
            dve.wait_ge(S["wi_ok"], 1)
            out = full(dve, "wiR")
            dve.wait_ge(S["pad_zero"], 1)
            w0 = wi_b[:, :, 0:DS]
            diag = bass.AP(tensor=w0.tensor, offset=w0.offset, ap=[list(w0.ap[0]), [64 + DS, DB], [1, DS]])
            free(nc.vector.tensor_tensor(diag, out[0:64, 0:TS].rearrange("p (b t) -> p b t", b=DB),
                                         cc("step", 64).rearrange("p (b t) -> p b t", b=DB), ALU.mult), "wiR")

            for t in range(1, NT):
                L = 128 * (t + 1)
                for h in range(H):
                    n = (t - 1) * H + h
                    evacuated(dve, ("ix", t, h))
                    r = rows[:, n % 2, 0:L]
                    if h == 0:
                        ins = nc.vector.tensor_scalar(score[t][:, 0:L], r, wi[:, t, h:h + 1], 0.0, ALU.mult, ALU.add)
                    else:
                        ins = nc.vector.scalar_tensor_tensor(score[t][:, 0:L], r, wi[:, t, h:h + 1], score[t][:, 0:L],
                                                             ALU.mult, ALU.add)
                    ins.then_inc(S["relu_added"], 1)
                    dve.wait_ge(S["relu_added"], n + 1)
                link(nc.vector.tensor_tensor(score[t][:, L - 128:L], score[t][:, L - 128:L], cc("causal"), ALU.add))
            free(nc.vector.tensor_copy(score_s[:, 0:PAST], full(dve, "scS")[0:TS, :]), "scS")
            free(nc.vector.tensor_tensor(score_s[:, PAST:LS], full(dve, "scSn")[0:TS, 0:DS], cc("newmask", TS), ALU.add), "scSn")
            evacuated(dve, "scS")
            evacuated(dve, "scSn")

            def choose(buf, n_sel):
                r = buf.shape[0]
                for left in range(n_sel, 0, -8):
                    link(nc.vector.max(top8[0:r, :], buf))
                    if left < 8:
                        link(nc.vector.memset(top8[0:r, left:8], TAKEN))
                    link(nc.vector.match_replace(buf, top8[0:r, :], buf, TAKEN))
                    yield
                nc.vector.tensor_scalar(buf, buf, TAKEN, NEG, ALU.not_equal, ALU.mult).then_inc(S["chosen"], 1)
                yield

            def all_choices():
                for t in range(1, NT):
                    yield from choose(score[t][:, :], SEL_P)
                yield from choose(score_s[:, :], SEL_S)

            rounds = all_choices()

            def some_rounds(n):
                for _ in range(n):
                    next(rounds, None)

            def k_pair(i):
                for c in (2 * i, 2 * i + 1):
                    dve.wait_ge(S["proj_hi"], 6 + c)
                    free(minus(k_lo[:, c, :], full(dve, ("k", c))[:, :], k_hi[:, c, :]), ("k", c))
                    some_rounds(3)
                lo_until(AT[("k", i)] + 3)

            def q_pair(i):
                for c in (2 * i, 2 * i + 1):
                    dve.wait_ge(S["proj_hi"], 10 + c)
                    free(scaled_minus(q_lo[:, c, :], full(dve, ("q", c))[:, :], HD ** -0.5, q_hi[:, c, :]), ("q", c))
                    some_rounds(3)
                lo_until(AT[("q", i)] + 3)

            for i in range(2):
                k_pair(i)
            for i in range(2):
                lo_until(AT[("u", i)] + 3)
                some_rounds(9)
            for i in range(2):
                q_pair(i)
            lo_until(AT[("v", 0)] + 3)
            some_rounds(7)
            lo_until(AT[("v", 1)] + 3)
            for t in range(NT):
                dve.wait_ge(S["v_staged"], t + 1)
                free(minus(qiv_lo[:, t, :], full(dve, ("v", t))[:, :], qiv_hi[:, t, :]), ("v", t))
            dve.wait_ge(S["v_low_rows"], 1)
            free(nc.vector.tensor_tensor(v_s[:, :], full(dve, ("v", NT))[0:TS, :], tmp_s[:, :], ALU.add), ("v", NT))
            for g in range(NG):
                dve.wait_ge(S["pool_hi"], g + 1)
                src = u_t[:, g, :]
                minus(pt_lo[:, 0:TP], src[:, 16:16 + TP], pt_hi[:, 0:TP])
                minus(pt_lo[:, TP:TP + TS].rearrange("p (b t) -> p b t", b=DB),
                      src[:, 16 + TP:].rearrange("p (b s) -> p b s", b=DB)[:, :, SEG - DS:],
                      pt_hi[:, TP:TP + TS].rearrange("p (b t) -> p b t", b=DB)).then_inc(S["pool_lo"], 1)
                sc = rows_t[:, 16 + g:17 + g]
                dve.wait_ge(S["mixed_hi"], 2 * g + 1)
                free(scaled_minus(act_lo[:, g, :], full(dve, ("pm", g))[:, :], sc, act_hi[:, g, :]), ("pm", g))
                dve.wait_ge(S["mixed_hi"], 2 * g + 2)
                free(scaled_minus(act_s[:, g, TS:2 * TS], full(dve, ("pmS", g))[:, 0:TS], sc, act_s[:, g, 0:TS]), ("pmS", g))
            lo_until(AT[("poolw", 0)] + 3)
            for n in range(N_AT + 5):
                if n == 18:
                    turned_hidden(1)
                if n < N_AT:
                    L = 128 * (n // H + 1)
                    out = full(dve, ("lg", n))
                    dve.wait_ge(S["near_ok"], n + 1)
                    if n >= 3:
                        full(dve, ("pT", n - 3))
                    free(nc.vector.tensor_tensor_reduce(probs[:, n % 3, 0:L], out[:, 0:L], near[:, n % 2, 0:L], 1.0, TAKEN,
                                                        ALU.add, ALU.max, soft[:, n % 3, 0:1]), ("lg", n))
                    evacuated(dve, ("lg", n))
                    nc.vector.tensor_scalar(soft[:, n % 3, 1:2], soft[:, n % 3, 0:1], -1.0, None, ALU.mult)\
                        .then_inc(S["peaks"], 1)
                if 3 <= n <= N_AT + 2:
                    m = n - 3
                    L = 128 * (m // H + 1)
                    dve.wait_ge(S["pt_hi_ok"], m + 1)
                    ph, pl = turned_probs(m)
                    free(minus(pl[:, 0:L], full(dve, ("pT", m))[:, 0:L], ph[:, 0:L]), ("pT", m))
                if 1 <= n <= N_AT:
                    m = n - 1
                    L = 128 * (m // H + 1)
                    dve.wait_ge(S["exps"], m + 1)
                    link(nc.vector.reciprocal(soft[:, m % 3, 3:4], soft[:, m % 3, 2:3]))
                    nc.vector.tensor_scalar(probs[:, m % 3, 0:L], probs[:, m % 3, 0:L], soft[:, m % 3, 3:4], None,
                                            ALU.mult).then_inc(S["probs_ok"], 1)
                if n >= 5:
                    m = n - 5
                    t, h = m // H, m % H
                    r = slice(64 * (h % 2), 64 * (h % 2) + 64)
                    tok = slice(128 * t, 128 * t + 128)
                    dve.wait_ge(S["o_hi"], m + 1)
                    free(minus(act_lo[r, 4 + h // 2, tok], full(dve, ("pv", m))[r, 0:128], act_hi[r, 4 + h // 2, tok]), ("pv", m))
                if 3 <= n <= N_AT + 1 and n % 2 == 1:
                    lo_until(AT[("ada", FILL[n // 2 - 1])] + 3)
                elif n < N_AT:
                    some_rounds(2)
            evacuated(dve, "toepS")
            def keep_keys(b):
                for c in (1, 3):
                    out = full(dve, ("KT", b, c))
                    if b >= 2:
                        full(dve, ("lgS", b // 2 - 1))
                    free(nc.vector.tensor_copy(k_t[:, b % 2, c, :], out[:, :]), ("KT", b, c))

            keep_keys(0)
            keep_keys(1)
            for bp in range(4):
                out = full(dve, ("lgS", bp))
                s = soft[:, bp % 2, :]
                if bp >= 2:
                    full(dve, ("pTSn", bp - 2))
                far = LS - 136
                link(nc.vector.tensor_tensor_reduce(rows[:, bp % 2, 0:far], out[:, 0:far], zero1[:, :].to_broadcast([128, far]),
                                                    1.0, TAKEN, ALU.add, ALU.max, s[:, 2:3]))
                free(nc.vector.tensor_tensor_reduce(rows[:, bp % 2, far:PAST], out[:, far:PAST], toep_s[:, 0:PAST - far],
                                                    1.0, s[:, 2:3], ALU.add, ALU.max, s[:, 3:4]), ("lgS", bp))
                evacuated(dve, ("lgS", bp))
                free(nc.vector.tensor_tensor_reduce(rows[:, bp % 2, PAST:LS], full(dve, ("lgSn", bp))[:, 0:DS],
                                                    toep_s[:, PAST - far:136], 1.0, s[:, 3:4], ALU.add, ALU.max, s[:, 0:1]), ("lgSn", bp))
                evacuated(dve, ("lgSn", bp))
                nc.vector.tensor_scalar(s[:, 1:2], s[:, 0:1], -1.0, None, ALU.mult).then_inc(S["peak_s"], 1)
                if bp < 3:
                    keep_keys(2 * bp + 2)
                dve.wait_ge(S["exp_s"], bp + 1)
                link(nc.vector.reciprocal(s[:, 3:4], s[:, 2:3]))
                link(nc.vector.tensor_scalar(rows[:, bp % 2, 0:LS], rows[:, bp % 2, 0:LS], s[:, 3:4], None, ALU.mult))
                if bp >= 1:
                    full(dve, ("pTSn", bp - 1))
                nc.vector.tensor_tensor(p_new[:, :].rearrange("p (b t) -> p b t", b=DB),
                                        rows[:, bp % 2, PAST:LS].unsqueeze(1).to_broadcast([128, DB, DS]),
                                        cc("own")[:, DB * bp:DB * bp + DB].unsqueeze(2).to_broadcast([128, DB, DS]),
                                        ALU.mult).then_inc(S["prob_new"], 1)
                if bp < 3:
                    keep_keys(2 * bp + 3)
                out = full(dve, ("pvS", bp))
                for hh in range(2):
                    r = slice(64 * hh, 64 * hh + 64)
                    dve.wait_ge(S["os_hi"], 2 * bp + 2)
                    ins = minus(act_s[r, 4:8, TS + 16 * bp:TS + 16 * bp + 16].rearrange("p c (b t) -> p b c t", b=2),
                                out[r, 0:128].rearrange("p (b c x t) -> p x b c t", b=2, c=4, x=2)[:, hh],
                                act_s[r, 4:8, 16 * bp:16 * bp + 16].rearrange("p c (b t) -> p b c t", b=2))
                free(ins, ("pvS", bp))

            def gates(k):
                dve.wait_ge(S["gain_in"], 16 * (k + 1))
                for j in range(2):
                    s = slice(512 * j, 512 * j + 512)
                    free(nc.vector.tensor_tensor(gate_p[:, s], full(dve, ("gP", k, j))[:, :], ln_post[:, s], ALU.mult), ("gP", k, j))
                    free(nc.vector.tensor_tensor(gate_s[:, s], full(dve, ("gS", k, j))[0:TS, :], ln_post[0:TS, s], ALU.mult), ("gS", k, j))
                evacuated(dve, ("gP", k, 1))
                evacuated(dve, ("gS", k, 1))

            gates(0)
            for nh in range(2):
                s = slice(512 * nh, 512 * nh + 512)
                lo_until(AT[("wo", 2 * nh)] + 3)
                lo_until(AT[("wo", 2 * nh + 1)] + 3)
                dve.wait_ge(S["low_rows"], nh + 1)
                free(nc.vector.tensor_tensor(out_t[0:TS, NT, s], full(dve, ("wo", nh, NT))[0:TS, :], half_s[:, :], ALU.add),
                     ("wo", nh, NT))
            evacuated(dve, ("wo", 1, NT))

            def gated(signal):
                for t in range(NT + 1):
                    r = rows_of(t)
                    gate = gate_p if t < NT else gate_s
                    link(nc.vector.scalar_tensor_tensor(out_t[0:r, t, :], out_t[0:r, t, :], rstd[0:r, t:t + 1],
                                                        gate[0:r, :], ALU.mult, ALU.mult))
                    nc.vector.tensor_tensor(x_res[0:r, t, :], x_res[0:r, t, :], out_t[0:r, t, :], ALU.add)\
                        .then_inc(S[signal], 1)

            mean(1)
            dve.wait_ge(S["x_again"], 32)
            gated("residual")
            dve.wait_ge(S["residual"], NT + 1)
            mean(2)
            normalise(out_t, x_res)
            split_hidden(1)
            gates(1)

            for f in range(QF):
                for i in range(4):
                    p = 4 * f + i
                    for n in (2 * p, 2 * p + 1):
                        evacuated(dve, ("w1", n))
                        nc.vector.tensor_tensor(stage[:, n % 2, :], stage[:, n % 2, :], stage[:, n % 2, :], ALU.mult)\
                            .then_inc(S["w1_squared"], 1)
                        dve.wait_ge(S["w1_squared"], n + 1)
                    for n in (2 * p, 2 * p + 1):
                        dve.wait_ge(S["w1_hi"], n + 1)
                        minus(hid_lo[:, n % 8, :], stage[:, n % 2, :], hid_hi[:, n % 8, :]).then_inc(S["w1_done"], 1)
                    lo_until(AT[("w1", p)] + 3)
                    evacuated(dve, ("w1S", p))
                    st = stage_s[:, 2 * (p % 2):2 * (p % 2) + 2, :]
                    nc.vector.tensor_tensor(st, st, st, ALU.mult).then_inc(S["w1s_squared"], 1)
                    dve.wait_ge(S["w1s_squared"], p + 1)
                    dve.wait_ge(S["w1s_hi"], p + 1)
                    minus(hid_s[:, 2 * i:2 * i + 2, TS:2 * TS], st, hid_s[:, 2 * i:2 * i + 2, 0:TS]).then_inc(S["w1s_done"], 1)
                for nh in range(2):
                    s = slice(512 * nh, 512 * nh + 512)
                    lo_until(AT[("w2", 4 * f + 2 * nh)] + 3)
                    if f:
                        for t in range(NT):
                            free(nc.vector.tensor_tensor(out_t[:, t, s], full(dve, ("w2", f, nh, t))[:, :], out_t[:, t, s],
                                                         ALU.add), ("w2", f, nh, t))
                    lo_until(AT[("w2", 4 * f + 2 * nh + 1)] + 3)
                    dve.wait_ge(S["low_rows"], 3 + 2 * f + nh)
                    y = out_t[0:TS, NT, s]
                    if f:
                        link(nc.vector.tensor_tensor(y, y, half_s[:, :], ALU.add))
                        free(nc.vector.tensor_tensor(y, full(dve, ("w2", f, nh, NT))[0:TS, :], y, ALU.add), ("w2", f, nh, NT))
                    else:
                        free(nc.vector.tensor_tensor(y, full(dve, ("w2", f, nh, NT))[0:TS, :], half_s[:, :], ALU.add),
                             ("w2", f, nh, NT))
            mean(3)
            gated("y_ok")


_OUTS = [("y_p", (1, TP, D)), ("y_s", (DB, DS, D)),
         ("k_p", (1, 1, TP, H, HD)), ("v_p", (1, 1, TP, H, HD)), ("kidx_p", (1, 1, TP, HD)), ("pool_p", (1, 1, HIST, CP_)),
         ("k_s", (1, DB, DS, H, HD)), ("v_s", (1, DB, DS, H, HD)), ("kidx_s", (1, DB, DS, HD)), ("pool_s", (1, DB, HIST, CP_))]


def kernel(**inputs):
    import concourse.bacc as bacc
    from concourse.bass_utils import run_bass_kernel_spmd

    nc = bacc.Bacc("TRN2", target_bir_lowering=False, num_devices=1)
    consts, spans = constants()
    given = {name: np.ascontiguousarray(value) for name, value in inputs.items()}
    given["consts"] = consts
    arrays, a, o = {}, {}, {}
    for name, value in given.items():
        arrays[f"in_{name}"] = value
        a[name] = nc.dram_tensor(f"in_{name}", value.shape, mybir.dt.from_np(value.dtype), kind="ExternalInput").ap()
    for name, shape in _OUTS:
        o[name] = nc.dram_tensor(f"out_{name}", shape, F32, kind="ExternalOutput").ap()
    build_program(nc, a, o, spans)
    r = run_bass_kernel_spmd(nc, [arrays], core_ids=[0])
    return tuple(r.results[0][f"out_{name}"] for name, _ in _OUTS)
```

```python
from contextlib import ExitStack

import numpy as np
import concourse.bass as bass
from concourse import mybir

F32 = mybir.dt.float32
F32R = mybir.dt.float32r
I32 = mybir.dt.int32
ALU = mybir.AluOpType
ACT = mybir.ActivationFunctionType
AX_X = mybir.AxisListType.X

D = 1024
KC = D // 128
TP = 512
NT = TP // 128
DB, DS = 8, 8
TS = DB * DS
PAST, PAGE = 512, 128
NPG = PAST // PAGE
H, HD = 8, 64
CP_ = 512
NG = 4
WINDOWS = (2, 4, 8, 16)
HIST = 15
NB, MAXD = 32, 128
DFF = 4096
D_IN = 4 * 512 + 512 + 64 + 8
OFF_Q, OFF_K, OFF_V, OFF_QI, OFF_KI, OFF_WI = 512, 1024, 1536, 2048, 2560, 2624
SEL_P = min(256, TP // 4)
SEL_S = min(256, (PAST + DS) // 4)
LS = PAST + DS
EPS = 1e-6
NEG = -(2.0 ** 100)
TAKEN = -3.0e38
NRAW, NSPLIT = 2, 2
QF = 4
SEG = 1 + HIST + DS
UW = 16 + TP + DB * SEG


def t5_bucket(n):
    n = np.maximum(n, 0)
    exact = NB // 2
    large = exact + (np.log(np.maximum(n, 1).astype(np.float32) / exact)
                     / np.log(MAXD / exact) * (NB - exact)).astype(np.int32)
    return np.where(n < exact, n, np.minimum(large, NB - 1))


def constants():
    parts = {}
    r = np.arange(128)
    parts["ident"] = np.eye(128)
    parts["flip"] = np.eye(128)[::-1]
    parts["causal"] = np.where(r[None, :] > r[:, None], NEG, 0.0)
    onehot = np.zeros((128, 384))
    x = np.arange(384)
    onehot[t5_bucket(255 - x), x] += 1.0
    onehot[NB - 1, :] -= 1.0
    parts["bucket"] = onehot
    unflip = np.zeros((128, 128))
    for b2 in range(2):
        for h in range(H):
            for t in range(DS):
                unflip[h * DS + (DS - 1 - t), b2 * 64 + h * DS + t] = 1.0
    parts["unflip"] = unflip
    own = np.zeros((128, 4, DB))
    for bp in range(4):
        for b2 in range(2):
            own[64 * b2:64 * b2 + 64, bp, 2 * bp + b2] = 1.0
    parts["own"] = own.reshape(128, 4 * DB)
    sel_t = np.zeros((128, 9)); sel_p = np.zeros((128, 128)); sel_s = np.zeros((128, 64))
    for m in range(9):
        sel_t[m, m] = sel_t[32 + m, m] = 1.0
    sel_t[41, :] = 1.0
    sel_p[[0, 32, 41], :] = 1.0
    for b in range(DB):
        sel_s[[1 + b, 33 + b], b * DS:(b + 1) * DS] = 1.0
    sel_s[41, :] = 1.0
    parts["sel_t"], parts["sel_p"], parts["sel_s"] = sel_t, sel_p, sel_s
    parts["fold"] = np.concatenate([np.eye(TS), np.eye(TS)])
    heads = np.zeros((128, 64)); step = np.zeros((128, 64))
    for h in range(H):
        heads[h, h * DS:(h + 1) * DS] = 1.0
        for t in range(DS):
            step[h * DS + t, t::DS] = 1.0
    parts["heads"], parts["step"] = heads, step
    inv = np.zeros((128, 4, 16))
    for g, w in enumerate(WINDOWS):
        inv[:, g, :] = 1.0 / np.minimum(np.arange(16) + 1, w)
    parts["invcnt"] = inv.reshape(128, 64)
    new = np.zeros((128, 8))
    for b in range(DB):
        for t in range(DS):
            new[b * DS + t, t + 1:] = NEG
    parts["newmask"] = new
    at, spans = 0, {}
    for k, v in parts.items():
        spans[k] = (at, at + v.shape[1])
        at += v.shape[1]
    return np.concatenate(list(parts.values()), axis=1).astype(np.float32), spans


FILL = [*range(12, 20), *range(8, 12), *range(20, 24)]


def plan_pieces():
    p = [("ada", i) for i in range(8)]
    p += [("qi", 0), ("qi", 1), ("kiwi", 0), ("k", 0), ("k", 1), ("u", 0), ("u", 1)]
    p += [("q", 0), ("q", 1), ("v", 0), ("v", 1), ("poolw", 0)]
    p += [("ada", i) for i in FILL]
    p += [("wo", i) for i in range(4)]
    for f in range(QF):
        p += [("w1", 4 * f + i) for i in range(4)] + [("w2", 4 * f + i) for i in range(4)]
    return p


PIECES = plan_pieces()
AT = {key: n for n, key in enumerate(PIECES)}
COL0 = {"qi": OFF_QI, "k": OFF_K, "q": OFF_Q, "u": 0}
ADA_ROW = {i: (i if i < 8 else i - 12 if 12 <= i < 20 else i - 8 if i < 12 else i - 16) for i in range(24)}


def piece_shape(kind):
    if kind in ("ada", "v", "wo", "w2"):
        return 4, 512
    return {"kiwi": (KC, 136), "poolw": (NG, 128)}.get(kind, (KC, 256))


def plan_norms():
    order = [(0, t) for t in range(NT + 1)]
    for j in range(NT + 2):
        order += [(1, j)] * (j <= NT) + [(2, j - 1)] * (j >= 1)
    order += [(3, t) for t in range(NT + 1)]
    return {key: n for n, key in enumerate(order)}


NORM = plan_norms()


def plan_banks():
    use, count = {}, [0] * 8

    def take(key, bank):
        count[bank] += 1
        use[key] = (bank, count[bank])

    take("cT", 3)
    take("rowsT", 4)
    for i in range(1, 8, 2):
        take(("ada", i), i // 2 % 2)
    take(("modT", 0), 3)
    for kc in range(KC):
        take(("hT", 0, kc), kc % 2)
    take(("hTS", 0), 2)
    for i in range(2):
        take(("qi", 2 * i), 0), take(("qi", 2 * i + 1), 1), take(("qiR", i), 2), take(("qiS", i), 2)
    take("ki", 0), take("kw", 1), take("kiR", 2), take("kiS", 3), take("kiwi", 4)
    take("wiT", 4), take("wiR", 5)
    take("biasrow", 6)
    for j in range(4):
        take(("toep", j), 6 + j % 2)
    take("toepS", 6)
    for t in range(1, NT):
        for h in range(H):
            take(("ix", t, h), 3 + h % 2)
    for b in range(DB):
        take(("kxT", b), 5)
        take(("ixS", b), 6), take(("ixSn", b), 7)
        if b == 0:
            take("scS", 3), take("scSn", 4)
    take("hist", 5)
    for kind in ("k", "u", "q"):
        for i in range(2):
            take((kind, 2 * i), 0), take((kind, 2 * i + 1), 1), take((kind + "R", i), 2), take((kind + "S", i), 2)
            if kind == "u":
                for g in (2 * i, 2 * i + 1):
                    take(("uo", g), 3 + g % 2)
        if kind == "k":
            for t in range(NT + 1):
                take(("kout", t), 5 + t % 2)
    for t in range(NT + 1):
        take(("v", t), 3 + t)
    for g in range(NG):
        take(("pm", g), g % 2), take(("pmS", g), 2)
    for n in range(NT * H + 4):
        if n < NT * H:
            take(("lg", n), 3 + n % 2)
        if n >= 4:
            take(("pv", n - 4), 6 + n % 2)
        if 2 <= n <= NT * H + 1:
            take(("pT", n - 2), 5 if n % 2 else 2)
        if n < NT * H and n % 4 == 3:
            take(("ada", FILL[n // 2]), n // 4 % 2)
        if n == 17:
            take(("modT", 1), 2)
    for b in range(DB):
        for c in range(4):
            take(("KT", b, c), c % 2)
    for bp in range(4):
        take(("lgS", bp), 3), take(("lgSn", bp), 4)
        take(("pTS", bp), 5), take(("pTSn", bp), 6)
        take(("pvS", bp), 7)
    for j in range(2):
        take(("gP", 0, j), j), take(("gS", 0, j), 2)
    for nh in range(2):
        for t in range(NT + 1):
            take(("wo", nh, t), 3 + t)
    for kc in range(KC):
        take(("hT", 1, kc), kc % 2)
    take(("hTS", 1), 2)
    for j in range(2):
        take(("gP", 1, j), 3 + 2 * j), take(("gS", 1, j), 4 + 2 * j)
    for f in range(QF):
        for i in range(4):
            take(("w1", 8 * f + 2 * i), 0), take(("w1", 8 * f + 2 * i + 1), 1)
            take(("w1R", 4 * f + i), 2), take(("w1S", 4 * f + i), 2)
        for nh in range(2):
            for t in range(NT + 1):
                take(("w2", f, nh, t), 3 + t)
    return use


USE = plan_banks()


def last_use(kind, i):
    if kind in ("qi", "k", "q", "u", "w1"):
        return (kind + "R", i)
    return {"ada": ("ada", i), "kiwi": "kiR", "v": ("v", NT), "poolw": ("pmS", NG - 1)}.get(kind) or {
        "wo": ("wo", i // 2, NT), "w2": ("w2", i // 4, i % 4 // 2, NT)}[kind]


def build_program(nc, a, o, spans):
    ctx = ExitStack()
    with ctx:
        def sem(name):
            return ctx.enter_context(nc.semaphore(name))

        psum = [ctx.enter_context(nc.psum_tensor(f"bank{i}", [128, 512], F32)) for i in range(8)]

        def sb(name, shape, dt=F32, stack=ctx):
            return stack.enter_context(nc.sbuf_tensor(name, shape, dt))

        cst = sb("cst", [128, spans["newmask"][1]])
        raw = sb("raw", [128, NRAW, 2048])
        w_split = sb("w_split", [128, NSPLIT, 4096], F32R)
        act_hi = sb("act_hi", [128, KC, TP], F32R)
        act_lo = sb("act_lo", [128, KC, TP], F32R)
        act_s = sb("act_s", [128, KC, 2 * TS], F32R)
        mod_rows = sb("mod_rows", [42, 2048])
        mod_t = sb("mod_t", [128, 4 * KC, 9])
        over = ExitStack()
        pu_hi = sb("pu_hi", [128, TP], F32R, over)
        pu_lo = sb("pu_lo", [128, TP], F32R, over)
        over.close()
        stage = sb("stage", [128, 2, TP])
        stage_s = sb("stage_s", [128, KC, TS])
        c_split = sb("c_split", [128, KC, 72], F32R)
        rows_t = sb("rows_t", [128, 20])
        ss = sb("ss", [128, 4 * (NT + 1)])
        rstd = sb("rstd", [128, 4 * (NT + 1)])

        def cc(name, rows=128):
            x, y = spans[name]
            return cst[0:rows, x:y]

        dram_bias = nc.dram_tensor("bias_rows", (H, 384), F32, kind="Internal").ap()

        mix = ExitStack()
        head = ExitStack()
        x_in = sb("x_in", [128, NT + 1, D], stack=head)
        x_nrm = sb("x_nrm", [128, NT + 1, D], stack=head)
        c_in = sb("c_in", [9, D], stack=head)
        rows_in = sb("rows_in", [20, 128], stack=head)
        head.close()
        q_hi = sb("q_hi", [128, 4, TP], F32R, mix)
        q_lo = sb("q_lo", [128, 4, TP], F32R, mix)
        k_hi = sb("k_hi", [128, 4, TP], F32R, mix)
        k_lo = sb("k_lo", [128, 4, TP], F32R, mix)
        qiv_hi = sb("qiv_hi", [128, 4, TP], F32R, mix)
        qiv_lo = sb("qiv_lo", [128, 4, TP], F32R, mix)
        kp_hi = sb("kp_hi", [128, TP + TS], F32R, mix)
        kp_lo = sb("kp_lo", [128, TP + TS], F32R, mix)
        ki_hi, ki_lo = kp_hi[:, 0:TP], kp_lo[:, 0:TP]
        pages = sb("pages", [128, 2, NPG, 512], stack=mix)
        score = [None] + [sb(f"score{t}", [128, 128 * (t + 1)], stack=mix) for t in range(1, NT)]
        score_s = sb("score_s", [TS, LS], stack=mix)
        probs = sb("probs", [128, 3, TP], stack=mix)
        rows = probs[:, :, :].rearrange("p a n -> p (a n)")[:, 0:2 * UW].rearrange("p (a n) -> p a n", a=2)
        toep = sb("toep", [128, H, 256], stack=mix)
        toep_s = sb("toep_s", [128, 136], stack=mix)
        small = sb("small", [128, 21], stack=mix)
        top8, zero1 = small[:, 0:8], small[:, 20:21]
        soft = small[:, 8:20].rearrange("p (m n) -> p m n", n=4)
        near = sb("near", [128, 2, TP], stack=mix)
        pt_hi, pt_lo = kp_hi, kp_lo
        halves = stage_s[:, :, :].rearrange("p a b -> p (a b)")
        kw_t = stage[0:72, 0, :]
        kw_halves = stage[:, 1, 0:272]
        new_u = near[:, 1, 0:4 * TS]
        slots = pages[:, :, :, :].rearrange("p s a b -> p (s a b)")
        u_t = slots[:, 0:NG * UW].rearrange("p (g u) -> p g u", g=NG)
        hist_t = slots[:, NG * UW:NG * (UW + DB * HIST)].rearrange("p (g n) -> p g n", g=NG)
        hist_in = pages[0:DB * HIST, 1, NPG - 1, :]
        qi_s = near[0:64, 0, :].rearrange("p (b n) -> p b n", b=DB)
        wi_b = near[0:64, 1, :].rearrange("p (b n) -> p b n", b=DB)
        tmp_s = near[0:TS, 1, :]
        brow = rows[0:H, 1, 0:384]
        expand = near[0:TS, 0, :]
        kiwi = sb("kiwi", [128, NT + 1, 72], stack=mix)
        wi = sb("wi", [128, NT + 1, 8], stack=mix)
        v_s = sb("v_s", [TS, 512], stack=mix)
        q_s = sb("q_s", [128, 4, TS], stack=mix)
        k_s = sb("k_s", [128, 4, TS], stack=mix)
        ki_s = sb("ki_s", [64, TS], stack=mix)
        wi_t = sb("wi_t", [8, TS], stack=mix)
        ident_r = sb("ident_r", [128, 128], F32R, mix)
        table = sb("table", [1, 32], I32, mix)
        relb = toep[0:NB, 0, 0:H]
        mix.close()
        dec = ExitStack()
        q_pad = sb("q_pad", [128, 4, DB, 64], stack=dec)
        k_t = sb("k_t", [128, 2, 4, PAST], stack=dec)
        p_t = sb("p_t", [128, 5, 128], stack=dec)
        p_new = sb("p_new", [128, 64], stack=dec)
        v_pages = sb("v_pages", [128, 2, NPG, 512], stack=dec)
        dec.close()
        mlp = ExitStack()
        hid_hi = sb("hid_hi", [128, 8, TP], F32R, mlp)
        hid_lo = sb("hid_lo", [128, 8, TP], F32R, mlp)
        hid_s = sb("hid_s", [128, 8, 2 * TS], F32R, mlp)
        x_res = sb("x_res", [128, NT + 1, D], stack=mlp)
        out_t = sb("out_t", [128, NT + 1, D], stack=mlp)
        gate_p = sb("gate_p", [128, D], stack=mlp)
        gate_s = sb("gate_s", [TS, D], stack=mlp)
        ln_post = sb("ln_post", [128, D], stack=mlp)
        half_s = sb("half_s", [TS, 512], stack=mlp)
        halves_mlp = sb("halves_mlp", [128, 512], stack=mlp)
        mlp.close()
        raw_landed = [sem(f"raw_landed{i}") for i in range(NRAW)]
        hi_ready, lo_ready = sem("hi_ready"), sem("lo_ready")
        bank_full = [sem(f"bank_full{i}") for i in range(8)]
        bank_free = [sem(f"bank_free{i}") for i in range(8)]
        act_chain, dve_chain, pool_chain = sem("act_chain"), sem("dve_chain"), sem("pool_chain")
        class Signals(dict):
            def __missing__(self, name):
                self[name] = sem(name)
                return self[name]

        S = Signals()
        stage_out = [sem("stage_out0"), sem("stage_out1")]
        k_page_in = [sem("k_page_in0"), sem("k_page_in1")]
        v_page_in = [sem("v_page_in0"), sem("v_page_in1")]
        block = ctx.enter_context(nc.Block())

        def full(eng, key):
            b, n = USE[key]
            eng.wait_ge(bank_full[b], n)
            return psum[b]

        def free(ins, key):
            ins.then_inc(bank_free[USE[key][0]], 1)

        def evacuated(eng, key):
            b, n = USE[key]
            eng.wait_ge(bank_free[b], n)

        class Chain:

            def __init__(self, eng, s):
                self.eng, self.s, self.n = eng, s, 0

            def __call__(self, ins):
                self.n += 1
                ins.then_inc(self.s, 1)
                self.eng.wait_ge(self.s, self.n)

        def parts_of(n):
            c, cols = piece_shape(PIECES[n][0])
            w = w_split[:, n % NSPLIT, 0:2 * c * cols]
            both = w.rearrange("p (c n) -> p c n", c=c)
            return both[:, :, 0:cols], both[:, :, cols:2 * cols], both

        def rows_of(t):
            return 128 if t < NT else TS

        landed_at, total = [], [0] * NRAW
        for n, (kind, i) in enumerate(PIECES):
            total[n % NRAW] += 16 * (3 if kind == "kiwi" else 1)
            landed_at.append(total[n % NRAW])

        w_in = a["w_in"][0].rearrange("(c p) n -> p c n", p=128)
        ada = a["ada_w"][0].rearrange("(c p) n -> p c n", p=128)
        w_o = a["w_out"][0].rearrange("(c p) n -> p c n", p=128)
        w_1 = a["w_ff1"][0].rearrange("(c p) n -> p c n", p=128)
        w_2 = a["w_ff2"][0].rearrange("(c p) n -> p c n", p=128)
        ck = a["cache_k"][0].rearrange("g p h d -> g p (h d)")
        cv = a["cache_v"][0].rearrange("g p h d -> g p (h d)")
        cx = a["cache_kidx"][0]
        xp = a["x_prompt"][0].rearrange("(t p) d -> p t d", p=128)
        xs = a["x_sample"].rearrange("b t d -> (b t) d")
        kidx_pages = pages[:, 0, :, :].rearrange("p a (b d) -> p (a b) d", d=HD)
        hankel = pages[:, 1, :, :].rearrange("p a (h j) -> p (a h) j", j=256)
        hankel_s = rows[0:64, 0, 0:136]
        N_AT = NT * H

        def turned_probs(m):
            return (pt_hi[:, 0:TP], pt_lo[:, 0:TP]) if m % 2 == 0 else (pu_hi[:, :], pu_lo[:, :])

        @block.sync
        def _(sp):
            def load_piece(n):
                kind, i = PIECES[n]
                if n >= NRAW:
                    sp.wait_ge(lo_ready, n - NRAW + 1)
                s, r = raw_landed[n % NRAW], raw[:, n % NRAW, :]

                c, cols = piece_shape(kind)
                v = r[:, 0:c * cols].rearrange("p (c n) -> p c n", c=c)
                half = slice(4 * (i % 2), 4 * (i % 2) + 4)
                if kind == "ada":
                    x = 512 * (i // 2)
                    sp.dma_start(v, ada[:, half, x:x + 512]).then_inc(s, 16)
                elif kind == "v":
                    sp.dma_start(v, w_in[:, half, OFF_V:OFF_QI]).then_inc(s, 16)
                elif kind in COL0:
                    x = COL0[kind] + 256 * i
                    sp.dma_start(v, w_in[:, :, x:x + 256]).then_inc(s, 16)
                elif kind == "kiwi":
                    sp.dma_start(v[:, :, 0:64], w_in[:, :, OFF_KI:OFF_WI]).then_inc(s, 16)
                    sp.dma_start(v[:, :, 64:128], w_in[:, :, OFF_KI:OFF_WI]).then_inc(s, 16)
                    sp.dma_start(v[:, :, 128:136], w_in[:, :, OFF_WI:D_IN]).then_inc(s, 16)
                elif kind == "poolw":
                    sp.dma_start(v, a["pool_w"][0].rearrange("g p n -> p g n")).then_inc(s, 16)
                elif kind == "wo":
                    nh = i // 2
                    sp.dma_start(v, w_o[:, half, 512 * nh:512 * nh + 512]).then_inc(s, 16)
                elif kind == "w1":
                    sp.dma_start(v, w_1[:, :, 256 * i:256 * i + 256]).then_inc(s, 16)
                else:
                    f, nh, k = i // 4, i % 4 // 2, 4 * (i % 2)
                    sp.dma_start(v, w_2[:, 8 * f + k:8 * f + k + 4, 512 * nh:512 * nh + 512]).then_inc(s, 16)

            def page_of(i):
                return sp.value_load(table[0:1, i:i + 1], min_val=0, max_val=ck.shape[0] - 1)

            sp.dma_start(c_in[0:1, :], a["c_prompt"]).then_inc(S["c_in_landed"], 16)
            sp.dma_start(c_in[1:9, :], a["c_sample"]).then_inc(S["c_in_landed"], 16)
            sp.dma_start(cst[:], a["consts"]).then_inc(S["consts_in"], 16)
            load_piece(0)
            load_piece(1)
            sp.dma_start(x_in[:, 0:NT, :], xp).then_inc(S["x_landed"], 16)
            sp.dma_start(x_in[0:TS, NT, :], xs).then_inc(S["x_landed"], 16)
            for n in range(2, AT[("k", 0)]):
                load_piece(n)
            sp.wait_ge(S["table_in"], 16)
            for i in range(DB * NPG):
                sp.dma_start(kidx_pages[:, i, :], cx[bass.ds(page_of(i), 1)].rearrange("o p d -> (o p) d"))\
                    .then_inc(S["kidx_in"], 16)
            for n in range(AT[("k", 0)], AT[("ada", 12)] + 2):
                load_piece(n)

            def load_pages(b, cache, slots, landed):
                for g in range(NPG):
                    sp.dma_start(slots[:, b % 2, g, :],
                                 cache[bass.ds(page_of(b * NPG + g), 1)].rearrange("o p n -> (o p) n"))\
                        .then_inc(landed[b % 2], 16)

            sp.wait_ge(S["pool_lo"], NG)
            for b in range(2):
                load_pages(b, ck, pages, k_page_in)
            for n in range(AT[("ada", 12)] + 2, AT[("wo", 0)] + 2):
                load_piece(n)
            full(sp, ("pv", N_AT - 1))
            for bp in range(4):
                if bp == 0:
                    for b in range(2):
                        load_pages(b, cv, v_pages, v_page_in)
                if bp < 3:
                    for b in (2 * bp + 2, 2 * bp + 3):
                        full(sp, ("KT", b - 2, 3))
                        load_pages(b, ck, pages, k_page_in)
                if bp:
                    full(sp, ("pvS", bp - 1))
                    for b in (2 * bp, 2 * bp + 1):
                        load_pages(b, cv, v_pages, v_page_in)
            for n in range(AT[("wo", 0)] + 2, len(PIECES)):
                load_piece(n)

        @block.gpsimd
        def _(pool):
            link = Chain(pool, pool_chain)
            pool.dma_start(rows_in[0:8, :], a["ln1_pre"].rearrange("o (c p) -> (o c) p", p=128)).then_inc(S["small_in"], 16)
            pool.dma_start(rows_in[8:16, :], a["ln2_pre"].rearrange("o (c p) -> (o c) p", p=128)).then_inc(S["small_in"], 16)
            pool.dma_start(rows_in[16:20, :], a["pool_scale"].rearrange("o (c p) -> (o c) p", p=128)).then_inc(S["small_in"], 16)
            pool.dma_start(relb, a["rel_bias"]).then_inc(S["small_in"], 16)
            pool.dma_start(mod_rows[41:42, :], a["ada_b"][:, 0:2048]).then_inc(S["bias_in"], 16)
            pool.dma_start(table[:], a["page_table"].rearrange("a b -> (a b)").rearrange("(o n) -> o n", o=1))\
                .then_inc(S["table_in"], 16)
            pool.dma_start(o["pool_s"][0, :, 0:HIST - DS, :], a["state_pool"][0, :, DS:HIST, :]).then_inc(S["outs"], 16)
            nc.gpsimd.memset(wi_b, 0.0).then_inc(S["pad_zero"], 1)
            full(pool, ("modT", 0))
            pool.dma_start(mod_rows[41:42, :], a["ada_b"][:, 3072:5120]).then_inc(S["bias_in"], 16)
            evacuated(pool, "biasrow")
            pool.dma_start(dram_bias, brow[:]).then_inc(S["bias_row_out"], 16)
            pool.wait_ge(S["bias_row_out"], 16)
            pool.dma_start(hankel, bass.AP(tensor=dram_bias.tensor, offset=0, ap=[[1, 128], [384, H], [1, 256]]))\
                .then_inc(S["hankel_in"], 16)
            for h in range(H):
                pool.dma_start(rows[h * DS:(h + 1) * DS, 0, 0:136],
                               bass.AP(tensor=dram_bias.tensor, offset=384 * h + 120, ap=[[1, DS], [1, 136]]))\
                    .then_inc(S["hankel_s_in"], 16)
            evacuated(pool, "kiwi")
            pool.dma_start(o["kidx_p"][0, 0].rearrange("(t p) d -> p t d", p=128), kiwi[:, 0:NT, 0:64]).then_inc(S["outs"], 16)
            pool.dma_start(o["kidx_s"][0].rearrange("b t d -> (b t) d"), kiwi[0:TS, NT, 0:64]).then_inc(S["outs"], 16)

            full(pool, ("ixSn", DB - 1))
            full(pool, ("ixS", DB - 1))
            pool.dma_start(hist_in, a["state_pool"][0].rearrange("b i c -> (b i) c")).then_inc(S["hist_in"], 16)
            nc.gpsimd.memset(u_t, 0.0).then_inc(S["u_zero"], 1)

            stored = [0]

            def store(dst, rows_from, rows_to):
                n = stored[0]
                pool.dma_start(dst, stage[rows_from:rows_to, n % 2, :]).then_inc(stage_out[n % 2], 16)
                stored[0] += 1

            for t in range(NT):
                evacuated(pool, ("kout", t))
                store(o["k_p"][0, 0, 128 * t:128 * t + 128].rearrange("p h d -> p (h d)"), 0, 128)
            evacuated(pool, ("kout", NT))
            store(o["k_s"][0].rearrange("b t h d -> (b t) (h d)"), 0, TS)
            for g in range(NG):
                u = u_t[:, g, :]
                evacuated(pool, ("uS", g // 2))
                if g == 0:
                    evacuated(pool, "hist")
                    evacuated(pool, "scSn")
                link(nc.gpsimd.tensor_copy(u[:, 16 + TP:].rearrange("p (b s) -> p b s", b=DB)[:, :, 1:1 + HIST],
                                           hist_t[:, g, :].rearrange("p (b i) -> p b i", b=DB)))
                if g >= 1:
                    pool.wait_ge(S["pooled"], g)
                src, lo = u, 0
                for lev in range(g + 1):
                    sh = 1 << lev
                    lo += sh
                    dst = rows[:, lev % 2, :]
                    ins = nc.gpsimd.tensor_tensor(dst[:, lo:UW], src[:, lo:UW], src[:, lo - sh:UW - sh], ALU.add)
                    if lev == g:
                        ins.then_inc(S["window_sums"], 1)
                    else:
                        link(ins)
                    src = dst
            evacuated(pool, ("uo", NG - 1))
            pool.dma_start(o["pool_p"][0, 0], near[128 - HIST:128, 0, :]).then_inc(S["state_out"], 16)
            for b in range(DB):
                pool.dma_start(o["pool_s"][0, b, HIST - DS:HIST, :], near[b * DS:(b + 1) * DS, 0, :])\
                    .then_inc(S["state_out"], 16)
            for t in range(NT):
                pool.wait_ge(S["v_staged"], t + 1)
                store(o["v_p"][0, 0, 128 * t:128 * t + 128].rearrange("p h d -> p (h d)"), 0, 128)
            evacuated(pool, ("v", NT))
            pool.dma_start(o["v_s"][0].rearrange("b t h d -> (b t) (h d)"), v_s[:]).then_inc(S["outs"], 16)

            pool.wait_ge(S["state_out"], 16 * (1 + DB))
            evacuated(pool, ("v", NT))
            for t in range(NT):
                L = 128 * (t + 1)
                w = min(L, 256)
                mask = cc("causal") if t == 0 else score[t]
                pool.wait_ge(S["chosen"], t)
                if t == 0:
                    evacuated(pool, ("toep", 3))
                for h in range(H):
                    n = t * H + h
                    if n >= 2:
                        pool.wait_ge(S["peaks"], n - 1)
                    if n == 18:
                        full(pool, ("modT", 1))
                        pool.dma_start(mod_rows[41:42, 0:1024], a["ada_b"][:, 2048:3072]).then_inc(S["bias_in"], 16)
                        pool.dma_start(mod_rows[41:42, 1024:2048], a["ada_b"][:, 5120:6144]).then_inc(S["bias_in"], 16)
                    if h < 2 and L > w:
                        link(nc.gpsimd.tensor_copy(near[:, n % 2, 0:L - w], mask[:, 0:L - w]))
                    nc.gpsimd.tensor_tensor(near[:, n % 2, L - w:L], toep[:, h, 256 - w:256], mask[:, L - w:L],
                                            ALU.add).then_inc(S["near_ok"], 1)
            evacuated(pool, ("qS", 1))
            full(pool, ("pv", N_AT - 1))
            link(nc.gpsimd.tensor_copy(expand.rearrange("p (b h t) -> p b h t", b=DB, h=H),
                                       cc("ident", TS)[:, 0:TS].rearrange("p (b t) -> p b t", b=DB).unsqueeze(2)
                                       .to_broadcast([TS, DB, H, DS])))
            link(nc.gpsimd.memset(q_pad[:], 0.0))
            for c in range(4):
                for hh in range(2):
                    nc.gpsimd.tensor_copy(
                        q_pad[64 * hh:64 * hh + 64, c, :, (2 * c + hh) * DS:(2 * c + hh + 1) * DS],
                        q_s[64 * hh:64 * hh + 64, c, :].rearrange("p (b t) -> p b t", b=DB)).then_inc(S["padded"], 1)
            evacuated(pool, ("pvS", 3))
            pool.wait_ge(S["outs"], 16 * 4)
            pool.dma_start(x_res[:, 0:NT, :], xp).then_inc(S["x_again"], 16)
            pool.dma_start(x_res[0:TS, NT, :], xs).then_inc(S["x_again"], 16)
            pool.dma_start(ln_post[:], a["ln1_post"].to_broadcast([128, D])).then_inc(S["gain_in"], 16)
            evacuated(pool, ("gS", 0, 1))
            pool.dma_start(ln_post[:], a["ln2_post"].to_broadcast([128, D])).then_inc(S["gain_in"], 16)
            yp = o["y_p"][0].rearrange("(t p) d -> p t d", p=128)
            for t in range(NT + 1):
                pool.wait_ge(S["y_ok"], t + 1)
                if t < NT:
                    pool.dma_start(yp[:, t, :], x_res[:, t, :]).then_inc(S["y_out"], 16)
                else:
                    pool.dma_start(o["y_s"].rearrange("b t d -> (b t) d"), x_res[0:TS, t, :]).then_inc(S["y_out"], 16)
            pool.wait_ge(S["y_out"], 16 * (NT + 1))
            for n in (stored[0], stored[0] + 1):
                pool.wait_ge(stage_out[n % 2], 16 * (n // 2))
            pool.wait_ge(S["outs"], 16 * 4)

        @block.tensor
        def _(pe):
            uses = [0] * 8

            def claim(key):
                b, n = USE[key]
                uses[b] += 1
                assert n == uses[b], key
                if n > 1:
                    pe.wait_ge(bank_free[b], n - 1)
                return psum[b]

            def done(ins, key):
                ins.then_inc(bank_full[USE[key][0]], 1)

            def piece(kind, i):
                n = AT[(kind, i)]
                pe.wait_ge(lo_ready, n + 1)
                return parts_of(n)

            def mm(out, lhsT, rhs, start, stop):
                return nc.tensor.matmul(out, lhsT, rhs, start=start, stop=stop, skip_group_check=True)

            def turn(out, in_, k, start=True, stop=True):
                return nc.tensor.transpose(out, in_, cc("ident")[0:k, 0:k])

            pe.wait_ge(S["c_in_landed"], 32)
            pe.wait_ge(S["consts_in"], 16)
            t_ = claim("cT")
            for kc in range(KC):
                last = turn(t_[:, 9 * kc:9 * kc + 9], c_in[:, 128 * kc:128 * kc + 128], 9)
            done(last, "cT")
            pe.wait_ge(S["small_in"], 64)
            done(turn(claim("rowsT")[:, 0:20], rows_in[:, :], 20), "rowsT")
            pe.wait_ge(S["c_hi"], 1)
            evacuated(pe, "cT")

            mod_bank = [None]

            def modulation(i):
                hi, lo, _ = piece("ada", i)
                if i % 2 == 0:
                    mod_bank[0] = claim(("ada", i + 1))[0:72, :]
                out = mod_bank[0]
                for k4 in range(4):
                    kc = 4 * (i % 2) + k4
                    mm(out, c_split[:, kc, :], hi[:, k4, :], kc == 0, False)
                    last = mm(out, c_split[:, kc, :], lo[:, k4, :], False, kc == KC - 1)
                if i % 2:
                    done(last, ("ada", i))
                else:
                    last.then_inc(S["ada_half"], 1)

            def turned_modulation(k):
                evacuated(pe, ("ada", 7 + 12 * k))
                pe.wait_ge(S["bias_in"], 16 * (k + 1))
                out = claim(("modT", k))
                for j in range(16):
                    last = mm(out[:, 9 * j:9 * j + 9], mod_rows[:, 128 * j:128 * j + 128], cc("sel_t", 42), True, True)
                done(last, ("modT", k))

            def turned_hidden(k, src):
                pe.wait_ge(S["normed"], (NT + 1) * (k + 1))
                for kc in range(KC):
                    out = claim(("hT", k, kc))
                    for t in range(NT):
                        last = turn(out[:, 128 * t:128 * t + 128], src[:, t, 128 * kc:128 * kc + 128], 128)
                    done(last, ("hT", k, kc))
                out = claim(("hTS", k))
                for kc in range(KC):
                    last = turn(out[:, TS * kc:TS * kc + TS], src[0:TS, NT, 128 * kc:128 * kc + 128], TS)
                done(last, ("hTS", k))

            for i in range(8):
                modulation(i)
            turned_modulation(0)
            turned_hidden(0, x_nrm)

            def chunk_p(out, hi, lo, cols):
                for kc in range(KC):
                    mm(out, hi[:, kc, cols], act_hi[:, kc, :], kc == 0, False)
                    mm(out, hi[:, kc, cols], act_lo[:, kc, :], False, False)
                    last = mm(out, lo[:, kc, cols], act_hi[:, kc, :], False, kc == KC - 1)
                return last

            def rows_s(out, both):
                for kc in range(KC):
                    last = mm(out, act_s[:, kc, :], both[:, kc, :], kc == 0, kc == KC - 1)
                return last

            pending = []

            def project(kind, i):
                hi, lo, both = piece(kind, i)
                for j in range(2):
                    k = (kind, 2 * i + j)
                    done(chunk_p(claim(k)[:, :], hi, lo, slice(128 * j, 128 * j + 128)), k)
                    if j == 0:
                        fold_pending()
                done(rows_s(claim((kind + "R", i))[:, :], both), (kind + "R", i))
                pending.append((kind, i))

            def fold_pending():
                while pending:
                    kind, i = pending.pop()
                    evacuated(pe, (kind + "R", i))
                    src = halves_mlp if kind == "w1" else halves
                    out = claim((kind + "S", i))
                    for j in range(2):
                        y = out[:, TS * j:TS * j + TS]
                        mm(y, src[:, 128 * j:128 * j + 128], cc("fold"), True, False)
                        last = mm(y, src[:, 256 + 128 * j:256 + 128 * j + 128], cc("fold"), False, True)
                    done(last, (kind + "S", i))

            evacuated(pe, ("hT", 0, 7))
            pe.wait_ge(S["h_hi"], KC)
            evacuated(pe, ("hTS", 0))
            pe.wait_ge(S["h_low"], KC)
            pe.wait_ge(S["hs_lo"], 1)
            for i in range(2):
                project("qi", i)
            hi, lo, both = piece("kiwi", 0)
            done(chunk_p(claim("ki")[:, :], hi, lo, slice(0, 128)), "ki")
            fold_pending()
            done(chunk_p(claim("kw")[0:72, :], hi, lo, slice(64, 136)), "kw")
            done(rows_s(claim("kiR")[:, 0:272], both), "kiR")
            out = claim("biasrow")
            done(mm(out[0:H, 0:384], relb, cc("bucket", NB), True, True), "biasrow")
            evacuated(pe, "kw")
            evacuated(pe, "kiR")
            out = claim("kiS")[0:64, 0:TS]
            mm(out, kw_halves[:, 0:64], cc("fold"), True, False)
            done(mm(out, kw_halves[:, 136:200], cc("fold"), False, True), "kiS")
            out = claim("kiwi")
            for t in range(NT):
                turn(out[:, 72 * t:72 * t + 72], kw_t[:, 128 * t:128 * t + 128], 72)
            y = out[0:TS, 72 * NT:72 * NT + 72]
            mm(y, cc("fold"), kw_halves[:, 64:136], True, False)
            done(mm(y, cc("fold"), kw_halves[:, 200:272], False, True), "kiwi")
            pe.wait_ge(S["wi_ok"], 1)
            done(turn(claim("wiT")[0:H, 0:TS], wi[0:TS, NT, :], TS), "wiT")
            evacuated(pe, "wiT")
            done(mm(claim("wiR")[0:64, 0:TS], cc("heads", H), wi_t[:, :], True, True), "wiR")
            pe.wait_ge(S["hankel_in"], 16)
            for j in range(4):
                done(mm(claim(("toep", j))[:, :], cc("flip"), hankel[:, 2 * j:2 * j + 2, :], True, True), ("toep", j))
            pe.wait_ge(S["hankel_s_in"], 16 * H)
            done(mm(claim("toepS")[:, 0:136], cc("unflip", 64), hankel_s, True, True), "toepS")

            def by_head(out, q_h, q_l, k_h, k_l, h, tok, L):
                r, c = slice(64 * (h % 2), 64 * (h % 2) + 64), h // 2
                mm(out, q_h[r, c, tok], k_h(r, c), True, False)
                mm(out, q_h[r, c, tok], k_l(r, c), False, False)
                return mm(out, q_l[r, c, tok], k_h(r, c), False, True)

            evacuated(pe, ("qi", 3))
            evacuated(pe, "ki")
            for t in range(1, NT):
                L = 128 * (t + 1)
                for h in range(H):
                    out = claim(("ix", t, h))
                    done(by_head(out[:, 0:L], qiv_hi, qiv_lo, lambda r, c: ki_hi[r, 0:L], lambda r, c: ki_lo[r, 0:L],
                                 h, slice(128 * t, 128 * t + 128), L), ("ix", t, h))
            kx_t = pages[0:64, 1, :, :].rearrange("p a b -> p (a b)")
            pe.wait_ge(S["kidx_in"], 16 * DB * NPG)
            evacuated(pe, "kiS")
            evacuated(pe, ("qiS", 1))
            evacuated(pe, "wiR")

            def turn_kidx(b):
                out = claim(("kxT", b))
                for g in range(NPG):
                    last = turn(out[0:64, 128 * g:128 * g + 128], kidx_pages[:, NPG * b + g, :], 128)
                done(last, ("kxT", b))

            turn_kidx(0)
            for b in range(DB):
                evacuated(pe, ("kxT", b))
                done(mm(claim(("ixS", b))[0:64, :], qi_s[:, b, :], kx_t[:, 512 * (b % 2):512 * (b % 2) + 512], True, True), ("ixS", b))
                done(mm(claim(("ixSn", b))[0:64, 0:DS], qi_s[:, b, :], ki_s[:, b * DS:(b + 1) * DS], True, True), ("ixSn", b))
                if b + 1 < DB:
                    turn_kidx(b + 1)
                if b == 0:
                    sc, scn = claim("scS"), claim("scSn")
                evacuated(pe, ("ixSn", b))
                evacuated(pe, ("ixS", b))
                last1 = mm(sc[0:TS, :], wi_b[:, b, :], rows[0:64, b % 2, 0:PAST], b == 0, b == DB - 1)
                last2 = mm(scn[0:TS, 0:DS], wi_b[:, b, :], rows[0:64, b % 2, PAST:LS], b == 0, b == DB - 1)
                if b == DB - 1:
                    done(last1, "scS")
                    done(last2, "scSn")
                else:
                    last2.then_inc(S["relu_used"], 1)

            def by_token(kind, first, name, x_hi, x_lo, x_s, f=None, between=None):
                outs = []
                for half in range(2):
                    hi, lo, _ = piece(kind, first + half)
                    if f is not None:
                        pe.wait_ge(S["w1_done"], 8 * f + 4 * (half + 1))
                        pe.wait_ge(S["w1s_done"], 4 * f + 2 * (half + 1))
                    for t in range(NT + 1):
                        if half == 0:
                            outs.append(claim(name + (t,)))
                        for k4 in range(4):
                            k = 4 * half + k4
                            if t < NT:
                                tok = slice(128 * t, 128 * t + 128)
                                mm(outs[t][:, :], x_hi[:, k, tok], hi[:, k4, :], k == 0, False)
                                mm(outs[t][:, :], x_hi[:, k, tok], lo[:, k4, :], False, False)
                                last = mm(outs[t][:, :], x_lo[:, k, tok], hi[:, k4, :], False, k == 7)
                            else:
                                mm(outs[t][:, :], x_s[:, k, :], hi[:, k4, :], k == 0, False)
                                last = mm(outs[t][:, :], x_s[:, k, :], lo[:, k4, :], False, k == 7)
                        if half == 1:
                            done(last, name + (t,))
                        if half == 0 and t == 0:
                            fold_pending()
                        if between is not None and half == 1:
                            between(t)
                    if half == 0:
                        last.then_inc(S["half_done"], 1)

            for i in range(2):
                project("k", i)
                if i == 0:
                    pe.wait_ge(S["hist_in"], 16)
                    out = claim("hist")
                    for g in range(NG):
                        last = turn(out[:, 120 * g:120 * g + 120], hist_in[:, 128 * g:128 * g + 128], 120)
                    done(last, "hist")

            def turn_keys():
                evacuated(pe, ("k", 3))
                evacuated(pe, ("kS", 1))
                pe.wait_ge(S["ident_ok"], 1)
                for t in range(NT + 1):
                    out = claim(("kout", t))
                    for c in range(4):
                        y = out[:, 128 * c:128 * c + 128]
                        if t < NT:
                            mm(y, k_hi[:, c, 128 * t:128 * t + 128], ident_r[:, :], True, False)
                            last = mm(y, k_lo[:, c, 128 * t:128 * t + 128], ident_r[:, :], False, True)
                        else:
                            last = turn(y[0:TS, :], k_s[:, c, :], 128)
                    done(last, ("kout", t))

            for i in range(2):
                project("u", i)
            project("q", 0)

            def turn_channels(g):
                out = claim(("uo", g))
                turn(out[:, 0:128], u_t[:, g, 16 + TP - 128:16 + TP], 128)
                done(turn(out[0:TS, 128:256], new_u[:, TS * g:TS * g + TS], 128), ("uo", g))

            evacuated(pe, ("u", 3))
            evacuated(pe, ("uS", 1))
            for g in range(NG):
                if g == 2:
                    fold_pending()
                turn_channels(g)
            turn_keys()
            project("q", 1)

            def pool_maps(g):
                if g == NG:
                    return
                hi, lo, _ = piece("poolw", 0)
                pe.wait_ge(S["pool_lo"], g + 1)
                wh, wl = hi[:, g, :], lo[:, g, :]
                for key, cols in ((("pm", g), slice(0, TP)), (("pmS", g), slice(TP, TP + TS))):
                    out = claim(key)[:, 0:cols.stop - cols.start]
                    mm(out, wh, pt_hi[:, cols], True, False)
                    mm(out, wh, pt_lo[:, cols], False, False)
                    done(mm(out, wl, pt_hi[:, cols], False, True), key)

            by_token("v", 0, ("v",), act_hi, act_lo, act_s, between=pool_maps)

            evacuated(pe, ("q", 3))
            for n in range(N_AT + 4):
                if n < N_AT:
                    t, h = n // H, n % H
                    L = 128 * (t + 1)
                    out = claim(("lg", n))
                    done(by_head(out[:, 0:L], q_hi, q_lo, lambda r, c: k_hi[r, c, 0:L], lambda r, c: k_lo[r, c, 0:L],
                                 h, slice(128 * t, 128 * t + 128), L), ("lg", n))
                if n >= 4:
                    m = n - 4
                    t, h = m // H, m % H
                    if m == 0:
                        evacuated(pe, ("v", NT - 1))
                    evacuated(pe, ("pT", m))
                    out = claim(("pv", m))[:, 0:128]
                    ph, pl = turned_probs(m)
                    for kb in range(t + 1):
                        v = slice(128 * (h // 2), 128 * (h // 2) + 128)
                        p = slice(128 * kb, 128 * kb + 128)
                        mm(out, qiv_hi[:, kb, v], ph[:, p], kb == 0, False)
                        mm(out, qiv_hi[:, kb, v], pl[:, p], False, False)
                        last = mm(out, qiv_lo[:, kb, v], ph[:, p], False, kb == t)
                    done(last, ("pv", m))
                if 2 <= n <= N_AT + 1:
                    m = n - 2
                    pe.wait_ge(S["probs_ok"], m + 1)
                    out = claim(("pT", m))
                    for kb in range(m // H + 1):
                        last = turn(out[:, 128 * kb:128 * kb + 128], probs[:, m % 3, 128 * kb:128 * kb + 128], 128)
                    done(last, ("pT", m))
                if n < N_AT and n % 2 == 1:
                    modulation(FILL[n // 2])
                if n == 17:
                    turned_modulation(1)

            def turn_pages(b):
                pe.wait_ge(k_page_in[b % 2], 16 * NPG * (b // 2 + 1))
                for c in range(4):
                    out = claim(("KT", b, c))
                    for g in range(NPG):
                        last = turn(out[:, 128 * g:128 * g + 128], pages[:, b % 2, g, 128 * c:128 * c + 128], 128)
                    done(last, ("KT", b, c))

            turn_pages(0)
            turn_pages(1)
            pe.wait_ge(S["padded"], 8)
            pe.wait_ge(S["chosen"], NT)
            evacuated(pe, ("kS", 1))
            for bp in range(4):
                out, new = claim(("lgS", bp)), claim(("lgSn", bp))
                ex = expand[:, 128 * bp:128 * bp + 128]
                mm(out[:, :], ex, score_s[:, 0:PAST], True, False)
                mm(new[:, 0:DS], ex, score_s[:, PAST:LS], True, False)
                for b2 in range(2):
                    b, r = 2 * bp + b2, slice(64 * b2, 64 * b2 + 64)
                    for c in range(4):
                        evacuated(pe, ("KT", b, c))
                        last1 = mm(out[r, :], q_pad[:, c, b, :], k_t[:, b2, c, :], False, c == 3 and b2 == 1)
                        last2 = mm(new[r, 0:DS], q_pad[:, c, b, :], k_s[:, c, b * DS:(b + 1) * DS], False, c == 3 and b2 == 1)
                done(last1, ("lgS", bp))
                done(last2, ("lgSn", bp))
                if bp < 3:
                    turn_pages(2 * bp + 2)
                    turn_pages(2 * bp + 3)
                pe.wait_ge(S["prob_new"], bp + 1)
                out = claim(("pTS", bp))
                for g in range(NPG):
                    last = turn(out[:, 128 * g:128 * g + 128], rows[:, bp % 2, 128 * g:128 * g + 128], 128)
                done(last, ("pTS", bp))
                done(turn(claim(("pTSn", bp))[0:64, 0:128], p_new[:, :], 128), ("pTSn", bp))
                evacuated(pe, ("pTSn", bp))
                evacuated(pe, ("pTS", bp))
                out = claim(("pvS", bp))
                for b2 in range(2):
                    pe.wait_ge(v_page_in[b2], 16 * NPG * (bp + 1))
                    for c in range(4):
                        y = out[:, 16 * (4 * b2 + c):16 * (4 * b2 + c) + 16]
                        col = slice(64 * b2 + 16 * c, 64 * b2 + 16 * c + 16)
                        v = slice(128 * c, 128 * c + 128)
                        for g in range(NPG):
                            mm(y, v_pages[:, b2, g, v], p_t[:, g, col], g == 0, False)
                        last = mm(y, v_s[:, v], p_t[0:64, 4, col], False, True)
                done(last, ("pvS", bp))

            pe.wait_ge(S["bias_in"], 16 * 4)

            def gates(k):
                for j in range(2):
                    r = mod_rows[:, 1024 * k + 512 * j:1024 * k + 512 * j + 512]
                    done(mm(claim(("gP", k, j))[:, :], cc("sel_p", 42), r, True, True), ("gP", k, j))
                    done(mm(claim(("gS", k, j))[0:TS, :], cc("sel_s", 42), r, True, True), ("gS", k, j))

            evacuated(pe, ("ada", 21))
            evacuated(pe, ("ada", 23))
            gates(0)

            evacuated(pe, ("pmS", NG - 1))
            evacuated(pe, ("pm", NG - 1))
            evacuated(pe, ("pv", N_AT - 1))
            evacuated(pe, ("pvS", 3))
            for nh in range(2):
                by_token("wo", 2 * nh, ("wo", nh), act_hi, act_lo, act_s)

            gates(1)
            turned_hidden(1, out_t)
            evacuated(pe, ("hT", 1, 7))
            pe.wait_ge(S["h_hi"], 2 * KC)
            pe.wait_ge(S["h_low"], 2 * KC)
            pe.wait_ge(S["hs_lo"], 2)
            for f in range(QF):
                for i in range(4):
                    project("w1", 4 * f + i)
                for nh in range(2):
                    by_token("w2", 4 * f + 2 * nh, ("w2", f, nh), hid_hi, hid_lo, hid_s, f)

        def split_hi_of(act, n):
            kind, i = PIECES[n]
            act.wait_ge(raw_landed[n % NRAW], landed_at[n])
            if n >= NSPLIT:
                pk = PIECES[n - NSPLIT]
                piece_used(act, pk)
            hi, c = parts_of(n)[0], piece_shape(kind)
            nc.scalar.activation(hi, raw[:, n % NRAW, 0:c[0] * c[1]].rearrange("p (c n) -> p c n", c=c[0]), ACT.Copy)\
                .then_inc(hi_ready, 1)

        def piece_used(eng, pk):
            kind, i = pk
            if kind == "ada" and i % 2 == 0:
                eng.wait_ge(S["ada_half"], 1 + [k for k in PIECES if k[0] == "ada"].index(pk) // 2)
            elif kind == "v" and i == 0:
                eng.wait_ge(S["half_done"], 1)
            elif kind == "wo" and i % 2 == 0:
                eng.wait_ge(S["half_done"], 2 + i // 2)
            elif kind == "w2" and i % 2 == 0:
                eng.wait_ge(S["half_done"], 4 + i // 2)
            else:
                full(eng, last_use(kind, i))

        @block.scalar
        def _(act):
            link = Chain(act, act_chain)
            split = [0]

            def hi_until(n):
                while split[0] < min(n, len(PIECES)):
                    split_hi_of(act, split[0])
                    split[0] += 1

            def run(out, in_, func=ACT.Copy, **kw):
                return nc.scalar.activation(out, in_, func, **kw)

            squared = [0]

            def square(k, t, src):
                r = rows_of(t)
                if NORM[k, t]:
                    act.wait_ge(S["squares"], NORM[k, t])
                junk = stage[:, :, :].rearrange("p a n -> p (a n)")
                x = (NT + 1) * k + t
                run(junk[0:r, :], src[0:r, t, :], ACT.Square, accum_out=ss[0:r, x:x + 1]).then_inc(S["squares"], 1)

            def root(k, t):
                x = (NT + 1) * k + t
                act.wait_ge(S["mean_ok"], NORM[k, t] + 1)
                run(rstd[0:rows_of(t), x:x + 1], ss[0:rows_of(t), x:x + 1], ACT.Sqrt).then_inc(S["root_ok"], 1)

            def turned_hidden(k):
                act.wait_ge(S["mod_ok"], 2 * (k + 1))
                for kc in range(KC):
                    out = full(act, ("hT", k, kc))
                    n = k * KC + kc
                    if k * KC + kc >= 2:
                        act.wait_ge(S["h_low"], n - 1)
                    free(run(stage[:, kc % 2, :], out[:, :], ACT.Identity,
                             scale=mod_t[:, 16 * k + 8 + kc, 0:1], bias=mod_t[:, 16 * k + kc, 0:1]), ("hT", k, kc))
                    evacuated(act, ("hT", k, kc))
                    run(act_hi[:, kc, :], stage[:, kc % 2, :]).then_inc(S["h_hi"], 1)
                act.wait_ge(S["hs_staged"], k + 1)
                run(act_s[:, :, 0:TS], stage_s[:, :, :]).then_inc(S["hs_hi"], 1)

            act.wait_ge(S["pad_zero2"], 1)
            out = full(act, "cT")
            run(c_split[:, :, 0:9], out[:, 0:72].rearrange("p (c m) -> p c m", m=9)).then_inc(S["c_hi"], 1)
            hi_until(2)
            free(run(rows_t[:, :], full(act, "rowsT")[:, 0:20]), "rowsT")
            act.wait_ge(S["x_landed"], 32)
            for t in range(NT + 1):
                square(0, t, x_in)
            for t in range(NT + 1):
                root(0, t)

            def modulation(i):
                if i % 2:
                    out = full(act, ("ada", i))
                hi_until(AT[("ada", i)] + 3)
                if i in (13, 9):
                    full(act, ("modT", 0 if i == 13 else 1))
                if i % 2:
                    x = 256 * (ADA_ROW[i] - 1)
                    free(run(mod_rows[0:41, x:x + 512], out[0:41, :]), ("ada", i))

            for i in range(8):
                modulation(i)
            turned_hidden(0)

            def pair(kind, i, chunk, tail):
                for j in range(2):
                    chunk(2 * i + j, full(act, (kind, 2 * i + j)))
                n = AT[(kind, i)]
                hi_until(n + 3)
                free(run(halves, full(act, (kind + "R", i))[:, :]), (kind + "R", i))
                tail(i, full(act, (kind + "S", i)))

            def qi_tail(i, out):
                for hh in range(2):
                    ins = run(qi_s.rearrange("p b (c x t) -> p x c b t", x=2, t=DS)[:, hh, 2 * i:2 * i + 2],
                              out[64 * hh:64 * hh + 64, 0:2 * TS].rearrange("p (c b t) -> p c b t", c=2, b=DB))
                free(ins, ("qiS", i))

            for i in range(2):
                pair("qi", i, lambda c, out: run(qiv_hi[:, c, :], out[:, :]).then_inc(S["proj_hi"], 1), qi_tail)
            run(ki_hi[:, :], full(act, "ki")[:, :]).then_inc(S["proj_hi"], 1)
            free(run(kw_t, full(act, "kw")[0:72, :]), "kw")
            hi_until(AT[("kiwi", 0)] + 3)
            free(run(kw_halves, full(act, "kiR")[:, 0:272]), "kiR")
            run(brow[:, :], full(act, "biasrow")[0:H, 0:384]).then_inc(bank_free[USE["biasrow"][0]], 1)
            free(run(ki_s[:, :], full(act, "kiS")[0:64, 0:TS]), "kiS")
            out = full(act, "kiwi")
            run(kiwi[:, 0:NT, :], out[:, 0:72 * NT].rearrange("p (t n) -> p t n", t=NT))
            free(run(kiwi[0:TS, NT, :], out[0:TS, 72 * NT:72 * NT + 72]), "kiwi")
            free(run(wi_t[:, :], full(act, "wiT")[0:H, 0:TS]), "wiT")
            for j in range(4):
                free(run(toep[:, 2 * j:2 * j + 2, :], full(act, ("toep", j))[:, :].rearrange("p (h j) -> p h j", h=2)), ("toep", j))
            free(run(toep_s[:, :], full(act, "toepS")[:, 0:136]), "toepS")
            act.wait_ge(S["consts_in"], 16)
            run(ident_r[:, :], cc("ident")).then_inc(S["ident_ok"], 1)

            full(act, "toepS")
            for t in range(1, NT):
                L = 128 * (t + 1)
                for h in range(H):
                    n = (t - 1) * H + h
                    out = full(act, ("ix", t, h))
                    if n >= 2:
                        act.wait_ge(S["relu_added"], n - 1)
                    free(run(rows[:, n % 2, 0:L], out[:, 0:L], ACT.Relu, scale=HD ** -0.5), ("ix", t, h))
            act.wait_ge(S["relu_added"], (NT - 1) * H)
            kx_t = pages[0:64, 1, :, :].rearrange("p a b -> p (a b)")

            def kidx_keep(b):
                free(run(kx_t[:, 512 * (b % 2):512 * (b % 2) + 512], full(act, ("kxT", b))[0:64, :]), ("kxT", b))

            kidx_keep(0)
            for b in range(DB):
                if b >= 2:
                    act.wait_ge(S["relu_used"], b - 1)
                free(run(rows[0:64, b % 2, 0:PAST], full(act, ("ixS", b))[0:64, :], ACT.Relu, scale=HD ** -0.5), ("ixS", b))
                free(run(rows[0:64, b % 2, PAST:LS], full(act, ("ixSn", b))[0:64, 0:DS], ACT.Relu, scale=HD ** -0.5), ("ixSn", b))
                if b + 1 < DB:
                    kidx_keep(b + 1)

            def k_tail(i, out):
                free(run(k_s[:, 2 * i:2 * i + 2, :], out[:, 0:2 * TS].rearrange("p (c n) -> p c n", c=2)), ("kS", i))

            def q_tail(i, out):
                free(run(q_s[:, 2 * i:2 * i + 2, :], out[:, 0:2 * TS].rearrange("p (c n) -> p c n", c=2),
                         scale=HD ** -0.5), ("qS", i))

            def k_chunk(c, out):
                run(k_hi[:, c, :], out[:, :]).then_inc(S["proj_hi"], 1)

            def q_chunk(c, out):
                run(q_hi[:, c, :], out[:, :], scale=HD ** -0.5).then_inc(S["proj_hi"], 1)

            staged = [0]

            def stage_copy(out, r):
                n = staged[0]
                if n >= 2:
                    act.wait_ge(stage_out[n % 2], 16 * (n // 2))
                ins = run(stage[0:r, n % 2, :], out)
                staged[0] += 1
                return ins

            pair("k", 0, k_chunk, k_tail)
            free(run(hist_t, full(act, "hist")[:, 0:480].rearrange("p (g n) -> p g n", g=NG)), "hist")
            pair("k", 1, k_chunk, k_tail)
            def u_chunk(g, out):
                if g == 0:
                    act.wait_ge(S["u_zero"], 1)
                free(run(u_t[:, g, 16:16 + TP], out[:, :]), ("u", g))

            def u_tail(i, out):
                run(new_u[:, 2 * TS * i:2 * TS * i + 2 * TS], out[:, 0:2 * TS])
                free(run(u_t[:, 2 * i:2 * i + 2, 16 + TP:].rearrange("p a (b s) -> p a b s", b=DB)[:, :, :, SEG - DS:],
                         out[:, 0:2 * TS].rearrange("p (a b t) -> p a b t", a=2, b=DB)), ("uS", i))

            for i in range(2):
                pair("u", i, u_chunk, u_tail)
            pair("q", 0, q_chunk, q_tail)
            for g in range(NG):
                out = full(act, ("uo", g))
                run(near[64:128, 0, 128 * g:128 * g + 128], out[64:128, 0:128])
                free(run(near[0:TS, 0, 128 * g:128 * g + 128], out[0:TS, 128:256]), ("uo", g))
            for t in range(NT + 1):
                out = full(act, ("kout", t))
                free(stage_copy(out[0:rows_of(t), :], rows_of(t)), ("kout", t))
            pair("q", 1, q_chunk, q_tail)

            hi_until(AT[("v", 0)] + 3)
            for g in range(NG):
                act.wait_ge(S["pooled"], g + 1)
                src = u_t[:, g, :]
                if g >= 1:
                    full(act, ("pmS", g - 1))
                run(pt_hi[:, 0:TP], src[:, 16:16 + TP])
                run(pt_hi[:, TP:TP + TS].rearrange("p (b t) -> p b t", b=DB),
                    src[:, 16 + TP:].rearrange("p (b s) -> p b s", b=DB)[:, :, SEG - DS:]).then_inc(S["pool_hi"], 1)
                if g == 0:
                    act.wait_ge(S["half_done"], 1)
                for key, dst in ((("pm", g), act_hi[:, g, :]), (("pmS", g), act_s[:, g, 0:TS])):
                    out = full(act, key)
                    n = dst.shape[1]
                    run(dst, out[:, 0:n], scale=rows_t[:, 16 + g:17 + g]).then_inc(S["mixed_hi"], 1)
            hi_until(AT[("v", 1)] + 3)
            for t in range(NT):
                out = full(act, ("v", t))
                run(qiv_hi[:, t, :], out[:, :])
                stage_copy(out[:, :], 128).then_inc(S["v_staged"], 1)
            run(tmp_s[:, :], full(act, ("v", NT))[TS:2 * TS, :]).then_inc(S["v_low_rows"], 1)

            hi_until(AT[("poolw", 0)] + 3)

            for k in (staged[0], staged[0] + 1):
                act.wait_ge(stage_out[k % 2], 16 * (k // 2))
            for n in range(N_AT + 5):
                if n >= 5:
                    m = n - 5
                    t, h = m // H, m % H
                    out = full(act, ("pv", m))
                    r = slice(64 * (h % 2), 64 * (h % 2) + 64)
                    run(act_hi[r, 4 + h // 2, 128 * t:128 * t + 128], out[r, 0:128]).then_inc(S["o_hi"], 1)
                if n < N_AT:
                    L = 128 * (n // H + 1)
                    act.wait_ge(S["peaks"], n + 1)
                    run(probs[:, n % 3, 0:L], probs[:, n % 3, 0:L], ACT.Exp, bias=soft[:, n % 3, 1:2],
                        accum_out=soft[:, n % 3, 2:3]).then_inc(S["exps"], 1)
                if 2 <= n <= N_AT + 1:
                    m = n - 2
                    L = 128 * (m // H + 1)
                    out = full(act, ("pT", m))
                    if m >= 2:
                        full(act, ("pv", m - 2))
                    run(turned_probs(m)[0][:, 0:L], out[:, 0:L]).then_inc(S["pt_hi_ok"], 1)
                if 0 < n <= N_AT and n % 2 == 0:
                    modulation(FILL[n // 2 - 1])

            def keep_keys(b, c):
                out = full(act, ("KT", b, c))
                if b >= 2:
                    full(act, ("lgS", b // 2 - 1))
                free(run(k_t[:, b % 2, c, :], out[:, :]), ("KT", b, c))

            for b in range(2):
                keep_keys(b, 0), keep_keys(b, 2)
            for bp in range(4):
                if bp < 3:
                    keep_keys(2 * bp + 2, 0)
                act.wait_ge(S["peak_s"], bp + 1)
                run(rows[:, bp % 2, 0:LS], rows[:, bp % 2, 0:LS], ACT.Exp, bias=soft[:, bp % 2, 1:2],
                    accum_out=soft[:, bp % 2, 2:3]).then_inc(S["exp_s"], 1)
                if bp < 3:
                    keep_keys(2 * bp + 2, 2), keep_keys(2 * bp + 3, 0), keep_keys(2 * bp + 3, 2)
                out = full(act, ("pTS", bp))
                if bp >= 1:
                    full(act, ("pvS", bp - 1))
                free(run(p_t[:, 0:4, :], out[:, :].rearrange("p (g n) -> p g n", g=NPG)), ("pTS", bp))
                free(run(p_t[0:64, 4, :], full(act, ("pTSn", bp))[0:64, 0:128]), ("pTSn", bp))
                out = full(act, ("pvS", bp))
                for hh in range(2):
                    r = slice(64 * hh, 64 * hh + 64)
                    run(act_s[r, 4:8, 16 * bp:16 * bp + 16].rearrange("p c (b t) -> p b c t", b=2),
                        out[r, 0:128].rearrange("p (b c x t) -> p x b c t", b=2, c=4, x=2)[:, hh]).then_inc(S["os_hi"], 1)

            def keep_tokens(kind, f, nh, copy, low, last_piece):
                for t in range(NT):
                    if copy:
                        free(run(out_t[:, t, 512 * nh:512 * nh + 512], full(act, (kind, *f, nh, t))[:, :]), (kind, *f, nh, t))
                out = full(act, (kind, *f, nh, NT))
                if low >= 1:
                    prev = ("wo", 0, NT) if low == 1 else ("wo", 1, NT) if low == 2 else ("w2", (low - 3) // 2, (low - 3) % 2, NT)
                    evacuated(act, prev)
                run(half_s[:, :], out[TS:2 * TS, :]).then_inc(S["low_rows"], 1)
                hi_until(last_piece + 3)

            hi_until(AT[("wo", 0)] + 3)
            keep_tokens("wo", (), 0, True, 0, AT[("wo", 1)])
            hi_until(AT[("wo", 2)] + 3)
            for j in range(NT + 2):
                if j < NT:
                    free(run(out_t[:, j, 512:D], full(act, ("wo", 1, j))[:, :]), ("wo", 1, j))
                elif j == NT:
                    out = full(act, ("wo", 1, NT))
                    evacuated(act, ("wo", 0, NT))
                    run(half_s[:, :], out[TS:2 * TS, :]).then_inc(S["low_rows"], 1)
                if j <= NT:
                    evacuated(act, ("wo", 1, j))
                    square(1, j, out_t)
                if j >= 1:
                    act.wait_ge(S["residual"], j)
                    square(2, j - 1, x_res)
                if j <= NT:
                    root(1, j)
                if j >= 1:
                    root(2, j - 1)
            hi_until(AT[("wo", 3)] + 3)
            turned_hidden(1)

            for f in range(QF):
                for i in range(4):
                    p = 4 * f + i
                    for n in (2 * p, 2 * p + 1):
                        out = full(act, ("w1", n))
                        if n >= 2:
                            act.wait_ge(S["w1_done"], n - 1)
                        free(run(stage[:, n % 2, :], out[:, :], ACT.Relu), ("w1", n))
                    for n in (2 * p, 2 * p + 1):
                        act.wait_ge(S["w1_squared"], n + 1)
                        run(hid_hi[:, n % 8, :], stage[:, n % 2, :]).then_inc(S["w1_hi"], 1)
                    hi_until(AT[("w1", p)] + 3)
                    free(run(halves_mlp[:, :], full(act, ("w1R", p))[:, :]), ("w1R", p))
                    out = full(act, ("w1S", p))
                    if p >= 2:
                        act.wait_ge(S["w1s_done"], p - 1)
                    st = stage_s[:, 2 * (p % 2):2 * (p % 2) + 2, :]
                    free(run(st, out[:, 0:2 * TS].rearrange("p (a n) -> p a n", a=2), ACT.Relu), ("w1S", p))
                    act.wait_ge(S["w1s_squared"], p + 1)
                    run(hid_s[:, 2 * i:2 * i + 2, 0:TS], st).then_inc(S["w1s_hi"], 1)
                for nh in range(2):
                    hi_until(AT[("w2", 4 * f + 2 * nh)] + 3)
                    if f < QF - 1 or nh == 0:
                        keep_tokens("w2", (f,), nh, f == 0, 2 + 2 * f + nh, AT[("w2", 4 * f + 2 * nh + 1)])
            act.wait_ge(S["w1_done"], 2 * DFF // 256)
            for t in range(NT):
                evacuated(act, ("w2", QF - 1, 1, t))
                square(3, t, out_t)
                root(3, t)
            keep_tokens("w2", (QF - 1,), 1, False, 1 + 2 * QF, 0)
            evacuated(act, ("w2", QF - 1, 1, NT))
            square(3, NT, out_t)
            root(3, NT)

        @block.vector
        def _(dve):
            link = Chain(dve, dve_chain)
            split = [0]

            def lo_until(n):
                while split[0] < min(n, len(PIECES)):
                    m = split[0]
                    c, cols = piece_shape(PIECES[m][0])
                    hi, lo, _ = parts_of(m)
                    dve.wait_ge(hi_ready, m + 1)
                    nc.vector.tensor_tensor(lo, raw[:, m % NRAW, 0:c * cols].rearrange("p (c n) -> p c n", c=c),
                                            hi.bitcast(F32), ALU.subtract).then_inc(lo_ready, 1)
                    split[0] += 1

            def minus(out, x, hi):
                return nc.vector.tensor_tensor(out, x, hi.bitcast(F32), ALU.subtract)

            def scaled_minus(out, x, scale, hi):
                return nc.vector.scalar_tensor_tensor(out, x, scale, hi.bitcast(F32), ALU.mult, ALU.subtract)

            nc.vector.memset(c_split[:].bitcast(F32), 0.0).then_inc(S["pad_zero2"], 1)
            nc.vector.memset(zero1, 0.0)
            out = full(dve, "cT")
            dve.wait_ge(S["c_hi"], 1)
            dve.wait_ge(S["pad_zero2"], 1)
            ins = minus(c_split[:, :, 32:41], out[:, 0:72].rearrange("p (c m) -> p c m", m=9), c_split[:, :, 0:9])
            free(ins, "cT")
            lo_until(2)

            def mean(k, t):
                x, r = (NT + 1) * k + t, rows_of(t)
                dve.wait_ge(S["squares"], NORM[k, t] + 1)
                nc.vector.tensor_scalar(ss[0:r, x:x + 1], ss[0:r, x:x + 1], 1.0 / D, EPS, ALU.mult, ALU.add)\
                    .then_inc(S["mean_ok"], 1)

            def rstd_of(k, t):
                x, r = (NT + 1) * k + t, rows_of(t)
                dve.wait_ge(S["root_ok"], NORM[k, t] + 1)
                link(nc.vector.reciprocal(rstd[0:r, x:x + 1], rstd[0:r, x:x + 1]))
                return rstd[0:r, x:x + 1]

            def normalise(k, t, dst, src):
                r = rows_of(t)
                nc.vector.tensor_scalar(dst[0:r, t, :], src[0:r, t, :], rstd_of(k, t), None, ALU.mult)\
                    .then_inc(S["normed"], 1)

            for t in range(NT + 1):
                mean(0, t)
            for t in range(NT + 1):
                normalise(0, t, x_nrm, x_in)
            for i in range(8):
                lo_until(i + 3)

            def turned_hidden(k):
                out = full(dve, ("modT", k))
                m = mod_t[:, 16 * k:16 * k + 16, :]
                evacuated(dve, "rowsT")
                free(nc.vector.tensor_copy(m, out[:, 0:144].rearrange("p (j m) -> p j m", m=9)), ("modT", k))
                evacuated(dve, ("modT", k))
                gain = rows_t[:, 8 * k:8 * k + 8].unsqueeze(2).to_broadcast([128, 8, 9])
                nc.vector.scalar_tensor_tensor(m[:, 8:16, :], m[:, 8:16, :], 1.0, gain, ALU.add, ALU.mult)\
                    .then_inc(S["mod_ok"], 2)
                dve.wait_ge(S["mod_ok"], 2 * (k + 1))

            def split_hidden(k):
                for kc in range(KC):
                    dve.wait_ge(S["h_hi"], k * KC + kc + 1)
                    minus(act_lo[:, kc, :], stage[:, kc % 2, :], act_hi[:, kc, :]).then_inc(S["h_low"], 1)
                out = full(dve, ("hTS", k))
                m = mod_t[:, 16 * k:16 * k + 16, 1:9]
                dims = [128, KC, DB, DS]
                shape = dict(b=DB)
                st = stage_s[:, :, :].rearrange("p c (b t) -> p c b t", b=DB)
                free(nc.vector.tensor_tensor(st, out[:, :].rearrange("p (c b t) -> p c b t", c=KC, b=DB),
                                             m[:, 8:16, :].unsqueeze(3).to_broadcast(dims), ALU.mult), ("hTS", k))
                evacuated(dve, ("hTS", k))
                nc.vector.tensor_tensor(st, st, m[:, 0:8, :].unsqueeze(3).to_broadcast(dims), ALU.add)\
                    .then_inc(S["hs_staged"], 1)
                dve.wait_ge(S["hs_staged"], k + 1)
                dve.wait_ge(S["hs_hi"], k + 1)
                minus(act_s[:, :, TS:2 * TS], stage_s[:, :, :], act_s[:, :, 0:TS]).then_inc(S["hs_lo"], 1)

            turned_hidden(0)
            split_hidden(0)

            for i in range(2):
                for c in (2 * i, 2 * i + 1):
                    dve.wait_ge(S["proj_hi"], c + 1)
                    free(minus(qiv_lo[:, c, :], full(dve, ("qi", c))[:, :], qiv_hi[:, c, :]), ("qi", c))
                lo_until(AT[("qi", i)] + 3)
            dve.wait_ge(S["proj_hi"], 5)
            free(minus(ki_lo[:, :], full(dve, "ki")[:, :], ki_hi[:, :]), "ki")
            lo_until(AT[("kiwi", 0)] + 3)
            evacuated(dve, "kiwi")
            nc.vector.tensor_scalar(wi[:, 0:NT, :], kiwi[:, 0:NT, 64:72], H ** -0.5, None, ALU.mult)
            nc.vector.tensor_scalar(wi[0:TS, NT, :], kiwi[0:TS, NT, 64:72], H ** -0.5, None, ALU.mult).then_inc(S["wi_ok"], 1)
            dve.wait_ge(S["wi_ok"], 1)
            out = full(dve, "wiR")
            dve.wait_ge(S["pad_zero"], 1)
            w0 = wi_b[:, :, 0:DS]
            diag = bass.AP(tensor=w0.tensor, offset=w0.offset, ap=[list(w0.ap[0]), [64 + DS, DB], [1, DS]])
            free(nc.vector.tensor_tensor(diag, out[0:64, 0:TS].rearrange("p (b t) -> p b t", b=DB),
                                         cc("step", 64).rearrange("p (b t) -> p b t", b=DB), ALU.mult), "wiR")

            for t in range(1, NT):
                L = 128 * (t + 1)
                for h in range(H):
                    n = (t - 1) * H + h
                    evacuated(dve, ("ix", t, h))
                    r = rows[:, n % 2, 0:L]
                    if h == 0:
                        ins = nc.vector.tensor_scalar(score[t][:, 0:L], r, wi[:, t, h:h + 1], 0.0, ALU.mult, ALU.add)
                    else:
                        ins = nc.vector.scalar_tensor_tensor(score[t][:, 0:L], r, wi[:, t, h:h + 1], score[t][:, 0:L],
                                                             ALU.mult, ALU.add)
                    ins.then_inc(S["relu_added"], 1)
                    dve.wait_ge(S["relu_added"], n + 1)
                link(nc.vector.tensor_tensor(score[t][:, L - 128:L], score[t][:, L - 128:L], cc("causal"), ALU.add))
            free(nc.vector.tensor_copy(score_s[:, 0:PAST], full(dve, "scS")[0:TS, :]), "scS")
            free(nc.vector.tensor_tensor(score_s[:, PAST:LS], full(dve, "scSn")[0:TS, 0:DS], cc("newmask", TS), ALU.add), "scSn")
            evacuated(dve, "scS")
            evacuated(dve, "scSn")

            def choose(buf, n_sel):
                r = buf.shape[0]
                for left in range(n_sel, 0, -8):
                    link(nc.vector.max(top8[0:r, :], buf))
                    if left < 8:
                        link(nc.vector.memset(top8[0:r, left:8], TAKEN))
                    link(nc.vector.match_replace(buf, top8[0:r, :], buf, TAKEN))
                    yield
                nc.vector.tensor_scalar(buf, buf, TAKEN, NEG, ALU.not_equal, ALU.mult).then_inc(S["chosen"], 1)
                yield

            def all_choices():
                for t in range(1, NT):
                    yield from choose(score[t][:, :], SEL_P)
                yield from choose(score_s[:, :], SEL_S)

            rounds = all_choices()

            def some_rounds(n):
                for _ in range(n):
                    next(rounds, None)

            def k_pair(i):
                for c in (2 * i, 2 * i + 1):
                    dve.wait_ge(S["proj_hi"], 6 + c)
                    free(minus(k_lo[:, c, :], full(dve, ("k", c))[:, :], k_hi[:, c, :]), ("k", c))
                    some_rounds(4)
                lo_until(AT[("k", i)] + 3)

            def q_pair(i):
                for c in (2 * i, 2 * i + 1):
                    dve.wait_ge(S["proj_hi"], 10 + c)
                    free(scaled_minus(q_lo[:, c, :], full(dve, ("q", c))[:, :], HD ** -0.5, q_hi[:, c, :]), ("q", c))
                    some_rounds(4)
                lo_until(AT[("q", i)] + 3)

            for i in range(2):
                k_pair(i)
            for i in range(2):
                lo_until(AT[("u", i)] + 3)
                some_rounds(9)
            q_pair(0)
            for g in range(NG):
                sums, u = rows[:, g % 2, :], u_t[:, g, :]
                full(dve, ("uo", g))
                dve.wait_ge(S["window_sums"], g + 1)
                link(nc.vector.tensor_tensor(sums[:, 16:32], sums[:, 16:32], cc("invcnt")[:, 16 * g:16 * g + 16], ALU.mult))
                nc.vector.tensor_tensor(u[:, 16:32], sums[:, 16:32], u[:, 16:32], ALU.subtract)
                nc.vector.scalar_tensor_tensor(u[:, 32:UW], sums[:, 32:UW], 1.0 / WINDOWS[g], u[:, 32:UW],
                                               ALU.mult, ALU.subtract).then_inc(S["pooled"], 1)
            q_pair(1)
            some_rounds(7)
            lo_until(AT[("v", 0)] + 3)
            for g in range(NG):
                dve.wait_ge(S["pool_hi"], g + 1)
                src = u_t[:, g, :]
                minus(pt_lo[:, 0:TP], src[:, 16:16 + TP], pt_hi[:, 0:TP])
                minus(pt_lo[:, TP:TP + TS].rearrange("p (b t) -> p b t", b=DB),
                      src[:, 16 + TP:].rearrange("p (b s) -> p b s", b=DB)[:, :, SEG - DS:],
                      pt_hi[:, TP:TP + TS].rearrange("p (b t) -> p b t", b=DB)).then_inc(S["pool_lo"], 1)
                sc = rows_t[:, 16 + g:17 + g]
                dve.wait_ge(S["mixed_hi"], 2 * g + 1)
                free(scaled_minus(act_lo[:, g, :], full(dve, ("pm", g))[:, :], sc, act_hi[:, g, :]), ("pm", g))
                dve.wait_ge(S["mixed_hi"], 2 * g + 2)
                free(scaled_minus(act_s[:, g, TS:2 * TS], full(dve, ("pmS", g))[:, 0:TS], sc, act_s[:, g, 0:TS]), ("pmS", g))
            lo_until(AT[("v", 1)] + 3)
            for t in range(NT):
                dve.wait_ge(S["v_staged"], t + 1)
                free(minus(qiv_lo[:, t, :], full(dve, ("v", t))[:, :], qiv_hi[:, t, :]), ("v", t))
            dve.wait_ge(S["v_low_rows"], 1)
            free(nc.vector.tensor_tensor(v_s[:, :], full(dve, ("v", NT))[0:TS, :], tmp_s[:, :], ALU.add), ("v", NT))
            lo_until(AT[("poolw", 0)] + 3)
            for n in range(N_AT + 5):
                if n == 18:
                    turned_hidden(1)
                if n < N_AT:
                    L = 128 * (n // H + 1)
                    out = full(dve, ("lg", n))
                    dve.wait_ge(S["near_ok"], n + 1)
                    if n >= 3:
                        full(dve, ("pT", n - 3))
                    free(nc.vector.tensor_tensor_reduce(probs[:, n % 3, 0:L], out[:, 0:L], near[:, n % 2, 0:L], 1.0, TAKEN,
                                                        ALU.add, ALU.max, soft[:, n % 3, 0:1]), ("lg", n))
                    evacuated(dve, ("lg", n))
                    nc.vector.tensor_scalar(soft[:, n % 3, 1:2], soft[:, n % 3, 0:1], -1.0, None, ALU.mult)\
                        .then_inc(S["peaks"], 1)
                if 3 <= n <= N_AT + 2:
                    m = n - 3
                    L = 128 * (m // H + 1)
                    dve.wait_ge(S["pt_hi_ok"], m + 1)
                    ph, pl = turned_probs(m)
                    free(minus(pl[:, 0:L], full(dve, ("pT", m))[:, 0:L], ph[:, 0:L]), ("pT", m))
                if 1 <= n <= N_AT:
                    m = n - 1
                    L = 128 * (m // H + 1)
                    dve.wait_ge(S["exps"], m + 1)
                    link(nc.vector.reciprocal(soft[:, m % 3, 3:4], soft[:, m % 3, 2:3]))
                    nc.vector.tensor_scalar(probs[:, m % 3, 0:L], probs[:, m % 3, 0:L], soft[:, m % 3, 3:4], None,
                                            ALU.mult).then_inc(S["probs_ok"], 1)
                if n >= 5:
                    m = n - 5
                    t, h = m // H, m % H
                    r = slice(64 * (h % 2), 64 * (h % 2) + 64)
                    tok = slice(128 * t, 128 * t + 128)
                    dve.wait_ge(S["o_hi"], m + 1)
                    free(minus(act_lo[r, 4 + h // 2, tok], full(dve, ("pv", m))[r, 0:128], act_hi[r, 4 + h // 2, tok]), ("pv", m))
                if 3 <= n <= N_AT + 1 and n % 2 == 1:
                    lo_until(AT[("ada", FILL[n // 2 - 1])] + 3)
                elif n < N_AT:
                    some_rounds(2)
            evacuated(dve, "toepS")
            def keep_keys(b):
                for c in (1, 3):
                    out = full(dve, ("KT", b, c))
                    if b >= 2:
                        full(dve, ("lgS", b // 2 - 1))
                    free(nc.vector.tensor_copy(k_t[:, b % 2, c, :], out[:, :]), ("KT", b, c))

            keep_keys(0)
            keep_keys(1)
            for bp in range(4):
                out = full(dve, ("lgS", bp))
                s = soft[:, bp % 2, :]
                if bp >= 2:
                    full(dve, ("pTSn", bp - 2))
                far = LS - 136
                link(nc.vector.tensor_tensor_reduce(rows[:, bp % 2, 0:far], out[:, 0:far], zero1[:, :].to_broadcast([128, far]),
                                                    1.0, TAKEN, ALU.add, ALU.max, s[:, 2:3]))
                free(nc.vector.tensor_tensor_reduce(rows[:, bp % 2, far:PAST], out[:, far:PAST], toep_s[:, 0:PAST - far],
                                                    1.0, s[:, 2:3], ALU.add, ALU.max, s[:, 3:4]), ("lgS", bp))
                evacuated(dve, ("lgS", bp))
                free(nc.vector.tensor_tensor_reduce(rows[:, bp % 2, PAST:LS], full(dve, ("lgSn", bp))[:, 0:DS],
                                                    toep_s[:, PAST - far:136], 1.0, s[:, 3:4], ALU.add, ALU.max, s[:, 0:1]), ("lgSn", bp))
                evacuated(dve, ("lgSn", bp))
                nc.vector.tensor_scalar(s[:, 1:2], s[:, 0:1], -1.0, None, ALU.mult).then_inc(S["peak_s"], 1)
                if bp < 3:
                    keep_keys(2 * bp + 2)
                dve.wait_ge(S["exp_s"], bp + 1)
                link(nc.vector.reciprocal(s[:, 3:4], s[:, 2:3]))
                link(nc.vector.tensor_scalar(rows[:, bp % 2, 0:LS], rows[:, bp % 2, 0:LS], s[:, 3:4], None, ALU.mult))
                if bp >= 1:
                    full(dve, ("pTSn", bp - 1))
                nc.vector.tensor_tensor(p_new[:, :].rearrange("p (b t) -> p b t", b=DB),
                                        rows[:, bp % 2, PAST:LS].unsqueeze(1).to_broadcast([128, DB, DS]),
                                        cc("own")[:, DB * bp:DB * bp + DB].unsqueeze(2).to_broadcast([128, DB, DS]),
                                        ALU.mult).then_inc(S["prob_new"], 1)
                if bp < 3:
                    keep_keys(2 * bp + 3)
                out = full(dve, ("pvS", bp))
                for hh in range(2):
                    r = slice(64 * hh, 64 * hh + 64)
                    dve.wait_ge(S["os_hi"], 2 * bp + 2)
                    ins = minus(act_s[r, 4:8, TS + 16 * bp:TS + 16 * bp + 16].rearrange("p c (b t) -> p b c t", b=2),
                                out[r, 0:128].rearrange("p (b c x t) -> p x b c t", b=2, c=4, x=2)[:, hh],
                                act_s[r, 4:8, 16 * bp:16 * bp + 16].rearrange("p c (b t) -> p b c t", b=2))
                free(ins, ("pvS", bp))

            def gates(k):
                dve.wait_ge(S["gain_in"], 16 * (k + 1))
                for j in range(2):
                    s = slice(512 * j, 512 * j + 512)
                    free(nc.vector.tensor_tensor(gate_p[:, s], full(dve, ("gP", k, j))[:, :], ln_post[:, s], ALU.mult), ("gP", k, j))
                    free(nc.vector.tensor_tensor(gate_s[:, s], full(dve, ("gS", k, j))[0:TS, :], ln_post[0:TS, s], ALU.mult), ("gS", k, j))
                evacuated(dve, ("gP", k, 1))
                evacuated(dve, ("gS", k, 1))

            gates(0)
            def gated(k, t, signal):
                r = rows_of(t)
                gate = gate_p if t < NT else gate_s
                link(nc.vector.scalar_tensor_tensor(out_t[0:r, t, :], out_t[0:r, t, :], rstd_of(k, t),
                                                    gate[0:r, :], ALU.mult, ALU.mult))
                nc.vector.tensor_tensor(x_res[0:r, t, :], x_res[0:r, t, :], out_t[0:r, t, :], ALU.add)\
                    .then_inc(S[signal], 1)

            def sum_rows(nh):
                s = slice(512 * nh, 512 * nh + 512)
                dve.wait_ge(S["low_rows"], nh + 1)
                free(nc.vector.tensor_tensor(out_t[0:TS, NT, s], full(dve, ("wo", nh, NT))[0:TS, :], half_s[:, :], ALU.add),
                     ("wo", nh, NT))

            lo_until(AT[("wo", 0)] + 3)
            sum_rows(0)
            lo_until(AT[("wo", 2)] + 3)
            dve.wait_ge(S["x_again"], 32)
            for j in range(NT + 2):
                if j == NT:
                    sum_rows(1)
                if j <= NT:
                    mean(1, j)
                if j >= 1:
                    mean(2, j - 1)
                if j <= NT:
                    gated(1, j, "residual")
                if j >= 1:
                    normalise(2, j - 1, out_t, x_res)
            lo_until(AT[("wo", 3)] + 3)
            split_hidden(1)
            gates(1)

            for f in range(QF):
                for i in range(4):
                    p = 4 * f + i
                    for n in (2 * p, 2 * p + 1):
                        evacuated(dve, ("w1", n))
                        nc.vector.tensor_tensor(stage[:, n % 2, :], stage[:, n % 2, :], stage[:, n % 2, :], ALU.mult)\
                            .then_inc(S["w1_squared"], 1)
                        dve.wait_ge(S["w1_squared"], n + 1)
                    for n in (2 * p, 2 * p + 1):
                        dve.wait_ge(S["w1_hi"], n + 1)
                        minus(hid_lo[:, n % 8, :], stage[:, n % 2, :], hid_hi[:, n % 8, :]).then_inc(S["w1_done"], 1)
                    lo_until(AT[("w1", p)] + 3)
                    evacuated(dve, ("w1S", p))
                    st = stage_s[:, 2 * (p % 2):2 * (p % 2) + 2, :]
                    nc.vector.tensor_tensor(st, st, st, ALU.mult).then_inc(S["w1s_squared"], 1)
                    dve.wait_ge(S["w1s_squared"], p + 1)
                    dve.wait_ge(S["w1s_hi"], p + 1)
                    minus(hid_s[:, 2 * i:2 * i + 2, TS:2 * TS], st, hid_s[:, 2 * i:2 * i + 2, 0:TS]).then_inc(S["w1s_done"], 1)
                for nh in range(2):
                    s = slice(512 * nh, 512 * nh + 512)
                    lo_until(AT[("w2", 4 * f + 2 * nh)] + 3)
                    last = f == QF - 1 and nh == 1
                    if f:
                        for t in range(NT):
                            if t and last:
                                mean(3, t - 1)
                            free(nc.vector.tensor_tensor(out_t[:, t, s], full(dve, ("w2", f, nh, t))[:, :], out_t[:, t, s],
                                                         ALU.add), ("w2", f, nh, t))
                            if t and last:
                                gated(3, t - 1, "y_ok")
                    if last:
                        mean(3, NT - 1)
                        gated(3, NT - 1, "y_ok")
                    dve.wait_ge(S["low_rows"], 3 + 2 * f + nh)
                    y = out_t[0:TS, NT, s]
                    if f:
                        link(nc.vector.tensor_tensor(y, y, half_s[:, :], ALU.add))
                        free(nc.vector.tensor_tensor(y, full(dve, ("w2", f, nh, NT))[0:TS, :], y, ALU.add), ("w2", f, nh, NT))
                    else:
                        free(nc.vector.tensor_tensor(y, full(dve, ("w2", f, nh, NT))[0:TS, :], half_s[:, :], ALU.add),
                             ("w2", f, nh, NT))
                    lo_until(AT[("w2", 4 * f + 2 * nh + 1)] + 3)
            mean(3, NT)
            gated(3, NT, "y_ok")


_OUTS = [("y_p", (1, TP, D)), ("y_s", (DB, DS, D)),
         ("k_p", (1, 1, TP, H, HD)), ("v_p", (1, 1, TP, H, HD)), ("kidx_p", (1, 1, TP, HD)), ("pool_p", (1, 1, HIST, CP_)),
         ("k_s", (1, DB, DS, H, HD)), ("v_s", (1, DB, DS, H, HD)), ("kidx_s", (1, DB, DS, HD)), ("pool_s", (1, DB, HIST, CP_))]


def kernel(**inputs):
    import concourse.bacc as bacc
    from concourse.bass_utils import run_bass_kernel_spmd

    nc = bacc.Bacc("TRN2", target_bir_lowering=False, num_devices=1)
    consts, spans = constants()
    given = {name: np.ascontiguousarray(value) for name, value in inputs.items()}
    given["consts"] = consts
    arrays, a, o = {}, {}, {}
    for name, value in given.items():
        arrays[f"in_{name}"] = value
        a[name] = nc.dram_tensor(f"in_{name}", value.shape, mybir.dt.from_np(value.dtype), kind="ExternalInput").ap()
    for name, shape in _OUTS:
        o[name] = nc.dram_tensor(f"out_{name}", shape, F32, kind="ExternalOutput").ap()
    build_program(nc, a, o, spans)
    r = run_bass_kernel_spmd(nc, [arrays], core_ids=[0])
    return tuple(r.results[0][f"out_{name}"] for name, _ in _OUTS)
```

```python
from contextlib import ExitStack

import numpy as np
import concourse.bass as bass
from concourse import mybir

F32 = mybir.dt.float32
F32R = mybir.dt.float32r
I32 = mybir.dt.int32
ALU = mybir.AluOpType
ACT = mybir.ActivationFunctionType
AX_X = mybir.AxisListType.X

D = 1024
KC = D // 128
TP = 512
NT = TP // 128
DB, DS = 8, 8
TS = DB * DS
PAST, PAGE = 512, 128
NPG = PAST // PAGE
H, HD = 8, 64
CP_ = 512
NG = 4
WINDOWS = (2, 4, 8, 16)
HIST = 15
NB, MAXD = 32, 128
DFF = 4096
D_IN = 4 * 512 + 512 + 64 + 8
OFF_Q, OFF_K, OFF_V, OFF_QI, OFF_KI, OFF_WI = 512, 1024, 1536, 2048, 2560, 2624
SEL_P = min(256, TP // 4)
SEL_S = min(256, (PAST + DS) // 4)
LS = PAST + DS
EPS = 1e-6
NEG = -(2.0 ** 100)
TAKEN = -3.0e38
NRAW, NSPLIT = 2, 2
LAG = 2
EARLY = 4
QF = 4
SEG = 1 + HIST + DS
UW = 16 + TP + DB * SEG


def t5_bucket(n):
    n = np.maximum(n, 0)
    exact = NB // 2
    large = exact + (np.log(np.maximum(n, 1).astype(np.float32) / exact)
                     / np.log(MAXD / exact) * (NB - exact)).astype(np.int32)
    return np.where(n < exact, n, np.minimum(large, NB - 1))


def constants():
    parts = {}
    r = np.arange(128)
    parts["ident"] = np.eye(128)
    parts["flip"] = np.eye(128)[::-1]
    parts["causal"] = np.where(r[None, :] > r[:, None], NEG, 0.0)
    onehot = np.zeros((128, 384))
    x = np.arange(384)
    onehot[t5_bucket(255 - x), x] += 1.0
    onehot[NB - 1, :] -= 1.0
    parts["bucket"] = onehot
    unflip = np.zeros((128, 128))
    for b2 in range(2):
        for h in range(H):
            for t in range(DS):
                unflip[h * DS + (DS - 1 - t), b2 * 64 + h * DS + t] = 1.0
    parts["unflip"] = unflip
    own = np.zeros((128, 4, DB))
    for bp in range(4):
        for b2 in range(2):
            own[64 * b2:64 * b2 + 64, bp, 2 * bp + b2] = 1.0
    parts["own"] = own.reshape(128, 4 * DB)
    sel_t = np.zeros((128, 9)); sel_p = np.zeros((128, 128)); sel_s = np.zeros((128, 64))
    for m in range(9):
        sel_t[m, m] = sel_t[32 + m, m] = 1.0
    sel_t[41, :] = 1.0
    sel_p[[0, 32, 41], :] = 1.0
    for b in range(DB):
        sel_s[[1 + b, 33 + b], b * DS:(b + 1) * DS] = 1.0
    sel_s[41, :] = 1.0
    parts["sel_t"], parts["sel_p"], parts["sel_s"] = sel_t, sel_p, sel_s
    parts["fold"] = np.concatenate([np.eye(TS), np.eye(TS)])
    heads = np.zeros((128, 64)); step = np.zeros((128, 64))
    for h in range(H):
        heads[h, h * DS:(h + 1) * DS] = 1.0
        for t in range(DS):
            step[h * DS + t, t::DS] = 1.0
    parts["heads"], parts["step"] = heads, step
    inv = np.zeros((128, 4, 16))
    for g, w in enumerate(WINDOWS):
        inv[:, g, :] = 1.0 / np.minimum(np.arange(16) + 1, w)
    parts["invcnt"] = inv.reshape(128, 64)
    new = np.zeros((128, 8))
    for b in range(DB):
        for t in range(DS):
            new[b * DS + t, t + 1:] = NEG
    parts["newmask"] = new
    at, spans = 0, {}
    for k, v in parts.items():
        spans[k] = (at, at + v.shape[1])
        at += v.shape[1]
    return np.concatenate(list(parts.values()), axis=1).astype(np.float32), spans


FILL = [*range(12, 20), *range(8, 12), *range(20, 24)]


def plan_pieces():
    p = [("ada", i) for i in range(8)]
    p += [("qi", 0), ("qi", 1), ("kiwi", 0), ("k", 0), ("k", 1), ("u", 0), ("u", 1)]
    p += [("q", 0), ("q", 1), ("v", 0), ("v", 1), ("poolw", 0)]
    p += [("ada", i) for i in FILL]
    p += [("wo", i) for i in range(4)]
    for f in range(QF):
        p += [("w1", 4 * f + i) for i in range(4)] + [("w2", 4 * f + i) for i in range(4)]
    return p


PIECES = plan_pieces()
AT = {key: n for n, key in enumerate(PIECES)}
COL0 = {"qi": OFF_QI, "k": OFF_K, "q": OFF_Q, "u": 0}
ADA_ROW = {i: (i if i < 8 else i - 12 if 12 <= i < 20 else i - 8 if i < 12 else i - 16) for i in range(24)}


def piece_shape(kind):
    if kind in ("ada", "v", "wo", "w2"):
        return 4, 512
    return {"kiwi": (KC, 136), "poolw": (NG, 128)}.get(kind, (KC, 256))


def plan_norms():
    order = [(0, t) for t in range(NT + 1)]
    for j in range(NT + 1 + LAG):
        order += [(1, j)] * (j <= NT) + [(2, j - LAG)] * (j >= LAG)
    order += [(3, t) for t in range(NT + 1)]
    return {key: n for n, key in enumerate(order)}


NORM = plan_norms()


def plan_banks():
    use, count = {}, [0] * 8

    def take(key, bank):
        count[bank] += 1
        use[key] = (bank, count[bank])

    take("cT", 3)
    take("rowsT", 4)
    for i in range(1, 8, 2):
        take(("ada", i), i // 2 % 2)
    take(("modT", 0), 3)
    for kc in range(KC):
        take(("hT", 0, kc), 3 + kc % 3)
    take(("hTS", 0), 6)
    for i in range(2):
        take(("qi", 2 * i), 0), take(("qi", 2 * i + 1), 1), take(("qiR", i), 2), take(("qiS", i), 2)
    take("ki", 0), take("kw", 1), take("kiR", 2), take("kiS", 3), take("kiwi", 4)
    take("wiT", 4), take("wiR", 5)
    take("biasrow", 6)
    for j in range(4):
        take(("toep", j), 6 + j % 2)
    take("toepS", 6)
    for t in range(1, NT):
        for h in range(H):
            take(("ix", t, h), 3 + h % 2)
    for b in range(DB):
        take(("kxT", b), 5)
        take(("ixS", b), 6), take(("ixSn", b), 7)
        if b == 0:
            take("scS", 3), take("scSn", 4)
    take("hist", 5)
    for kind in ("k", "u", "q"):
        for i in range(2):
            take((kind, 2 * i), 0), take((kind, 2 * i + 1), 1), take((kind + "R", i), 2), take((kind + "S", i), 2)
            if kind == "u":
                for g in (2 * i, 2 * i + 1):
                    take(("uo", g), 3 + g % 2)
        if kind == "k":
            for t in range(NT + 1):
                take(("kout", t), 5 + t % 2)
    for t in range(NT + 1):
        take(("v", t), 3 + t)
    for g in range(NG):
        take(("pm", g), g % 2), take(("pmS", g), 2)
    for n in range(NT * H + 4):
        if n < NT * H:
            take(("lg", n), 3 + n % 2)
        if n >= 5 and n % 2 == 1:
            take(("pv", (n - 5) // 2), 6 + n // 2 % 2)
        if 2 <= n <= NT * H + 1:
            take(("pT", n - 2), 5 if n % 2 else 2)
        if n >= 2 and n % 4 == 0 and n <= NT * H:
            take(("ada", FILL[n // 2 - 1]), n // 4 % 2)
        if n == 17:
            take(("modT", 1), 2)
    for b in range(DB):
        for c in range(4):
            take(("KT", b, c), (4 * b + c) % 3)
    for bp in range(4):
        take(("lgS", bp), 3), take(("lgSn", bp), 4)
        take(("pTS", bp), 5), take(("pTSn", bp), 6)
        take(("pvR", bp), 7), take(("pvS", bp), 6)
    for j in range(2):
        take(("gP", 0, j), j), take(("gS", 0, j), 2 + 5 * j)
    for nh in range(2):
        for t in range(NT + 1):
            take(("wo", nh, t), 3 + t)
    for kc in range(KC):
        take(("hT", 1, kc), 3 + kc % 3)
    take(("hTS", 1), 6)
    for j in range(2):
        take(("gP", 1, j), 3 + 2 * j), take(("gS", 1, j), 4 + 2 * j)
    for f in range(QF):
        for i in range(4):
            take(("w1", 8 * f + 2 * i), 0), take(("w1", 8 * f + 2 * i + 1), 1)
            take(("w1R", 4 * f + i), 2), take(("w1S", 4 * f + i), 2)
        for nh in range(2):
            for t in range(NT + 1):
                take(("w2", f, nh, t), 3 + t)
    return use


USE = plan_banks()


def raw_slot(n):
    return n % EARLY if n < 8 else n % NRAW


def last_use(kind, i):
    if kind in ("qi", "k", "q", "u", "w1"):
        return (kind + "R", i)
    return {"ada": ("ada", i), "kiwi": "kiR", "v": ("v", NT), "poolw": ("pmS", NG - 1)}.get(kind) or {
        "wo": ("wo", i // 2, NT), "w2": ("w2", i // 4, i % 4 // 2, NT)}[kind]


def build_program(nc, a, o, spans):
    ctx = ExitStack()
    with ctx:
        def sem(name):
            return ctx.enter_context(nc.semaphore(name))

        psum = [ctx.enter_context(nc.psum_tensor(f"bank{i}", [128, 512], F32)) for i in range(8)]

        def sb(name, shape, dt=F32, stack=ctx):
            return stack.enter_context(nc.sbuf_tensor(name, shape, dt))

        cst = sb("cst", [128, spans["newmask"][1]])
        raw = sb("raw", [128, NRAW, 2048])
        w_split = sb("w_split", [128, NSPLIT, 4096], F32R)
        act_hi = sb("act_hi", [128, KC, TP], F32R)
        act_lo = sb("act_lo", [128, KC, TP], F32R)
        act_s = sb("act_s", [128, KC, 2 * TS], F32R)
        mod_rows = sb("mod_rows", [42, 2048])
        mod_t = sb("mod_t", [128, 4 * KC, 9])
        over = ExitStack()
        turned_hi = sb("turned_hi", [128, 3, TP], F32R, over)
        over.close()
        stage = sb("stage", [128, 2, TP])
        stage_s = sb("stage_s", [128, KC, TS])
        c_split = sb("c_split", [128, KC, 72], F32R)
        rows_t = sb("rows_t", [128, 20])
        ss = sb("ss", [128, 4 * (NT + 1)])
        rstd = sb("rstd", [128, 4 * (NT + 1)])

        def cc(name, rows=128):
            x, y = spans[name]
            return cst[0:rows, x:y]

        dram_bias = nc.dram_tensor("bias_rows", (H, 384), F32, kind="Internal").ap()

        mix = ExitStack()
        head = ExitStack()
        x_in = sb("x_in", [128, NT + 1, D], stack=head)
        x_nrm = sb("x_nrm", [128, NT + 1, D], stack=head)
        c_in = sb("c_in", [9, D], stack=head)
        rows_in = sb("rows_in", [20, 128], stack=head)
        head.close()
        q_hi = sb("q_hi", [128, 4, TP], F32R, mix)
        q_lo = sb("q_lo", [128, 4, TP], F32R, mix)
        k_hi = sb("k_hi", [128, 4, TP], F32R, mix)
        k_lo = sb("k_lo", [128, 4, TP], F32R, mix)
        qiv_hi = sb("qiv_hi", [128, 4, TP], F32R, mix)
        qiv_lo = sb("qiv_lo", [128, 4, TP], F32R, mix)
        keys = sb("keys", [128, 3 * TP], F32R, mix)
        kp_hi, kp_lo = keys[:, 0:TP + TS], keys[:, TP + TS:2 * (TP + TS)]
        turned_lo = keys.rearrange("p (s n) -> p s n", s=3)
        ki_hi, ki_lo = kp_hi[:, 0:TP], kp_lo[:, 0:TP]
        pages = sb("pages", [128, 2, NPG, 512], stack=mix)
        score = [None] + [sb(f"score{t}", [128, 128 * (t + 1)], stack=mix) for t in range(1, NT)]
        score_and_v = sb("score_and_v", [128, LS], stack=mix)
        score_s, v_s = score_and_v[0:TS, :], score_and_v[TS:2 * TS, 0:512]
        probs = sb("probs", [128, 3, TP], stack=mix)
        rows = probs[:, :, :].rearrange("p a n -> p (a n)")[:, 0:2 * UW].rearrange("p (a n) -> p a n", a=2)
        toep = sb("toep", [128, H, 256], stack=mix)
        toep_s = sb("toep_s", [128, 136], stack=mix)
        small = sb("small", [128, 21], stack=mix)
        top8, zero1 = small[:, 0:8], small[:, 20:21]
        soft = small[:, 8:20].rearrange("p (m n) -> p m n", n=4)
        near = sb("near", [128, 2, TP], stack=mix)
        pt_hi, pt_lo = kp_hi, kp_lo
        halves = stage_s[:, :, :].rearrange("p a b -> p (a b)")
        kw_t = stage[0:72, 0, :]
        kw_halves = stage[:, 1, 0:272]
        new_u = near[:, 1, 0:4 * TS]
        slots = pages[:, :, :, :].rearrange("p s a b -> p (s a b)")
        u_t = slots[:, 0:NG * UW].rearrange("p (g u) -> p g u", g=NG)
        hist_t = slots[:, NG * UW:NG * (UW + DB * HIST)].rearrange("p (g n) -> p g n", g=NG)
        hist_in = pages[0:DB * HIST, 1, NPG - 1, :]
        qi_s = near[0:64, 0, :].rearrange("p (b n) -> p b n", b=DB)
        wi_b = near[0:64, 1, :].rearrange("p (b n) -> p b n", b=DB)
        tmp_s = near[0:TS, 1, :]
        brow = rows[0:H, 1, 0:384]
        expand = near[0:TS, 0, :]
        kiwi = sb("kiwi", [128, NT + 1, 72], stack=mix)
        wi = sb("wi", [128, NT + 1, 8], stack=mix)
        q_s = sb("q_s", [128, 4, TS], stack=mix)
        k_s = sb("k_s", [128, 4, TS], stack=mix)
        ki_s = sb("ki_s", [64, TS], stack=mix)
        wi_t = sb("wi_t", [8, TS], stack=mix)
        ident_r = sb("ident_r", [128, 128], F32R, mix)
        table = sb("table", [1, 32], I32, mix)
        relb = toep[0:NB, 0, 0:H]
        mix.close()
        dec = ExitStack()
        q_pad = sb("q_pad", [128, 4, DB, 64], stack=dec)
        k_t = sb("k_t", [128, 2, 4, PAST], stack=dec)
        p_t = sb("p_t", [128, 5, 128], stack=dec)
        p_new = sb("p_new", [128, 64], stack=dec)
        pv_rows = sb("pv_rows", [128, 512], stack=dec)
        v_pages = sb("v_pages", [128, 2, NPG, 512], stack=dec)
        dec.close()
        mlp = ExitStack()
        hid_hi = sb("hid_hi", [128, 8, TP], F32R, mlp)
        hid_lo = sb("hid_lo", [128, 8, TP], F32R, mlp)
        hid_s = sb("hid_s", [128, 8, 2 * TS], F32R, mlp)
        x_res = sb("x_res", [128, NT + 1, D], stack=mlp)
        out_t = sb("out_t", [128, NT + 1, D], stack=mlp)
        gate_p = sb("gate_p", [128, D], stack=mlp)
        gate_s = sb("gate_s", [TS, D], stack=mlp)
        ln_post = sb("ln_post", [128, D], stack=mlp)
        half_s = sb("half_s", [TS, 512], stack=mlp)
        halves_mlp = sb("halves_mlp", [128, 512], stack=mlp)
        mlp.close()
        raw_landed = [sem(f"raw_landed{i}") for i in range(EARLY)]
        hi_ready, lo_ready = sem("hi_ready"), sem("lo_ready")
        bank_full = [sem(f"bank_full{i}") for i in range(8)]
        bank_free = [sem(f"bank_free{i}") for i in range(8)]
        act_chain, dve_chain, pool_chain = sem("act_chain"), sem("dve_chain"), sem("pool_chain")
        class Signals(dict):
            def __missing__(self, name):
                self[name] = sem(name)
                return self[name]

        S = Signals()
        stage_out = [sem("stage_out0"), sem("stage_out1")]
        k_page_in = [sem("k_page_in0"), sem("k_page_in1")]
        v_page_in = [sem("v_page_in0"), sem("v_page_in1")]
        block = ctx.enter_context(nc.Block())

        def full(eng, key):
            b, n = USE[key]
            eng.wait_ge(bank_full[b], n)
            return psum[b]

        def free(ins, key):
            ins.then_inc(bank_free[USE[key][0]], 1)

        def evacuated(eng, key):
            b, n = USE[key]
            eng.wait_ge(bank_free[b], n)

        class Chain:

            def __init__(self, eng, s):
                self.eng, self.s, self.n = eng, s, 0

            def __call__(self, ins):
                self.n += 1
                ins.then_inc(self.s, 1)
                self.eng.wait_ge(self.s, self.n)

        def parts_of(n):
            c, cols = piece_shape(PIECES[n][0])
            w = w_split[:, n % NSPLIT, 0:2 * c * cols]
            both = w.rearrange("p (c n) -> p c n", c=c)
            return both[:, :, 0:cols], both[:, :, cols:2 * cols], both

        def raw_piece(n):
            slot = raw_slot(n)
            if slot < NRAW:
                return raw[:, slot, :]
            return pages[:, slot - NRAW, :, :].rearrange("p a b -> p (a b)")

        def rows_of(t):
            return 128 if t < NT else TS

        landed_at, total = [], [0] * EARLY
        for n, (kind, i) in enumerate(PIECES):
            total[raw_slot(n)] += 16 * (3 if kind == "kiwi" else 1)
            landed_at.append(total[raw_slot(n)])

        w_in = a["w_in"][0].rearrange("(c p) n -> p c n", p=128)
        ada = a["ada_w"][0].rearrange("(c p) n -> p c n", p=128)
        w_o = a["w_out"][0].rearrange("(c p) n -> p c n", p=128)
        w_1 = a["w_ff1"][0].rearrange("(c p) n -> p c n", p=128)
        w_2 = a["w_ff2"][0].rearrange("(c p) n -> p c n", p=128)
        ck = a["cache_k"][0].rearrange("g p h d -> g p (h d)")
        cv = a["cache_v"][0].rearrange("g p h d -> g p (h d)")
        cx = a["cache_kidx"][0]
        xp = a["x_prompt"][0].rearrange("(t p) d -> p t d", p=128)
        xs = a["x_sample"].rearrange("b t d -> (b t) d")
        kidx_pages = pages[:, 0, :, :].rearrange("p a (b d) -> p (a b) d", d=HD)
        hankel = pages[:, 1, :, :].rearrange("p a (h j) -> p (a h) j", j=256)
        hankel_s = stage[0:64, 0, 0:136]
        N_AT = NT * H

        def pair_probs(ring, p, kb):
            a, b = sorted((2 * p % 3, (2 * p + 1) % 3))
            return ring[:, a:b + 1:b - a, 128 * kb:128 * kb + 128]

        def head_output(out, m):
            p = m // 2
            first = (2 * p % 3 < (2 * p + 1) % 3) == (m % 2 == 0)
            r = slice(64 * (m % 2), 64 * (m % 2) + 64)
            return out[r, 0:128] if first else out[r, 128:256]

        def turned_out(out, hh, b2):
            y = out[64 * hh:64 * hh + 64, :].rearrange("p (c b x h t) -> p c b x h t", c=4, b=2, x=4, h=2)
            first = y[:, 0, b2, 0, hh, :]
            return bass.AP(tensor=first.tensor, offset=first.offset, ap=[list(first.ap[0]), [128 + 2 * DS, 4], [1, DS]])

        def split_lo(eng, ops, m, chunks=slice(None), ready=None):
            c, cols = piece_shape(PIECES[m][0])
            hi, lo, _ = parts_of(m)
            if ready is None:
                eng.wait_ge(hi_ready, m + 1)
            else:
                eng.wait_ge(S["hi_half"], ready)
            r = raw_piece(m)[:, 0:c * cols].rearrange("p (c n) -> p c n", c=c)
            return ops.tensor_tensor(lo[:, chunks], r[:, chunks], hi[:, chunks].bitcast(F32), ALU.subtract)

        @block.sync
        def _(sp):
            def load_piece(n):
                kind, i = PIECES[n]
                before = [m for m in range(n) if raw_slot(m) == raw_slot(n)]
                if before:
                    sp.wait_ge(lo_ready, before[-1] + 1)
                s, r = raw_landed[raw_slot(n)], raw_piece(n)

                c, cols = piece_shape(kind)
                v = r[:, 0:c * cols].rearrange("p (c n) -> p c n", c=c)
                half = slice(4 * (i % 2), 4 * (i % 2) + 4)
                if kind == "ada":
                    x = 512 * (i // 2)
                    sp.dma_start(v, ada[:, half, x:x + 512]).then_inc(s, 16)
                elif kind == "v":
                    sp.dma_start(v, w_in[:, half, OFF_V:OFF_QI]).then_inc(s, 16)
                elif kind in COL0:
                    x = COL0[kind] + 256 * i
                    sp.dma_start(v, w_in[:, :, x:x + 256]).then_inc(s, 16)
                elif kind == "kiwi":
                    sp.dma_start(v[:, :, 0:64], w_in[:, :, OFF_KI:OFF_WI]).then_inc(s, 16)
                    sp.dma_start(v[:, :, 64:128], w_in[:, :, OFF_KI:OFF_WI]).then_inc(s, 16)
                    sp.dma_start(v[:, :, 128:136], w_in[:, :, OFF_WI:D_IN]).then_inc(s, 16)
                elif kind == "poolw":
                    sp.dma_start(v, a["pool_w"][0].rearrange("g p n -> p g n")).then_inc(s, 16)
                elif kind == "wo":
                    nh = i // 2
                    sp.dma_start(v, w_o[:, half, 512 * nh:512 * nh + 512]).then_inc(s, 16)
                elif kind == "w1":
                    sp.dma_start(v, w_1[:, :, 256 * i:256 * i + 256]).then_inc(s, 16)
                else:
                    f, nh, k = i // 4, i % 4 // 2, 4 * (i % 2)
                    sp.dma_start(v, w_2[:, 8 * f + k:8 * f + k + 4, 512 * nh:512 * nh + 512]).then_inc(s, 16)

            def page_of(i):
                return sp.value_load(table[0:1, i:i + 1], min_val=0, max_val=ck.shape[0] - 1)

            sp.dma_start(c_in[0:1, :], a["c_prompt"]).then_inc(S["c_in_landed"], 16)
            sp.dma_start(c_in[1:9, :], a["c_sample"]).then_inc(S["c_in_landed"], 16)
            sp.dma_start(cst[:], a["consts"]).then_inc(S["consts_in"], 16)
            for n in range(4):
                load_piece(n)
            sp.dma_start(x_in[:, 0:NT, :], xp).then_inc(S["x_landed"], 16)
            sp.dma_start(x_in[0:TS, NT, :], xs).then_inc(S["x_landed"], 16)
            for n in range(4, AT[("k", 0)]):
                load_piece(n)
            sp.wait_ge(S["table_in"], 16)
            for i in range(DB * NPG):
                sp.dma_start(kidx_pages[:, i, :], cx[bass.ds(page_of(i), 1)].rearrange("o p d -> (o p) d"))\
                    .then_inc(S["kidx_in"], 16)
            for n in range(AT[("k", 0)], AT[("ada", 12)] + 2):
                load_piece(n)

            def load_pages(b, cache, slots, landed):
                for g in range(NPG):
                    sp.dma_start(slots[:, b % 2, g, :],
                                 cache[bass.ds(page_of(b * NPG + g), 1)].rearrange("o p n -> (o p) n"))\
                        .then_inc(landed[b % 2], 16)

            sp.wait_ge(S["pool_lo"], NG)
            for b in range(2):
                load_pages(b, ck, pages, k_page_in)
            for n in range(AT[("ada", 12)] + 2, AT[("wo", 0)] + 2):
                load_piece(n)
            full(sp, ("pv", N_AT // 2 - 1))
            for bp in range(4):
                if bp == 0:
                    for b in range(2):
                        load_pages(b, cv, v_pages, v_page_in)
                if bp < 3:
                    for b in (2 * bp + 2, 2 * bp + 3):
                        full(sp, ("KT", b - 2, 3))
                        load_pages(b, ck, pages, k_page_in)
                if bp:
                    full(sp, ("pvR", bp - 1))
                    for b in (2 * bp, 2 * bp + 1):
                        load_pages(b, cv, v_pages, v_page_in)
            for n in range(AT[("wo", 0)] + 2, len(PIECES)):
                load_piece(n)

        @block.gpsimd
        def _(pool):
            link = Chain(pool, pool_chain)
            pool.dma_start(rows_in[0:8, :], a["ln1_pre"].rearrange("o (c p) -> (o c) p", p=128)).then_inc(S["small_in"], 16)
            pool.dma_start(rows_in[8:16, :], a["ln2_pre"].rearrange("o (c p) -> (o c) p", p=128)).then_inc(S["small_in"], 16)
            pool.dma_start(rows_in[16:20, :], a["pool_scale"].rearrange("o (c p) -> (o c) p", p=128)).then_inc(S["small_in"], 16)
            pool.dma_start(relb, a["rel_bias"]).then_inc(S["small_in"], 16)
            pool.dma_start(mod_rows[41:42, :], a["ada_b"][:, 0:2048]).then_inc(S["bias_in"], 16)
            pool.dma_start(table[:], a["page_table"].rearrange("a b -> (a b)").rearrange("(o n) -> o n", o=1))\
                .then_inc(S["table_in"], 16)
            pool.dma_start(o["pool_s"][0, :, 0:HIST - DS, :], a["state_pool"][0, :, DS:HIST, :]).then_inc(S["outs"], 16)
            nc.gpsimd.memset(wi_b, 0.0).then_inc(S["pad_zero"], 1)
            full(pool, ("modT", 0))
            pool.dma_start(mod_rows[41:42, :], a["ada_b"][:, 3072:5120]).then_inc(S["bias_in"], 16)
            evacuated(pool, "biasrow")
            pool.dma_start(dram_bias, brow[:]).then_inc(S["bias_row_out"], 16)
            pool.wait_ge(S["bias_row_out"], 16)
            pool.dma_start(hankel, bass.AP(tensor=dram_bias.tensor, offset=0, ap=[[1, 128], [384, H], [1, 256]]))\
                .then_inc(S["hankel_in"], 16)
            full(pool, "kiwi")
            for h in range(H):
                pool.dma_start(hankel_s[h * DS:(h + 1) * DS, :],
                               bass.AP(tensor=dram_bias.tensor, offset=384 * h + 120, ap=[[1, DS], [1, 136]]))\
                    .then_inc(S["hankel_s_in"], 16)
            evacuated(pool, "kiwi")
            pool.dma_start(o["kidx_p"][0, 0].rearrange("(t p) d -> p t d", p=128), kiwi[:, 0:NT, 0:64]).then_inc(S["outs"], 16)
            pool.dma_start(o["kidx_s"][0].rearrange("b t d -> (b t) d"), kiwi[0:TS, NT, 0:64]).then_inc(S["outs"], 16)

            full(pool, ("ixSn", DB - 1))
            full(pool, ("ixS", DB - 1))
            pool.dma_start(hist_in, a["state_pool"][0].rearrange("b i c -> (b i) c")).then_inc(S["hist_in"], 16)
            nc.gpsimd.memset(u_t, 0.0).then_inc(S["u_zero"], 1)

            for g in range(NG):
                u = u_t[:, g, :]
                evacuated(pool, ("uS", g // 2))
                if g == 0:
                    evacuated(pool, "hist")
                    evacuated(pool, "scSn")
                link(nc.gpsimd.tensor_copy(u[:, 16 + TP:].rearrange("p (b s) -> p b s", b=DB)[:, :, 1:1 + HIST],
                                           hist_t[:, g, :].rearrange("p (b i) -> p b i", b=DB)))
                if g >= 1:
                    pool.wait_ge(S["pooled"], g)
                src, lo = u, 0
                for lev in range(g + 1):
                    sh = 1 << lev
                    lo += sh
                    dst = rows[:, lev % 2, :]
                    ins = nc.gpsimd.tensor_tensor(dst[:, lo:UW], src[:, lo:UW], src[:, lo - sh:UW - sh], ALU.add)
                    if lev == g:
                        ins.then_inc(S["window_sums"], 1)
                    else:
                        link(ins)
                    src = dst
            evacuated(pool, ("uo", NG - 1))
            pool.dma_start(o["pool_p"][0, 0], near[128 - HIST:128, 0, :]).then_inc(S["state_out"], 16)
            for b in range(DB):
                pool.dma_start(o["pool_s"][0, b, HIST - DS:HIST, :], near[b * DS:(b + 1) * DS, 0, :])\
                    .then_inc(S["state_out"], 16)

            def split_half(k):
                pool.wait_ge(S["lo_half"], k - 1)
                split_lo(pool, nc.gpsimd, AT[("ada", FILL[k])], slice(0, 2)).then_inc(lo_ready, 1)

            pool.wait_ge(S["state_out"], 16 * (1 + DB))
            for t in range(NT):
                L = 128 * (t + 1)
                w = min(L, 256)
                mask = cc("causal") if t == 0 else score[t]
                pool.wait_ge(S["chosen"], t)
                if t == 0:
                    evacuated(pool, ("toep", 3))
                for h in range(H):
                    n = t * H + h
                    if n == 1:
                        evacuated(pool, ("v", NT))
                    if n == 2:
                        pool.dma_start(o["v_s"][0].rearrange("b t h d -> (b t) (h d)"), v_s).then_inc(S["outs"], 16)
                    if n >= 2:
                        pool.wait_ge(S["peaks"], n - 1)
                    if n == 20:
                        full(pool, ("modT", 1))
                        pool.dma_start(mod_rows[41:42, 0:1024], a["ada_b"][:, 2048:3072]).then_inc(S["bias_in"], 16)
                        pool.dma_start(mod_rows[41:42, 1024:2048], a["ada_b"][:, 5120:6144]).then_inc(S["bias_in"], 16)
                    if h < 2 and L > w:
                        link(nc.gpsimd.tensor_copy(near[:, n % 2, 0:L - w], mask[:, 0:L - w]))
                    nc.gpsimd.tensor_tensor(near[:, n % 2, L - w:L], toep[:, h, 256 - w:256], mask[:, L - w:L],
                                            ALU.add).then_inc(S["near_ok"], 1)
                    if n >= 6 and n % 2 == 0:
                        split_half(n // 2 - 1)
            split_half(len(FILL) - 1)
            evacuated(pool, ("qS", 1))
            full(pool, ("pv", N_AT // 2 - 1))
            link(nc.gpsimd.tensor_copy(expand.rearrange("p (b h t) -> p b h t", b=DB, h=H),
                                       cc("ident", TS)[:, 0:TS].rearrange("p (b t) -> p b t", b=DB).unsqueeze(2)
                                       .to_broadcast([TS, DB, H, DS])))
            link(nc.gpsimd.memset(q_pad[:], 0.0))
            for c in range(4):
                for hh in range(2):
                    nc.gpsimd.tensor_copy(
                        q_pad[64 * hh:64 * hh + 64, c, :, (2 * c + hh) * DS:(2 * c + hh + 1) * DS],
                        q_s[64 * hh:64 * hh + 64, c, :].rearrange("p (b t) -> p b t", b=DB)).then_inc(S["padded"], 1)
            evacuated(pool, ("pvS", 3))
            pool.wait_ge(S["outs"], 16 * 4)
            pool.dma_start(ln_post[:], a["ln1_post"].to_broadcast([128, D])).then_inc(S["gain_in"], 16)
            pool.dma_start(x_res[:, 0:NT, :], xp).then_inc(S["x_again"], 16)
            pool.dma_start(x_res[0:TS, NT, :], xs).then_inc(S["x_again"], 16)
            for t in range(NT + 1):
                r = rows_of(t)
                pool.wait_ge(S["gated"], t + 1)
                if t == 0:
                    pool.wait_ge(S["x_again"], 32)
                nc.gpsimd.tensor_tensor(x_res[0:r, t, :], x_res[0:r, t, :], out_t[0:r, t, :], ALU.add)\
                    .then_inc(S["residual"], 1)
            evacuated(pool, ("gS", 0, 1))
            pool.dma_start(ln_post[:], a["ln2_post"].to_broadcast([128, D])).then_inc(S["gain_in"], 16)
            yp = o["y_p"][0].rearrange("(t p) d -> p t d", p=128)
            for t in range(NT + 1):
                pool.wait_ge(S["y_ok"], t + 1)
                if t < NT:
                    pool.dma_start(yp[:, t, :], x_res[:, t, :]).then_inc(S["y_out"], 16)
                else:
                    pool.dma_start(o["y_s"].rearrange("b t d -> (b t) d"), x_res[0:TS, t, :]).then_inc(S["y_out"], 16)
            pool.wait_ge(S["y_out"], 16 * (NT + 1))
            stores = 2 * NT + 1
            for n in (stores, stores + 1):
                pool.wait_ge(stage_out[n % 2], 16 * (n // 2))
            pool.wait_ge(S["outs"], 16 * 4)

        @block.tensor
        def _(pe):
            uses = [0] * 8

            def claim(key):
                b, n = USE[key]
                uses[b] += 1
                assert n == uses[b], key
                if n > 1:
                    pe.wait_ge(bank_free[b], n - 1)
                return psum[b]

            def done(ins, key):
                ins.then_inc(bank_full[USE[key][0]], 1)

            def piece(kind, i):
                n = AT[(kind, i)]
                pe.wait_ge(lo_ready, n + 1)
                return parts_of(n)

            def mm(out, lhsT, rhs, start, stop):
                return nc.tensor.matmul(out, lhsT, rhs, start=start, stop=stop, skip_group_check=True)

            def turn(out, in_, k, start=True, stop=True):
                return nc.tensor.transpose(out, in_, cc("ident")[0:k, 0:k])

            pe.wait_ge(S["c_in_landed"], 32)
            pe.wait_ge(S["consts_in"], 16)
            t_ = claim("cT")
            for kc in range(KC):
                last = turn(t_[:, 9 * kc:9 * kc + 9], c_in[:, 128 * kc:128 * kc + 128], 9)
            done(last, "cT")
            pe.wait_ge(S["c_hi"], 1)
            evacuated(pe, "cT")

            mod_bank = [None]

            def modulation(i):
                hi, lo, _ = piece("ada", i)
                if i % 2 == 0:
                    mod_bank[0] = claim(("ada", i + 1))[0:72, :]
                out = mod_bank[0]
                for k4 in range(4):
                    kc = 4 * (i % 2) + k4
                    mm(out, c_split[:, kc, :], hi[:, k4, :], kc == 0, False)
                    last = mm(out, c_split[:, kc, :], lo[:, k4, :], False, kc == KC - 1)
                if i % 2:
                    done(last, ("ada", i))
                else:
                    last.then_inc(S["ada_half"], 1)

            def turned_modulation(k):
                evacuated(pe, ("ada", 7 + 12 * k))
                pe.wait_ge(S["bias_in"], 16 * (k + 1))
                out = claim(("modT", k))
                for j in range(16):
                    last = mm(out[:, 9 * j:9 * j + 9], mod_rows[:, 128 * j:128 * j + 128], cc("sel_t", 42), True, True)
                done(last, ("modT", k))

            def turned_hidden(k, src):
                pe.wait_ge(S["normed"], (NT + 1) * (k + 1))
                for kc in range(KC):
                    out = claim(("hT", k, kc))
                    for t in range(NT):
                        last = turn(out[:, 128 * t:128 * t + 128], src[:, t, 128 * kc:128 * kc + 128], 128)
                    done(last, ("hT", k, kc))
                out = claim(("hTS", k))
                for kc in range(KC):
                    last = turn(out[:, TS * kc:TS * kc + TS], src[0:TS, NT, 128 * kc:128 * kc + 128], TS)
                done(last, ("hTS", k))

            for i in range(8):
                modulation(i)
            pe.wait_ge(S["small_in"], 64)
            done(turn(claim("rowsT")[:, 0:20], rows_in[:, :], 20), "rowsT")
            turned_modulation(0)
            turned_hidden(0, x_nrm)

            hidden_ready = []

            def chunk_p(out, hi, lo, cols):
                for kc in range(KC):
                    if hidden_ready:
                        pe.wait_ge(S["h_hi"], hidden_ready[0] * KC + kc + 1)
                        pe.wait_ge(S["h_low"], hidden_ready[0] * KC + kc + 1)
                    mm(out, hi[:, kc, cols], act_hi[:, kc, :], kc == 0, False)
                    mm(out, hi[:, kc, cols], act_lo[:, kc, :], False, False)
                    last = mm(out, lo[:, kc, cols], act_hi[:, kc, :], False, kc == KC - 1)
                return last

            def rows_s(out, both):
                for kc in range(KC):
                    last = mm(out, act_s[:, kc, :], both[:, kc, :], kc == 0, kc == KC - 1)
                return last

            pending = []

            def project(kind, i):
                hi, lo, both = piece(kind, i)
                for j in range(2):
                    k = (kind, 2 * i + j)
                    done(chunk_p(claim(k)[:, :], hi, lo, slice(128 * j, 128 * j + 128)), k)
                    if j == 0:
                        fold_pending()
                        hidden_ready.clear()
                if i == 0 and kind in ("qi", "w1"):
                    pe.wait_ge(S["hs_lo"], 1 if kind == "qi" else 2)
                done(rows_s(claim((kind + "R", i))[:, :], both), (kind + "R", i))
                pending.append((kind, i))

            def fold_pending():
                while pending:
                    kind, i = pending.pop()
                    evacuated(pe, (kind + "R", i))
                    src = halves_mlp if kind == "w1" else halves
                    out = claim((kind + "S", i))
                    for j in range(2):
                        y = out[:, TS * j:TS * j + TS]
                        mm(y, src[:, 128 * j:128 * j + 128], cc("fold"), True, False)
                        last = mm(y, src[:, 256 + 128 * j:256 + 128 * j + 128], cc("fold"), False, True)
                    done(last, (kind + "S", i))

            hidden_ready.append(0)
            for i in range(2):
                project("qi", i)
            hi, lo, both = piece("kiwi", 0)
            done(chunk_p(claim("ki")[:, :], hi, lo, slice(0, 128)), "ki")
            fold_pending()
            done(chunk_p(claim("kw")[0:72, :], hi, lo, slice(64, 136)), "kw")
            done(rows_s(claim("kiR")[:, 0:272], both), "kiR")
            out = claim("biasrow")
            done(mm(out[0:H, 0:384], relb, cc("bucket", NB), True, True), "biasrow")
            evacuated(pe, "kw")
            evacuated(pe, "kiR")
            out = claim("kiS")[0:64, 0:TS]
            mm(out, kw_halves[:, 0:64], cc("fold"), True, False)
            done(mm(out, kw_halves[:, 136:200], cc("fold"), False, True), "kiS")
            out = claim("kiwi")
            for t in range(NT):
                turn(out[:, 72 * t:72 * t + 72], kw_t[:, 128 * t:128 * t + 128], 72)
            y = out[0:TS, 72 * NT:72 * NT + 72]
            mm(y, cc("fold"), kw_halves[:, 64:136], True, False)
            done(mm(y, cc("fold"), kw_halves[:, 200:272], False, True), "kiwi")
            pe.wait_ge(S["wi_ok"], 1)
            done(turn(claim("wiT")[0:H, 0:TS], wi[0:TS, NT, :], TS), "wiT")
            evacuated(pe, "wiT")
            done(mm(claim("wiR")[0:64, 0:TS], cc("heads", H), wi_t[:, :], True, True), "wiR")
            def by_head(out, q_h, q_l, k_h, k_l, h, tok, L):
                r, c = slice(64 * (h % 2), 64 * (h % 2) + 64), h // 2
                mm(out, q_h[r, c, tok], k_h(r, c), True, False)
                mm(out, q_h[r, c, tok], k_l(r, c), False, False)
                return mm(out, q_l[r, c, tok], k_h(r, c), False, True)

            evacuated(pe, ("qi", 3))
            evacuated(pe, "ki")
            for t in range(1, NT):
                L = 128 * (t + 1)
                for h in range(H):
                    out = claim(("ix", t, h))
                    done(by_head(out[:, 0:L], qiv_hi, qiv_lo, lambda r, c: ki_hi[r, 0:L], lambda r, c: ki_lo[r, 0:L],
                                 h, slice(128 * t, 128 * t + 128), L), ("ix", t, h))
            pe.wait_ge(S["hankel_in"], 16)
            for j in range(4):
                done(mm(claim(("toep", j))[:, :], cc("flip"), hankel[:, 2 * j:2 * j + 2, :], True, True), ("toep", j))
            pe.wait_ge(S["hankel_s_in"], 16 * H)
            done(mm(claim("toepS")[:, 0:136], cc("unflip", 64), hankel_s, True, True), "toepS")
            kx_t = pages[0:64, 1, :, :].rearrange("p a b -> p (a b)")
            pe.wait_ge(S["kidx_in"], 16 * DB * NPG)
            evacuated(pe, "kiS")
            evacuated(pe, ("qiS", 1))
            evacuated(pe, "wiR")

            def turn_kidx(b):
                out = claim(("kxT", b))
                for g in range(NPG):
                    last = turn(out[0:64, 128 * g:128 * g + 128], kidx_pages[:, NPG * b + g, :], 128)
                done(last, ("kxT", b))

            turn_kidx(0)
            for b in range(DB):
                evacuated(pe, ("kxT", b))
                done(mm(claim(("ixS", b))[0:64, :], qi_s[:, b, :], kx_t[:, 512 * (b % 2):512 * (b % 2) + 512], True, True), ("ixS", b))
                done(mm(claim(("ixSn", b))[0:64, 0:DS], qi_s[:, b, :], ki_s[:, b * DS:(b + 1) * DS], True, True), ("ixSn", b))
                if b + 1 < DB:
                    turn_kidx(b + 1)
                if b == 0:
                    sc, scn = claim("scS"), claim("scSn")
                evacuated(pe, ("ixSn", b))
                evacuated(pe, ("ixS", b))
                last1 = mm(sc[0:TS, :], wi_b[:, b, :], rows[0:64, b % 2, 0:PAST], b == 0, b == DB - 1)
                last2 = mm(scn[0:TS, 0:DS], wi_b[:, b, :], rows[0:64, b % 2, PAST:LS], b == 0, b == DB - 1)
                if b == DB - 1:
                    done(last1, "scS")
                    done(last2, "scSn")
                else:
                    last2.then_inc(S["relu_used"], 1)

            def by_token(kind, first, name, x_hi, x_lo, x_s, f=None, between=None):
                outs = []
                for half in range(2):
                    hi, lo, _ = piece(kind, first + half)
                    if f is not None:
                        pe.wait_ge(S["w1_done"], 8 * f + 4 * (half + 1))
                        pe.wait_ge(S["w1s_done"], 4 * f + 2 * (half + 1))
                    for t in range(NT + 1):
                        if half == 0:
                            outs.append(claim(name + (t,)))
                        for k4 in range(4):
                            k = 4 * half + k4
                            if t < NT:
                                tok = slice(128 * t, 128 * t + 128)
                                mm(outs[t][:, :], x_hi[:, k, tok], hi[:, k4, :], k == 0, False)
                                mm(outs[t][:, :], x_hi[:, k, tok], lo[:, k4, :], False, False)
                                last = mm(outs[t][:, :], x_lo[:, k, tok], hi[:, k4, :], False, k == 7)
                            else:
                                mm(outs[t][:, :], x_s[:, k, :], hi[:, k4, :], k == 0, False)
                                last = mm(outs[t][:, :], x_s[:, k, :], lo[:, k4, :], False, k == 7)
                        if half == 1:
                            done(last, name + (t,))
                        if half == 0 and t == 0:
                            fold_pending()
                        if between is not None and half == 1:
                            between(t)
                    if half == 0:
                        last.then_inc(S["half_done"], 1)

            for i in range(2):
                project("k", i)
                if i == 0:
                    pe.wait_ge(S["hist_in"], 16)
                    out = claim("hist")
                    for g in range(NG):
                        last = turn(out[:, 120 * g:120 * g + 120], hist_in[:, 128 * g:128 * g + 128], 120)
                    done(last, "hist")

            def turn_keys():
                evacuated(pe, ("k", 3))
                evacuated(pe, ("kS", 1))
                pe.wait_ge(S["ident_ok"], 1)
                for t in range(NT + 1):
                    out = claim(("kout", t))
                    for c in range(4):
                        y = out[:, 128 * c:128 * c + 128]
                        if t < NT:
                            mm(y, k_hi[:, c, 128 * t:128 * t + 128], ident_r[:, :], True, False)
                            last = mm(y, k_lo[:, c, 128 * t:128 * t + 128], ident_r[:, :], False, True)
                        else:
                            last = turn(y[0:TS, :], k_s[:, c, :], 128)
                    done(last, ("kout", t))

            for i in range(2):
                project("u", i)
            project("q", 0)

            def turn_channels(g):
                out = claim(("uo", g))
                turn(out[:, 0:128], u_t[:, g, 16 + TP - 128:16 + TP], 128)
                done(turn(out[0:TS, 128:256], new_u[:, TS * g:TS * g + TS], 128), ("uo", g))

            evacuated(pe, ("u", 3))
            evacuated(pe, ("uS", 1))
            for g in range(NG):
                if g == 2:
                    fold_pending()
                turn_channels(g)
            turn_keys()
            project("q", 1)

            def pool_maps(g):
                if g == NG:
                    return
                hi, lo, _ = piece("poolw", 0)
                pe.wait_ge(S["pool_lo"], g + 1)
                wh, wl = hi[:, g, :], lo[:, g, :]
                for key, cols in ((("pm", g), slice(0, TP)), (("pmS", g), slice(TP, TP + TS))):
                    out = claim(key)[:, 0:cols.stop - cols.start]
                    mm(out, wh, pt_hi[:, cols], True, False)
                    mm(out, wh, pt_lo[:, cols], False, False)
                    done(mm(out, wl, pt_hi[:, cols], False, True), key)

            by_token("v", 0, ("v",), act_hi, act_lo, act_s, between=pool_maps)

            evacuated(pe, ("q", 3))
            for n in range(N_AT + 4):
                if n < N_AT:
                    t, h = n // H, n % H
                    L = 128 * (t + 1)
                    out = claim(("lg", n))
                    done(by_head(out[:, 0:L], q_hi, q_lo, lambda r, c: k_hi[r, c, 0:L], lambda r, c: k_lo[r, c, 0:L],
                                 h, slice(128 * t, 128 * t + 128), L), ("lg", n))
                if n >= 5 and n % 2 == 1:
                    p = (n - 5) // 2
                    t, c = 2 * p // H, 2 * p % H // 2
                    if p == 0:
                        evacuated(pe, ("v", NT - 1))
                    evacuated(pe, ("pT", 2 * p))
                    evacuated(pe, ("pT", 2 * p + 1))
                    out = claim(("pv", p))[:, 0:256].rearrange("p (x n) -> p x n", x=2)
                    v = slice(128 * c, 128 * c + 128)
                    for kb in range(t + 1):
                        ph, pl = pair_probs(turned_hi, p, kb), pair_probs(turned_lo, p, kb)
                        mm(out, qiv_hi[:, kb, v], ph, kb == 0, False)
                        mm(out, qiv_hi[:, kb, v], pl, False, False)
                        last = mm(out, qiv_lo[:, kb, v], ph, False, kb == t)
                    done(last, ("pv", p))
                if 2 <= n <= N_AT + 1:
                    m = n - 2
                    pe.wait_ge(S["probs_ok"], m + 1)
                    out = claim(("pT", m))
                    for kb in range(m // H + 1):
                        last = turn(out[:, 128 * kb:128 * kb + 128], probs[:, m % 3, 128 * kb:128 * kb + 128], 128)
                    done(last, ("pT", m))
                if 2 <= n <= N_AT and n % 2 == 0:
                    modulation(FILL[n // 2 - 1])
                if n == 17:
                    turned_modulation(1)

            def turn_pages(b):
                pe.wait_ge(k_page_in[b % 2], 16 * NPG * (b // 2 + 1))
                for c in range(4):
                    out = claim(("KT", b, c))
                    for g in range(NPG):
                        last = turn(out[:, 128 * g:128 * g + 128], pages[:, b % 2, g, 128 * c:128 * c + 128], 128)
                    done(last, ("KT", b, c))

            turn_pages(0)
            turn_pages(1)
            pe.wait_ge(S["padded"], 8)
            pe.wait_ge(S["chosen"], NT)
            evacuated(pe, ("kS", 1))
            for bp in range(4):
                out, new = claim(("lgS", bp)), claim(("lgSn", bp))
                ex = expand[:, 128 * bp:128 * bp + 128]
                mm(out[:, :], ex, score_s[:, 0:PAST], True, False)
                mm(new[:, 0:DS], ex, score_s[:, PAST:LS], True, False)
                for b2 in range(2):
                    b, r = 2 * bp + b2, slice(64 * b2, 64 * b2 + 64)
                    for c in range(4):
                        evacuated(pe, ("KT", b, c))
                        last1 = mm(out[r, :], q_pad[:, c, b, :], k_t[:, b2, c, :], False, c == 3 and b2 == 1)
                        last2 = mm(new[r, 0:DS], q_pad[:, c, b, :], k_s[:, c, b * DS:(b + 1) * DS], False, c == 3 and b2 == 1)
                done(last1, ("lgS", bp))
                done(last2, ("lgSn", bp))
                if bp < 3:
                    turn_pages(2 * bp + 2)
                pe.wait_ge(S["prob_new"], bp + 1)
                out = claim(("pTS", bp))
                for g in range(NPG):
                    last = turn(out[:, 128 * g:128 * g + 128], rows[:, bp % 2, 128 * g:128 * g + 128], 128)
                done(last, ("pTS", bp))
                done(turn(claim(("pTSn", bp))[0:64, 0:128], p_new[:, :], 128), ("pTSn", bp))
                if bp < 3:
                    turn_pages(2 * bp + 3)
                evacuated(pe, ("pTSn", bp))
                evacuated(pe, ("pTS", bp))
                out = claim(("pvR", bp))
                for b2 in range(2):
                    pe.wait_ge(v_page_in[b2], 16 * NPG * (bp + 1))
                    r = slice(64 * b2, 64 * b2 + 64)
                    for g in range(NPG):
                        mm(out[r, :], p_t[:, g, r], v_pages[:, b2, g, :], g == 0, False)
                    last = mm(out[r, :], p_t[64:128, 4, r], v_s, False, True)
                done(last, ("pvR", bp))
                evacuated(pe, ("pvR", bp))
                out = claim(("pvS", bp))
                for c in range(4):
                    last = turn(out[:, 128 * c:128 * c + 128], pv_rows[:, 128 * c:128 * c + 128], 128)
                done(last, ("pvS", bp))

            pe.wait_ge(S["bias_in"], 16 * 4)

            def gates(k):
                for j in range(2):
                    r = mod_rows[:, 1024 * k + 512 * j:1024 * k + 512 * j + 512]
                    done(mm(claim(("gP", k, j))[:, :], cc("sel_p", 42), r, True, True), ("gP", k, j))
                    done(mm(claim(("gS", k, j))[0:TS, :], cc("sel_s", 42), r, True, True), ("gS", k, j))

            evacuated(pe, ("ada", 21))
            evacuated(pe, ("ada", 23))
            gates(0)

            evacuated(pe, ("pmS", NG - 1))
            evacuated(pe, ("pm", NG - 1))
            evacuated(pe, ("pv", N_AT // 2 - 1))
            evacuated(pe, ("pvS", 3))
            for nh in range(2):
                by_token("wo", 2 * nh, ("wo", nh), act_hi, act_lo, act_s)

            turned_hidden(1, out_t)
            hidden_ready.append(1)
            for f in range(QF):
                for i in range(4):
                    project("w1", 4 * f + i)
                    if f == 0 and i == 0:
                        gates(1)
                for nh in range(2):
                    by_token("w2", 4 * f + 2 * nh, ("w2", f, nh), hid_hi, hid_lo, hid_s, f)

        def split_hi_of(act, n, chunks=slice(None)):
            act.wait_ge(raw_landed[raw_slot(n)], landed_at[n])
            if n >= NSPLIT:
                piece_used(act, PIECES[n - NSPLIT])
            hi, (c, cols) = parts_of(n)[0], piece_shape(PIECES[n][0])
            r = raw_piece(n)[:, 0:c * cols].rearrange("p (c n) -> p c n", c=c)
            return nc.scalar.activation(hi[:, chunks], r[:, chunks], ACT.Copy)

        def piece_used(eng, pk):
            kind, i = pk
            if kind == "ada" and i % 2 == 0:
                eng.wait_ge(S["ada_half"], 1 + [k for k in PIECES if k[0] == "ada"].index(pk) // 2)
            elif kind == "v" and i == 0:
                eng.wait_ge(S["half_done"], 1)
            elif kind == "wo" and i % 2 == 0:
                eng.wait_ge(S["half_done"], 2 + i // 2)
            elif kind == "w2" and i % 2 == 0:
                eng.wait_ge(S["half_done"], 4 + i // 2)
            else:
                full(eng, last_use(kind, i))

        @block.scalar
        def _(act):
            link = Chain(act, act_chain)
            split = [0]

            def hi_until(n):
                while split[0] < min(n, len(PIECES)):
                    split_hi_of(act, split[0]).then_inc(hi_ready, 1)
                    split[0] += 1

            def run(out, in_, func=ACT.Copy, **kw):
                return nc.scalar.activation(out, in_, func, **kw)

            def square(k, t, src):
                r = rows_of(t)
                if NORM[k, t]:
                    act.wait_ge(S["squares"], NORM[k, t])
                junk = stage[:, :, :].rearrange("p a n -> p (a n)")
                x = (NT + 1) * k + t
                run(junk[0:r, :], src[0:r, t, :], ACT.Square, accum_out=ss[0:r, x:x + 1]).then_inc(S["squares"], 1)

            def root(k, t):
                x = (NT + 1) * k + t
                act.wait_ge(S["mean_ok"], NORM[k, t] + 1)
                run(rstd[0:rows_of(t), x:x + 1], ss[0:rows_of(t), x:x + 1], ACT.Sqrt).then_inc(S["root_ok"], 1)

            def turned_hidden(k):
                act.wait_ge(S["mod_ok"], 2 * (k + 1))
                for kc in range(KC):
                    out = full(act, ("hT", k, kc))
                    n = k * KC + kc
                    if k * KC + kc >= 2:
                        act.wait_ge(S["h_low"], n - 1)
                    free(run(stage[:, kc % 2, :], out[:, :], ACT.Identity,
                             scale=mod_t[:, 16 * k + 8 + kc, 0:1], bias=mod_t[:, 16 * k + kc, 0:1]), ("hT", k, kc))
                    evacuated(act, ("hT", k, kc))
                    run(act_hi[:, kc, :], stage[:, kc % 2, :]).then_inc(S["h_hi"], 1)
                act.wait_ge(S["hs_staged"], k + 1)
                run(act_s[:, :, 0:TS], stage_s[:, :, :]).then_inc(S["hs_hi"], 1)

            act.wait_ge(S["split_zero"], 1)
            out = full(act, "cT")
            run(c_split[:, :, 0:9], out[:, 0:72].rearrange("p (c m) -> p c m", m=9)).then_inc(S["c_hi"], 1)
            hi_until(2)

            def modulation(i, split=True):
                if i % 2:
                    out = full(act, ("ada", i))
                if split:
                    hi_until(AT[("ada", i)] + 3)
                if i in (13, 9):
                    full(act, ("modT", 0 if i == 13 else 1))
                if i % 2:
                    x = 256 * (ADA_ROW[i] - 1)
                    free(run(mod_rows[0:41, x:x + 512], out[0:41, :]), ("ada", i))

            for i in range(8):
                modulation(i)
                if i == 1:
                    act.wait_ge(S["x_landed"], 32)
                if 1 <= i <= NT + 1:
                    square(0, i - 1, x_in)
                if i == 6:
                    for t in range(NT + 1):
                        root(0, t)
            free(run(rows_t[:, :], full(act, "rowsT")[:, 0:20]), "rowsT")
            turned_hidden(0)

            def pair(kind, i, chunk, tail):
                for j in range(2):
                    chunk(2 * i + j, full(act, (kind, 2 * i + j)))
                n = AT[(kind, i)]
                free(run(halves, full(act, (kind + "R", i))[:, :]), (kind + "R", i))
                hi_until(n + 3)
                tail(i, full(act, (kind + "S", i)))

            def qi_tail(i, out):
                for hh in range(2):
                    ins = run(qi_s.rearrange("p b (c x t) -> p x c b t", x=2, t=DS)[:, hh, 2 * i:2 * i + 2],
                              out[64 * hh:64 * hh + 64, 0:2 * TS].rearrange("p (c b t) -> p c b t", c=2, b=DB))
                free(ins, ("qiS", i))

            for i in range(2):
                pair("qi", i, lambda c, out: run(qiv_hi[:, c, :], out[:, :]).then_inc(S["proj_hi"], 1), qi_tail)
            run(ki_hi[:, :], full(act, "ki")[:, :]).then_inc(S["proj_hi"], 1)
            free(run(kw_t, full(act, "kw")[0:72, :]), "kw")
            hi_until(AT[("kiwi", 0)] + 3)
            free(run(kw_halves, full(act, "kiR")[:, 0:272]), "kiR")
            run(brow[:, :], full(act, "biasrow")[0:H, 0:384]).then_inc(bank_free[USE["biasrow"][0]], 1)
            free(run(ki_s[:, :], full(act, "kiS")[0:64, 0:TS]), "kiS")
            out = full(act, "kiwi")
            run(kiwi[:, 0:NT, :], out[:, 0:72 * NT].rearrange("p (t n) -> p t n", t=NT))
            free(run(kiwi[0:TS, NT, :], out[0:TS, 72 * NT:72 * NT + 72]), "kiwi")
            free(run(wi_t[:, :], full(act, "wiT")[0:H, 0:TS]), "wiT")
            act.wait_ge(S["consts_in"], 16)
            run(ident_r[:, :], cc("ident")).then_inc(S["ident_ok"], 1)

            act.wait_ge(S["bias_row_out"], 16)
            for t in range(1, NT):
                L = 128 * (t + 1)
                for h in range(H):
                    n = (t - 1) * H + h
                    out = full(act, ("ix", t, h))
                    if n >= 2:
                        act.wait_ge(S["relu_added"], n - 1)
                    free(run(rows[:, n % 2, 0:L], out[:, 0:L], ACT.Relu, scale=HD ** -0.5), ("ix", t, h))
            for j in range(4):
                free(run(toep[:, 2 * j:2 * j + 2, :], full(act, ("toep", j))[:, :].rearrange("p (h j) -> p h j", h=2)), ("toep", j))
            free(run(toep_s[:, :], full(act, "toepS")[:, 0:136]), "toepS")
            act.wait_ge(S["relu_added"], (NT - 1) * H)
            kx_t = pages[0:64, 1, :, :].rearrange("p a b -> p (a b)")

            def kidx_keep(b):
                free(run(kx_t[:, 512 * (b % 2):512 * (b % 2) + 512], full(act, ("kxT", b))[0:64, :]), ("kxT", b))

            kidx_keep(0)
            for b in range(DB):
                if b >= 2:
                    act.wait_ge(S["relu_used"], b - 1)
                free(run(rows[0:64, b % 2, 0:PAST], full(act, ("ixS", b))[0:64, :], ACT.Relu, scale=HD ** -0.5), ("ixS", b))
                free(run(rows[0:64, b % 2, PAST:LS], full(act, ("ixSn", b))[0:64, 0:DS], ACT.Relu, scale=HD ** -0.5), ("ixSn", b))
                if b + 1 < DB:
                    kidx_keep(b + 1)

            def k_tail(i, out):
                free(run(k_s[:, 2 * i:2 * i + 2, :], out[:, 0:2 * TS].rearrange("p (c n) -> p c n", c=2)), ("kS", i))

            def q_tail(i, out):
                free(run(q_s[:, 2 * i:2 * i + 2, :], out[:, 0:2 * TS].rearrange("p (c n) -> p c n", c=2),
                         scale=HD ** -0.5), ("qS", i))

            def k_chunk(c, out):
                run(k_hi[:, c, :], out[:, :]).then_inc(S["proj_hi"], 1)

            def q_chunk(c, out):
                run(q_hi[:, c, :], out[:, :], scale=HD ** -0.5).then_inc(S["proj_hi"], 1)

            staged = [0]

            def stage_copy(out, r):
                n = staged[0]
                if n >= 2:
                    act.wait_ge(stage_out[n % 2], 16 * (n // 2))
                staged[0] += 1
                return n, run(stage[0:r, n % 2, :], out)

            def store(n, r, dst):
                act.dma_start(dst, stage[0:r, n % 2, :]).then_inc(stage_out[n % 2], 16)

            def heads(x):
                return x.rearrange("p h d -> p (h d)")

            pair("k", 0, k_chunk, k_tail)
            free(run(hist_t, full(act, "hist")[:, 0:480].rearrange("p (g n) -> p g n", g=NG)), "hist")
            pair("k", 1, k_chunk, k_tail)
            def u_chunk(g, out):
                if g == 0:
                    act.wait_ge(S["u_zero"], 1)
                free(run(u_t[:, g, 16:16 + TP], out[:, :]), ("u", g))

            def u_tail(i, out):
                run(new_u[:, 2 * TS * i:2 * TS * i + 2 * TS], out[:, 0:2 * TS])
                free(run(u_t[:, 2 * i:2 * i + 2, 16 + TP:].rearrange("p a (b s) -> p a b s", b=DB)[:, :, :, SEG - DS:],
                         out[:, 0:2 * TS].rearrange("p (a b t) -> p a b t", a=2, b=DB)), ("uS", i))

            for i in range(2):
                pair("u", i, u_chunk, u_tail)
            pair("q", 0, q_chunk, q_tail)
            for g in range(NG):
                out = full(act, ("uo", g))
                run(near[64:128, 0, 128 * g:128 * g + 128], out[64:128, 0:128])
                free(run(near[0:TS, 0, 128 * g:128 * g + 128], out[0:TS, 128:256]), ("uo", g))
            for t in range(NT + 1):
                r = rows_of(t)
                n, ins = stage_copy(full(act, ("kout", t))[0:r, :], r)
                free(ins, ("kout", t))
                evacuated(act, ("kout", t))
                store(n, r, heads(o["k_p"][0, 0, 128 * t:128 * t + 128]) if t < NT
                      else o["k_s"][0].rearrange("b t h d -> (b t) (h d)"))
            pair("q", 1, q_chunk, q_tail)

            hi_until(AT[("v", 0)] + 3)
            for g in range(NG):
                act.wait_ge(S["pooled"], g + 1)
                src = u_t[:, g, :]
                if g >= 1:
                    full(act, ("pmS", g - 1))
                run(pt_hi[:, 0:TP], src[:, 16:16 + TP])
                run(pt_hi[:, TP:TP + TS].rearrange("p (b t) -> p b t", b=DB),
                    src[:, 16 + TP:].rearrange("p (b s) -> p b s", b=DB)[:, :, SEG - DS:]).then_inc(S["pool_hi"], 1)
                if g == 0:
                    act.wait_ge(S["half_done"], 1)
                out = full(act, ("v", g))
                run(qiv_hi[:, g, :], out[:, :])
                n, ins = stage_copy(out[:, :], 128)
                ins.then_inc(S["v_staged"], 1)
                act.wait_ge(S["v_staged"], g + 1)
                store(n, 128, heads(o["v_p"][0, 0, 128 * g:128 * g + 128]))
                for key, dst in ((("pm", g), act_hi[:, g, :]), (("pmS", g), act_s[:, g, 0:TS])):
                    out = full(act, key)
                    n = dst.shape[1]
                    run(dst, out[:, 0:n], scale=rows_t[:, 16 + g:17 + g]).then_inc(S["mixed_hi"], 1)
            run(tmp_s[:, :], full(act, ("v", NT))[TS:2 * TS, :]).then_inc(S["v_low_rows"], 1)
            hi_until(AT[("v", 1)] + 3)


            for k in (staged[0], staged[0] + 1):
                act.wait_ge(stage_out[k % 2], 16 * (k // 2))
            for n in range(N_AT + 5):
                if n >= 6 and n % 2 == 0:
                    out = full(act, ("pv", (n - 6) // 2))
                    for m in (n - 6, n - 5):
                        t, h = m // H, m % H
                        r = slice(64 * (h % 2), 64 * (h % 2) + 64)
                        run(act_hi[r, 4 + h // 2, 128 * t:128 * t + 128], head_output(out, m)).then_inc(S["o_hi"], 1)
                if n < N_AT:
                    L = 128 * (n // H + 1)
                    act.wait_ge(S["peaks"], n + 1)
                    run(probs[:, n % 3, 0:L], probs[:, n % 3, 0:L], ACT.Exp, bias=soft[:, n % 3, 1:2],
                        accum_out=soft[:, n % 3, 2:3]).then_inc(S["exps"], 1)
                if 2 <= n <= N_AT + 1:
                    m = n - 2
                    L = 128 * (m // H + 1)
                    out = full(act, ("pT", m))
                    if m >= 3:
                        full(act, ("pv", (m - 3) // 2))
                    run(turned_hi[:, m % 3, 0:L], out[:, 0:L]).then_inc(S["pt_hi_ok"], 1)
                if n == 0:
                    hi_until(AT[("poolw", 0)] + 3)
                m = AT[("ada", FILL[0])] + n // 2 + (n % 2)
                if 3 <= n <= N_AT + 1 and n % 2 == 1:
                    modulation(FILL[(n - 3) // 2], False)
                    if n < N_AT - 1:
                        split_hi_of(act, m, slice(2, 4)).then_inc(S["hi_half"], 1)
                if 4 <= n < N_AT and n % 2 == 0:
                    split_hi_of(act, m, slice(0, 2)).then_inc(hi_ready, 1)

            split[0] = AT[("wo", 0)]

            def keep_keys(b, c):
                out = full(act, ("KT", b, c))
                if b >= 2:
                    full(act, ("lgS", b // 2 - 1))
                free(run(k_t[:, b % 2, c, :], out[:, :]), ("KT", b, c))

            for b in range(2):
                keep_keys(b, 0), keep_keys(b, 2)
            hi_until(AT[("wo", 0)] + 2)
            for bp in range(4):
                if bp < 3:
                    keep_keys(2 * bp + 2, 0)
                act.wait_ge(S["peak_s"], bp + 1)
                run(rows[:, bp % 2, 0:LS], rows[:, bp % 2, 0:LS], ACT.Exp, bias=soft[:, bp % 2, 1:2],
                    accum_out=soft[:, bp % 2, 2:3]).then_inc(S["exp_s"], 1)
                if bp < 3:
                    keep_keys(2 * bp + 2, 2)
                out = full(act, ("pTS", bp))
                if bp >= 1:
                    full(act, ("pvR", bp - 1))
                free(run(p_t[:, 0:4, :], out[:, :].rearrange("p (g n) -> p g n", g=NPG)), ("pTS", bp))
                free(run(p_t[64:128, 4, :], full(act, ("pTSn", bp))[0:64, 0:128]), ("pTSn", bp))
                if bp < 3:
                    keep_keys(2 * bp + 3, 0), keep_keys(2 * bp + 3, 2)
                if bp >= 1:
                    full(act, ("pvS", bp - 1))
                free(run(pv_rows[:, :], full(act, ("pvR", bp))[:, :]), ("pvR", bp))
                out = full(act, ("pvS", bp))
                for hh in range(2):
                    for b2 in range(2):
                        run(act_s[64 * hh:64 * hh + 64, 4:8, 16 * bp + 8 * b2:16 * bp + 8 * b2 + 8],
                            turned_out(out, hh, b2)).then_inc(S["os_hi"], 1)

            def keep_tokens(kind, f, nh, copy, low, last_piece):
                for t in range(NT):
                    if copy:
                        free(run(out_t[:, t, 512 * nh:512 * nh + 512], full(act, (kind, *f, nh, t))[:, :]), (kind, *f, nh, t))
                out = full(act, (kind, *f, nh, NT))
                if low >= 1:
                    prev = ("wo", 0, NT) if low == 1 else ("wo", 1, NT) if low == 2 else ("w2", (low - 3) // 2, (low - 3) % 2, NT)
                    evacuated(act, prev)
                run(half_s[:, :], out[TS:2 * TS, :]).then_inc(S["low_rows"], 1)
                hi_until(last_piece + 3)

            hi_until(AT[("wo", 0)] + 3)
            keep_tokens("wo", (), 0, True, 0, AT[("wo", 1)])
            hi_until(AT[("wo", 2)] + 3)
            for j in range(NT + 1 + LAG):
                if j < NT:
                    free(run(out_t[:, j, 512:D], full(act, ("wo", 1, j))[:, :]), ("wo", 1, j))
                elif j == NT:
                    out = full(act, ("wo", 1, NT))
                    evacuated(act, ("wo", 0, NT))
                    run(half_s[:, :], out[TS:2 * TS, :]).then_inc(S["low_rows"], 1)
                if j <= NT:
                    evacuated(act, ("wo", 1, j))
                    square(1, j, out_t)
                if j >= LAG:
                    act.wait_ge(S["residual"], j - LAG + 1)
                    square(2, j - LAG, x_res)
                if j <= NT:
                    root(1, j)
                if j >= LAG:
                    root(2, j - LAG)
            turned_hidden(1)
            hi_until(AT[("wo", 3)] + 3)

            for f in range(QF):
                for i in range(4):
                    p = 4 * f + i
                    for n in (2 * p, 2 * p + 1):
                        out = full(act, ("w1", n))
                        if n >= 2:
                            act.wait_ge(S["w1_done"], n - 1)
                        free(run(stage[:, n % 2, :], out[:, :], ACT.Relu), ("w1", n))
                    for n in (2 * p, 2 * p + 1):
                        act.wait_ge(S["w1_squared"], n + 1)
                        run(hid_hi[:, n % 8, :], stage[:, n % 2, :]).then_inc(S["w1_hi"], 1)
                    hi_until(AT[("w1", p)] + 3)
                    free(run(halves_mlp[:, :], full(act, ("w1R", p))[:, :]), ("w1R", p))
                    out = full(act, ("w1S", p))
                    if p >= 2:
                        act.wait_ge(S["w1s_done"], p - 1)
                    st = stage_s[:, 2 * (p % 2):2 * (p % 2) + 2, :]
                    free(run(st, out[:, 0:2 * TS].rearrange("p (a n) -> p a n", a=2), ACT.Relu), ("w1S", p))
                    act.wait_ge(S["w1s_squared"], p + 1)
                    run(hid_s[:, 2 * i:2 * i + 2, 0:TS], st).then_inc(S["w1s_hi"], 1)
                for nh in range(2):
                    hi_until(AT[("w2", 4 * f + 2 * nh)] + 3)
                    if f < QF - 1 or nh == 0:
                        keep_tokens("w2", (f,), nh, f == 0, 2 + 2 * f + nh, AT[("w2", 4 * f + 2 * nh + 1)])
            act.wait_ge(S["w1_done"], 2 * DFF // 256)
            for t in range(NT):
                evacuated(act, ("w2", QF - 1, 1, t))
                square(3, t, out_t)
                root(3, t)
            keep_tokens("w2", (QF - 1,), 1, False, 1 + 2 * QF, 0)
            evacuated(act, ("w2", QF - 1, 1, NT))
            square(3, NT, out_t)
            root(3, NT)

        @block.vector
        def _(dve):
            link = Chain(dve, dve_chain)
            split = [0]

            def lo_until(n):
                while split[0] < min(n, len(PIECES)):
                    split_lo(dve, nc.vector, split[0]).then_inc(lo_ready, 1)
                    split[0] += 1

            def minus(out, x, hi):
                return nc.vector.tensor_tensor(out, x, hi.bitcast(F32), ALU.subtract)

            def scaled_minus(out, x, scale, hi):
                return nc.vector.scalar_tensor_tensor(out, x, scale, hi.bitcast(F32), ALU.mult, ALU.subtract)

            nc.vector.memset(c_split[:].bitcast(F32), 0.0).then_inc(S["split_zero"], 1)
            nc.vector.memset(zero1, 0.0)
            out = full(dve, "cT")
            dve.wait_ge(S["c_hi"], 1)
            dve.wait_ge(S["split_zero"], 1)
            ins = minus(c_split[:, :, 32:41], out[:, 0:72].rearrange("p (c m) -> p c m", m=9), c_split[:, :, 0:9])
            free(ins, "cT")
            lo_until(2)

            def mean(k, t):
                x, r = (NT + 1) * k + t, rows_of(t)
                dve.wait_ge(S["squares"], NORM[k, t] + 1)
                nc.vector.tensor_scalar(ss[0:r, x:x + 1], ss[0:r, x:x + 1], 1.0 / D, EPS, ALU.mult, ALU.add)\
                    .then_inc(S["mean_ok"], 1)

            def rstd_of(k, t):
                x, r = (NT + 1) * k + t, rows_of(t)
                dve.wait_ge(S["root_ok"], NORM[k, t] + 1)
                link(nc.vector.reciprocal(rstd[0:r, x:x + 1], rstd[0:r, x:x + 1]))
                return rstd[0:r, x:x + 1]

            def normalise(k, t, dst, src):
                r = rows_of(t)
                nc.vector.tensor_scalar(dst[0:r, t, :], src[0:r, t, :], rstd_of(k, t), None, ALU.mult)\
                    .then_inc(S["normed"], 1)

            for i in range(8):
                lo_until(i + 3)
                if 1 <= i <= NT + 1:
                    mean(0, i - 1)
                if i == 6:
                    for t in range(NT + 1):
                        normalise(0, t, x_nrm, x_in)

            def turned_hidden(k):
                out = full(dve, ("modT", k))
                m = mod_t[:, 16 * k:16 * k + 16, :]
                evacuated(dve, "rowsT")
                free(nc.vector.tensor_copy(m, out[:, 0:144].rearrange("p (j m) -> p j m", m=9)), ("modT", k))
                evacuated(dve, ("modT", k))
                gain = rows_t[:, 8 * k:8 * k + 8].unsqueeze(2).to_broadcast([128, 8, 9])
                nc.vector.scalar_tensor_tensor(m[:, 8:16, :], m[:, 8:16, :], 1.0, gain, ALU.add, ALU.mult)\
                    .then_inc(S["mod_ok"], 2)
                dve.wait_ge(S["mod_ok"], 2 * (k + 1))

            def split_hidden(k):
                for kc in range(KC):
                    dve.wait_ge(S["h_hi"], k * KC + kc + 1)
                    minus(act_lo[:, kc, :], stage[:, kc % 2, :], act_hi[:, kc, :]).then_inc(S["h_low"], 1)
                out = full(dve, ("hTS", k))
                m = mod_t[:, 16 * k:16 * k + 16, 1:9]
                dims = [128, KC, DB, DS]
                st = stage_s[:, :, :].rearrange("p c (b t) -> p c b t", b=DB)
                free(nc.vector.tensor_tensor(st, out[:, :].rearrange("p (c b t) -> p c b t", c=KC, b=DB),
                                             m[:, 8:16, :].unsqueeze(3).to_broadcast(dims), ALU.mult), ("hTS", k))
                evacuated(dve, ("hTS", k))
                nc.vector.tensor_tensor(st, st, m[:, 0:8, :].unsqueeze(3).to_broadcast(dims), ALU.add)\
                    .then_inc(S["hs_staged"], 1)
                dve.wait_ge(S["hs_staged"], k + 1)
                dve.wait_ge(S["hs_hi"], k + 1)
                minus(act_s[:, :, TS:2 * TS], stage_s[:, :, :], act_s[:, :, 0:TS]).then_inc(S["hs_lo"], 1)

            turned_hidden(0)
            split_hidden(0)

            for i in range(2):
                for c in (2 * i, 2 * i + 1):
                    dve.wait_ge(S["proj_hi"], c + 1)
                    free(minus(qiv_lo[:, c, :], full(dve, ("qi", c))[:, :], qiv_hi[:, c, :]), ("qi", c))
                lo_until(AT[("qi", i)] + 3)
            dve.wait_ge(S["proj_hi"], 5)
            free(minus(ki_lo[:, :], full(dve, "ki")[:, :], ki_hi[:, :]), "ki")
            lo_until(AT[("kiwi", 0)] + 3)
            evacuated(dve, "kiwi")
            nc.vector.tensor_scalar(wi[:, 0:NT, :], kiwi[:, 0:NT, 64:72], H ** -0.5, None, ALU.mult)
            nc.vector.tensor_scalar(wi[0:TS, NT, :], kiwi[0:TS, NT, 64:72], H ** -0.5, None, ALU.mult).then_inc(S["wi_ok"], 1)
            dve.wait_ge(S["wi_ok"], 1)
            out = full(dve, "wiR")
            dve.wait_ge(S["pad_zero"], 1)
            w0 = wi_b[:, :, 0:DS]
            diag = bass.AP(tensor=w0.tensor, offset=w0.offset, ap=[list(w0.ap[0]), [64 + DS, DB], [1, DS]])
            free(nc.vector.tensor_tensor(diag, out[0:64, 0:TS].rearrange("p (b t) -> p b t", b=DB),
                                         cc("step", 64).rearrange("p (b t) -> p b t", b=DB), ALU.mult), "wiR")

            for t in range(1, NT):
                L = 128 * (t + 1)
                for h in range(H):
                    n = (t - 1) * H + h
                    evacuated(dve, ("ix", t, h))
                    r = rows[:, n % 2, 0:L]
                    if h == 0:
                        ins = nc.vector.tensor_scalar(score[t][:, 0:L], r, wi[:, t, h:h + 1], 0.0, ALU.mult, ALU.add)
                    else:
                        ins = nc.vector.scalar_tensor_tensor(score[t][:, 0:L], r, wi[:, t, h:h + 1], score[t][:, 0:L],
                                                             ALU.mult, ALU.add)
                    ins.then_inc(S["relu_added"], 1)
                    dve.wait_ge(S["relu_added"], n + 1)
                link(nc.vector.tensor_tensor(score[t][:, L - 128:L], score[t][:, L - 128:L], cc("causal"), ALU.add))
            def choose(buf, n_sel):
                r = buf.shape[0]
                for left in range(n_sel, 0, -8):
                    link(nc.vector.max(top8[0:r, :], buf))
                    if left < 8:
                        link(nc.vector.memset(top8[0:r, left:8], TAKEN))
                    link(nc.vector.match_replace(buf, top8[0:r, :], buf, TAKEN))
                    yield
                nc.vector.tensor_scalar(buf, buf, TAKEN, NEG, ALU.not_equal, ALU.mult).then_inc(S["chosen"], 1)
                yield

            def all_choices():
                for t in range(1, NT):
                    yield from choose(score[t][:, :], SEL_P)
                yield from choose(score_s[:, :], SEL_S)

            rounds = all_choices()

            def some_rounds(n):
                for _ in range(n):
                    next(rounds, None)

            some_rounds(36)
            free(nc.vector.tensor_copy(score_s[:, 0:PAST], full(dve, "scS")[0:TS, :]), "scS")
            free(nc.vector.tensor_tensor(score_s[:, PAST:LS], full(dve, "scSn")[0:TS, 0:DS], cc("newmask", TS), ALU.add), "scSn")
            evacuated(dve, "scS")
            evacuated(dve, "scSn")

            def k_pair(i):
                for c in (2 * i, 2 * i + 1):
                    dve.wait_ge(S["proj_hi"], 6 + c)
                    free(minus(k_lo[:, c, :], full(dve, ("k", c))[:, :], k_hi[:, c, :]), ("k", c))
                    some_rounds(3)
                lo_until(AT[("k", i)] + 3)

            def q_pair(i):
                for c in (2 * i, 2 * i + 1):
                    dve.wait_ge(S["proj_hi"], 10 + c)
                    free(scaled_minus(q_lo[:, c, :], full(dve, ("q", c))[:, :], HD ** -0.5, q_hi[:, c, :]), ("q", c))
                    some_rounds(1)
                lo_until(AT[("q", i)] + 3)

            for i in range(2):
                k_pair(i)
            for i in range(2):
                lo_until(AT[("u", i)] + 3)
                some_rounds(4)
            q_pair(0)
            for g in range(NG):
                sums, u = rows[:, g % 2, :], u_t[:, g, :]
                some_rounds((0, 2, 3, 4)[g])
                full(dve, ("uo", g))
                dve.wait_ge(S["window_sums"], g + 1)
                link(nc.vector.tensor_tensor(sums[:, 16:32], sums[:, 16:32], cc("invcnt")[:, 16 * g:16 * g + 16], ALU.mult))
                nc.vector.tensor_tensor(u[:, 16:32], sums[:, 16:32], u[:, 16:32], ALU.subtract)
                nc.vector.scalar_tensor_tensor(u[:, 32:UW], sums[:, 32:UW], 1.0 / WINDOWS[g], u[:, 32:UW],
                                               ALU.mult, ALU.subtract).then_inc(S["pooled"], 1)
            q_pair(1)
            lo_until(AT[("v", 0)] + 3)
            for g in range(NG):
                dve.wait_ge(S["pool_hi"], g + 1)
                src = u_t[:, g, :]
                minus(pt_lo[:, 0:TP], src[:, 16:16 + TP], pt_hi[:, 0:TP])
                minus(pt_lo[:, TP:TP + TS].rearrange("p (b t) -> p b t", b=DB),
                      src[:, 16 + TP:].rearrange("p (b s) -> p b s", b=DB)[:, :, SEG - DS:],
                      pt_hi[:, TP:TP + TS].rearrange("p (b t) -> p b t", b=DB)).then_inc(S["pool_lo"], 1)
                dve.wait_ge(S["v_staged"], g + 1)
                free(minus(qiv_lo[:, g, :], full(dve, ("v", g))[:, :], qiv_hi[:, g, :]), ("v", g))
                sc = rows_t[:, 16 + g:17 + g]
                dve.wait_ge(S["mixed_hi"], 2 * g + 1)
                free(scaled_minus(act_lo[:, g, :], full(dve, ("pm", g))[:, :], sc, act_hi[:, g, :]), ("pm", g))
                dve.wait_ge(S["mixed_hi"], 2 * g + 2)
                free(scaled_minus(act_s[:, g, TS:2 * TS], full(dve, ("pmS", g))[:, 0:TS], sc, act_s[:, g, 0:TS]), ("pmS", g))
            dve.wait_ge(S["v_low_rows"], 1)
            free(nc.vector.tensor_tensor(v_s, full(dve, ("v", NT))[0:TS, :], tmp_s[:, :], ALU.add), ("v", NT))
            for n in range(N_AT + 5):
                if n == 18:
                    turned_hidden(1)
                if n < N_AT:
                    L = 128 * (n // H + 1)
                    out = full(dve, ("lg", n))
                    dve.wait_ge(S["near_ok"], n + 1)
                    if n >= 3:
                        full(dve, ("pT", n - 3))
                    free(nc.vector.tensor_tensor_reduce(probs[:, n % 3, 0:L], out[:, 0:L], near[:, n % 2, 0:L], 1.0, TAKEN,
                                                        ALU.add, ALU.max, soft[:, n % 3, 0:1]), ("lg", n))
                    evacuated(dve, ("lg", n))
                    nc.vector.tensor_scalar(soft[:, n % 3, 1:2], soft[:, n % 3, 0:1], -1.0, None, ALU.mult)\
                        .then_inc(S["peaks"], 1)
                if 4 <= n < N_AT and n % 2 == 0:
                    m = AT[("ada", FILL[n // 2])]
                    if n == 4:
                        dve.wait_ge(lo_ready, m)
                    split_lo(dve, nc.vector, m, slice(2, 4), n // 2 - 1).then_inc(S["lo_half"], 1)
                if 3 <= n <= N_AT + 2:
                    m = n - 3
                    L = 128 * (m // H + 1)
                    dve.wait_ge(S["pt_hi_ok"], m + 1)
                    free(minus(turned_lo[:, m % 3, 0:L], full(dve, ("pT", m))[:, 0:L], turned_hi[:, m % 3, 0:L]), ("pT", m))
                if 1 <= n <= N_AT:
                    m = n - 1
                    L = 128 * (m // H + 1)
                    dve.wait_ge(S["exps"], m + 1)
                    link(nc.vector.reciprocal(soft[:, m % 3, 3:4], soft[:, m % 3, 2:3]))
                    nc.vector.tensor_scalar(probs[:, m % 3, 0:L], probs[:, m % 3, 0:L], soft[:, m % 3, 3:4], None,
                                            ALU.mult).then_inc(S["probs_ok"], 1)
                if n >= 6 and n % 2 == 0:
                    for m in (n - 6, n - 5):
                        t, h = m // H, m % H
                        r = slice(64 * (h % 2), 64 * (h % 2) + 64)
                        tok = slice(128 * t, 128 * t + 128)
                        dve.wait_ge(S["o_hi"], m + 1)
                        ins = minus(act_lo[r, 4 + h // 2, tok], head_output(full(dve, ("pv", m // 2)), m),
                                    act_hi[r, 4 + h // 2, tok])
                    free(ins, ("pv", m // 2))
                if n < 2:
                    lo_until(AT[("ada", FILL[n])] + 1)
                elif n < N_AT:
                    some_rounds(1)
            dve.wait_ge(lo_ready, AT[("wo", 0)])
            split[0] = AT[("wo", 0)]

            evacuated(dve, "toepS")
            def keep_keys(b):
                for c in (1, 3):
                    out = full(dve, ("KT", b, c))
                    if b >= 2:
                        full(dve, ("lgS", b // 2 - 1))
                    free(nc.vector.tensor_copy(k_t[:, b % 2, c, :], out[:, :]), ("KT", b, c))

            keep_keys(0)
            keep_keys(1)
            lo_until(AT[("wo", 0)] + 2)
            for bp in range(4):
                out = full(dve, ("lgS", bp))
                s = soft[:, bp % 2, :]
                if bp >= 2:
                    full(dve, ("pTSn", bp - 2))
                far = LS - 136
                link(nc.vector.tensor_tensor_reduce(rows[:, bp % 2, 0:far], out[:, 0:far], zero1[:, :].to_broadcast([128, far]),
                                                    1.0, TAKEN, ALU.add, ALU.max, s[:, 2:3]))
                free(nc.vector.tensor_tensor_reduce(rows[:, bp % 2, far:PAST], out[:, far:PAST], toep_s[:, 0:PAST - far],
                                                    1.0, s[:, 2:3], ALU.add, ALU.max, s[:, 3:4]), ("lgS", bp))
                evacuated(dve, ("lgS", bp))
                free(nc.vector.tensor_tensor_reduce(rows[:, bp % 2, PAST:LS], full(dve, ("lgSn", bp))[:, 0:DS],
                                                    toep_s[:, PAST - far:136], 1.0, s[:, 3:4], ALU.add, ALU.max, s[:, 0:1]), ("lgSn", bp))
                evacuated(dve, ("lgSn", bp))
                nc.vector.tensor_scalar(s[:, 1:2], s[:, 0:1], -1.0, None, ALU.mult).then_inc(S["peak_s"], 1)
                if bp < 3:
                    keep_keys(2 * bp + 2)
                dve.wait_ge(S["exp_s"], bp + 1)
                link(nc.vector.reciprocal(s[:, 3:4], s[:, 2:3]))
                link(nc.vector.tensor_scalar(rows[:, bp % 2, 0:LS], rows[:, bp % 2, 0:LS], s[:, 3:4], None, ALU.mult))
                if bp >= 1:
                    full(dve, ("pTSn", bp - 1))
                nc.vector.tensor_tensor(p_new[:, :].rearrange("p (b t) -> p b t", b=DB),
                                        rows[:, bp % 2, PAST:LS].unsqueeze(1).to_broadcast([128, DB, DS]),
                                        cc("own")[:, DB * bp:DB * bp + DB].unsqueeze(2).to_broadcast([128, DB, DS]),
                                        ALU.mult).then_inc(S["prob_new"], 1)
                if bp < 3:
                    keep_keys(2 * bp + 3)
                out = full(dve, ("pvS", bp))
                dve.wait_ge(S["os_hi"], 4 * bp + 4)
                for hh in range(2):
                    r = slice(64 * hh, 64 * hh + 64)
                    for b2 in range(2):
                        x = 16 * bp + 8 * b2
                        ins = minus(act_s[r, 4:8, TS + x:TS + x + 8], turned_out(out, hh, b2), act_s[r, 4:8, x:x + 8])
                free(ins, ("pvS", bp))

            def gates(k):
                dve.wait_ge(S["gain_in"], 16 * (k + 1))
                for j in range(2):
                    s = slice(512 * j, 512 * j + 512)
                    free(nc.vector.tensor_tensor(gate_p[:, s], full(dve, ("gP", k, j))[:, :], ln_post[:, s], ALU.mult), ("gP", k, j))
                    free(nc.vector.tensor_tensor(gate_s[:, s], full(dve, ("gS", k, j))[0:TS, :], ln_post[0:TS, s], ALU.mult), ("gS", k, j))
                evacuated(dve, ("gP", k, 1))
                evacuated(dve, ("gS", k, 1))

            gates(0)
            def gated(k, t):
                r = rows_of(t)
                gate = gate_p if t < NT else gate_s
                nc.vector.scalar_tensor_tensor(out_t[0:r, t, :], out_t[0:r, t, :], rstd_of(k, t),
                                               gate[0:r, :], ALU.mult, ALU.mult).then_inc(S["gated"], 1)

            def last_residual(t):
                gated(3, t)
                dve.wait_ge(S["gated"], NT + 2 + t)
                r = rows_of(t)
                nc.vector.tensor_tensor(x_res[0:r, t, :], x_res[0:r, t, :], out_t[0:r, t, :], ALU.add)\
                    .then_inc(S["y_ok"], 1)

            def sum_rows(nh):
                s = slice(512 * nh, 512 * nh + 512)
                dve.wait_ge(S["low_rows"], nh + 1)
                free(nc.vector.tensor_tensor(out_t[0:TS, NT, s], full(dve, ("wo", nh, NT))[0:TS, :], half_s[:, :], ALU.add),
                     ("wo", nh, NT))

            lo_until(AT[("wo", 0)] + 3)
            sum_rows(0)
            lo_until(AT[("wo", 2)] + 3)
            dve.wait_ge(S["x_again"], 32)
            for j in range(NT + 1 + LAG):
                if j == NT:
                    sum_rows(1)
                if j <= NT:
                    mean(1, j)
                if j >= LAG:
                    mean(2, j - LAG)
                if j <= NT:
                    gated(1, j)
                if j >= LAG:
                    normalise(2, j - LAG, out_t, x_res)
            split_hidden(1)
            lo_until(AT[("wo", 3)] + 3)

            for f in range(QF):
                for i in range(4):
                    p = 4 * f + i
                    for n in (2 * p, 2 * p + 1):
                        evacuated(dve, ("w1", n))
                        nc.vector.tensor_tensor(stage[:, n % 2, :], stage[:, n % 2, :], stage[:, n % 2, :], ALU.mult)\
                            .then_inc(S["w1_squared"], 1)
                        dve.wait_ge(S["w1_squared"], n + 1)
                    for n in (2 * p, 2 * p + 1):
                        dve.wait_ge(S["w1_hi"], n + 1)
                        minus(hid_lo[:, n % 8, :], stage[:, n % 2, :], hid_hi[:, n % 8, :]).then_inc(S["w1_done"], 1)
                    lo_until(AT[("w1", p)] + 3)
                    evacuated(dve, ("w1S", p))
                    st = stage_s[:, 2 * (p % 2):2 * (p % 2) + 2, :]
                    nc.vector.tensor_tensor(st, st, st, ALU.mult).then_inc(S["w1s_squared"], 1)
                    dve.wait_ge(S["w1s_squared"], p + 1)
                    dve.wait_ge(S["w1s_hi"], p + 1)
                    minus(hid_s[:, 2 * i:2 * i + 2, TS:2 * TS], st, hid_s[:, 2 * i:2 * i + 2, 0:TS]).then_inc(S["w1s_done"], 1)
                    if p == 0:
                        gates(1)
                for nh in range(2):
                    s = slice(512 * nh, 512 * nh + 512)
                    lo_until(AT[("w2", 4 * f + 2 * nh)] + 3)
                    last = f == QF - 1 and nh == 1
                    if f:
                        for t in range(NT):
                            if t and last:
                                mean(3, t - 1)
                            free(nc.vector.tensor_tensor(out_t[:, t, s], full(dve, ("w2", f, nh, t))[:, :], out_t[:, t, s],
                                                         ALU.add), ("w2", f, nh, t))
                            if t and last:
                                last_residual(t - 1)
                    if last:
                        mean(3, NT - 1)
                        last_residual(NT - 1)
                    dve.wait_ge(S["low_rows"], 3 + 2 * f + nh)
                    y = out_t[0:TS, NT, s]
                    if f:
                        link(nc.vector.tensor_tensor(y, y, half_s[:, :], ALU.add))
                        free(nc.vector.tensor_tensor(y, full(dve, ("w2", f, nh, NT))[0:TS, :], y, ALU.add), ("w2", f, nh, NT))
                    else:
                        free(nc.vector.tensor_tensor(y, full(dve, ("w2", f, nh, NT))[0:TS, :], half_s[:, :], ALU.add),
                             ("w2", f, nh, NT))
                    lo_until(AT[("w2", 4 * f + 2 * nh + 1)] + 3)
            mean(3, NT)
            last_residual(NT)


_OUTS = [("y_p", (1, TP, D)), ("y_s", (DB, DS, D)),
         ("k_p", (1, 1, TP, H, HD)), ("v_p", (1, 1, TP, H, HD)), ("kidx_p", (1, 1, TP, HD)), ("pool_p", (1, 1, HIST, CP_)),
         ("k_s", (1, DB, DS, H, HD)), ("v_s", (1, DB, DS, H, HD)), ("kidx_s", (1, DB, DS, HD)), ("pool_s", (1, DB, HIST, CP_))]


def kernel(**inputs):
    import concourse.bacc as bacc
    from concourse.bass_utils import run_bass_kernel_spmd

    nc = bacc.Bacc("TRN2", target_bir_lowering=False, num_devices=1)
    consts, spans = constants()
    given = {name: np.ascontiguousarray(value) for name, value in inputs.items()}
    given["consts"] = consts
    arrays, a, o = {}, {}, {}
    for name, value in given.items():
        arrays[f"in_{name}"] = value
        a[name] = nc.dram_tensor(f"in_{name}", value.shape, mybir.dt.from_np(value.dtype), kind="ExternalInput").ap()
    for name, shape in _OUTS:
        o[name] = nc.dram_tensor(f"out_{name}", shape, F32, kind="ExternalOutput").ap()
    build_program(nc, a, o, spans)
    r = run_bass_kernel_spmd(nc, [arrays], core_ids=[0])
    return tuple(r.results[0][f"out_{name}"] for name, _ in _OUTS)
```
